# Optimizing a Trainium2 kernel written in Bass

```python
import math
import jax
import jax.numpy as jnp
from jax import lax
import numpy as np
import jax, jax.numpy as jnp

D_MODEL = 1024
BATCH = 1
SEQ = 256
DEPTH = 2

D_FF = 4 * D_MODEL
NORM_EPS = 1e-6
N_EVEN = (DEPTH + 1) // 2
N_ODD = DEPTH // 2

GDN_HEADS = 8
GDN_HEAD_DIM = 64
GDN_WIDTH = GDN_HEADS * GDN_HEAD_DIM
GDN_CONV = 4
GDN_CHUNK = 64

SC_WIDTH = D_MODEL - GDN_WIDTH
SC_CONV = 3

EVEN_IN = 4 * GDN_WIDTH + 2 * GDN_HEADS + 3 * SC_WIDTH

NSA_HEADS = 16
NSA_HEAD_DIM = D_MODEL // NSA_HEADS
NSA_KV_GROUPS = 4
NSA_HPG = NSA_HEADS // NSA_KV_GROUPS
NSA_KV_WIDTH = NSA_KV_GROUPS * NSA_HEAD_DIM
CMP_BLOCK = 32
CMP_STRIDE = 16
CMP_HIDDEN = 256
SEL_BLOCK = 64
N_SELECT = 16
WINDOW = 512
Q_BLOCK = 128
ODD_IN = NSA_HEADS * NSA_HEAD_DIM + 6 * NSA_KV_WIDTH + 3 * NSA_HEADS

ROPE_THETA = 500000.0
ROPE_DIM = NSA_HEAD_DIM // 4


def _split_points(sizes):
    return [int(v) for v in np.cumsum(sizes)[:-1]]

def rms_norm(x, w):
    xf = x.astype(jnp.float32)
    y = xf * lax.rsqrt(jnp.mean(xf * xf, axis=-1, keepdims=True) + NORM_EPS)
    return (y * w.astype(jnp.float32)).astype(x.dtype)

def l2_normalize(x):
    xf = x.astype(jnp.float32)
    return xf * lax.rsqrt(jnp.sum(xf * xf, axis=-1, keepdims=True) + NORM_EPS)

def causal_dwconv(x, w):
    k_width = w.shape[0]
    t_len = x.shape[1]
    xp = jnp.pad(x, ((0, 0), (k_width - 1, 0), (0, 0)))
    return sum(xp[:, j:j + t_len] * w[j] for j in range(k_width))

def masked_softmax(s, mask):
    s = jnp.where(mask, s, -jnp.inf)
    m = jnp.max(s, axis=-1, keepdims=True)
    m = jnp.where(jnp.isfinite(m), m, 0.0)
    e = jnp.exp(s - m)
    den = jnp.sum(e, axis=-1, keepdims=True)
    return e / jnp.where(den > 0.0, den, 1.0)

def rope_tables(t_len):
    inv_freq = ROPE_THETA ** (-jnp.arange(0, ROPE_DIM, 2, dtype=jnp.float32) / ROPE_DIM)
    ang = jnp.arange(t_len, dtype=jnp.float32)[:, None] * inv_freq[None, :]
    return jnp.cos(ang), jnp.sin(ang)

def apply_partial_rope(x, cos, sin):
    half = ROPE_DIM // 2
    xf = x.astype(jnp.float32)
    x1, x2, rest = xf[..., :half], xf[..., half:ROPE_DIM], xf[..., ROPE_DIM:]
    c = cos[None, :, None, :]
    s = sin[None, :, None, :]
    return jnp.concatenate([x1 * c - x2 * s, x2 * c + x1 * s, rest], axis=-1).astype(x.dtype)

def squared_relu_mlp(h, w_up, w_down):
    return jnp.square(jax.nn.relu(h @ w_up)) @ w_down

def gated_delta_rule_chunked(q, k, v, g, beta):
    f32 = jnp.float32
    b_sz, t_len, n_h, dk = q.shape
    dv = v.shape[-1]
    c = GDN_CHUNK
    n_chunks = t_len // c

    def chunks(a):
        a = a.astype(f32).reshape((b_sz, n_chunks, c, n_h) + a.shape[3:])
        return jnp.moveaxis(a, (1, 3), (0, 2))

    qc = chunks(q) * (dk ** -0.5)
    kc = chunks(k)
    vc = chunks(v)
    bc = chunks(beta)
    gc = jnp.cumsum(chunks(g), axis=-1)
    incl = jnp.tril(jnp.ones((c, c), bool))
    strict = jnp.tril(jnp.ones((c, c), bool), -1)
    decay = jnp.exp(jnp.where(incl, gc[..., :, None] - gc[..., None, :], -jnp.inf))
    kb = kc * bc[..., None]
    m_low = jnp.where(strict, jnp.einsum('nbhik,nbhjk->nbhij', kb, kc) * decay, 0.0)
    a_mat = m_low + jnp.eye(c, dtype=f32)
    u = lax.linalg.triangular_solve(a_mat, vc * bc[..., None], left_side=True, lower=True, unit_diagonal=True)
    w = lax.linalg.triangular_solve(a_mat, kb * jnp.exp(gc)[..., None], left_side=True, lower=True, unit_diagonal=True)
    attn = jnp.einsum('nbhik,nbhjk->nbhij', qc, kc) * decay

    def step(state, inp):
        q_c, k_c, u_c, w_c, attn_c, g_c = inp
        v_new = u_c - jnp.einsum('bhck,bhkv->bhcv', w_c, state)
        o_c = (jnp.einsum('bhck,bhkv->bhcv', q_c * jnp.exp(g_c)[..., None], state)
               + jnp.einsum('bhij,bhjv->bhiv', attn_c, v_new))
        g_last = g_c[..., -1:]
        state = (state * jnp.exp(g_last)[..., None]
                 + jnp.einsum('bhck,bhcv->bhkv', k_c * jnp.exp(g_last - g_c)[..., None], v_new))
        return state, o_c

    s0 = jnp.zeros((b_sz, n_h, dk, dv), f32)
    _, o = lax.scan(step, s0, (qc, kc, u, w, attn, gc))
    return jnp.moveaxis(o, (0, 2), (1, 3)).reshape(b_sz, t_len, n_h, dv)

def gdn_shortconv_mixer(h, w_in, qkv_conv, a_log, dt_bias, o_norm, sc_conv, w_out):
    f32 = jnp.float32
    b_sz, t_len, _ = h.shape
    sizes = (3 * GDN_WIDTH, GDN_WIDTH, GDN_HEADS, GDN_HEADS, SC_WIDTH, SC_WIDTH, SC_WIDTH)
    qkv, z, a, b, b_gate, c_gate, hs = jnp.split(h @ w_in, _split_points(sizes), axis=-1)
    qkv = jax.nn.silu(causal_dwconv(qkv, qkv_conv))
    q, k, v = [t.reshape(b_sz, t_len, GDN_HEADS, GDN_HEAD_DIM) for t in jnp.split(qkv, 3, axis=-1)]
    g = -jnp.exp(a_log.astype(f32)) * jax.nn.softplus(a.astype(f32) + dt_bias.astype(f32))
    beta = jax.nn.sigmoid(b.astype(f32))
    o = gated_delta_rule_chunked(l2_normalize(q), l2_normalize(k), v, g, beta)
    o = rms_norm(o, o_norm) * jax.nn.silu(z.reshape(b_sz, t_len, GDN_HEADS, GDN_HEAD_DIM).astype(f32))
    y_a = o.reshape(b_sz, t_len, GDN_WIDTH).astype(h.dtype)
    y_b = b_gate * causal_dwconv(c_gate * hs, sc_conv)
    return jnp.concatenate([y_a, y_b], axis=-1) @ w_out

def compress_blocks(x, pos, w1, w2):
    b_sz, t_len, g_sz, d = x.shape
    r = CMP_BLOCK // CMP_STRIDE
    n_cmp = t_len // CMP_STRIDE - r + 1
    ch = x.reshape(b_sz, t_len // CMP_STRIDE, CMP_STRIDE, g_sz, d)
    blk = jnp.concatenate([ch[:, i:i + n_cmp] for i in range(r)], axis=2)
    blk = blk + pos[None, None, :, None, :].astype(x.dtype)
    blk = jnp.moveaxis(blk, 3, 2).reshape(b_sz, n_cmp, g_sz, CMP_BLOCK * d)
    return jax.nn.silu(blk @ w1) @ w2

def gather_blocks(blocks, idx):
    return jax.vmap(jax.vmap(lambda bl, ix: bl[ix]))(blocks, idx)

def nsa_mixer(h, w_in, cmp_pos, cmp_k_w1, cmp_k_w2, cmp_v_w1, cmp_v_w2, w_out):
    f32 = jnp.float32
    b_sz, t_len, _ = h.shape
    n_g, hpg, dh = NSA_KV_GROUPS, NSA_HPG, NSA_HEAD_DIM
    sizes = (NSA_HEADS * dh,) + (NSA_KV_WIDTH,) * 6 + (3 * NSA_HEADS,)
    q, k_c, v_c, k_s, v_s, k_w, v_w, gl = jnp.split(h @ w_in, _split_points(sizes), axis=-1)
    q = q.reshape(b_sz, t_len, NSA_HEADS, dh)
    k_c, v_c, k_s, v_s, k_w, v_w = [a.reshape(b_sz, t_len, n_g, dh) for a in (k_c, v_c, k_s, v_s, k_w, v_w)]
    gates = jax.nn.sigmoid(gl.astype(f32)).reshape(b_sz, t_len, n_g, hpg, 3)
    cos, sin = rope_tables(t_len)
    q_r = apply_partial_rope(q, cos, sin)
    k_s = apply_partial_rope(k_s, cos, sin)
    k_w = apply_partial_rope(k_w, cos, sin)
    kc_blk = compress_blocks(k_c, cmp_pos, cmp_k_w1, cmp_k_w2).astype(f32)
    vc_blk = compress_blocks(v_c, cmp_pos, cmp_v_w1, cmp_v_w2).astype(f32)
    n_cmp = kc_blk.shape[1]
    cmp_end = jnp.arange(n_cmp) * CMP_STRIDE + CMP_BLOCK - 1
    n_sel_blocks = t_len // SEL_BLOCK
    n_sel = min(N_SELECT, n_sel_blocks)
    c_start = jnp.arange(n_cmp)[:, None] * CMP_STRIDE
    s_start = jnp.arange(n_sel_blocks)[None, :] * SEL_BLOCK
    overlap = ((c_start < s_start + SEL_BLOCK) & (c_start + CMP_BLOCK > s_start)).astype(f32)
    ks_blk = jnp.moveaxis(k_s.reshape(b_sz, n_sel_blocks, SEL_BLOCK, n_g, dh), 3, 1)
    vs_blk = jnp.moveaxis(v_s.reshape(b_sz, n_sel_blocks, SEL_BLOCK, n_g, dh), 3, 1)
    pad = ((0, 0), (WINDOW, 0), (0, 0), (0, 0))
    kw_pad = jnp.pad(k_w, pad)
    vw_pad = jnp.pad(v_w, pad)
    scale = dh ** -0.5
    blk_ids = jnp.arange(n_sel_blocks)
    in_blk = jnp.arange(SEL_BLOCK)
    win_off = jnp.arange(Q_BLOCK + WINDOW)

    def query_block(qb):
        q0 = qb * Q_BLOCK
        t = q0 + jnp.arange(Q_BLOCK)
        take = lambda a: lax.dynamic_slice_in_dim(a, q0, Q_BLOCK, axis=1)
        qn = take(q).astype(f32).reshape(b_sz, Q_BLOCK, n_g, hpg, dh) * scale
        qr = take(q_r).astype(f32).reshape(b_sz, Q_BLOCK, n_g, hpg, dh) * scale
        p_c = masked_softmax(jnp.einsum('bqghd,bcgd->bghqc', qn, kc_blk), cmp_end[None, :] <= t[:, None])
        o_c = jnp.einsum('bghqc,bcgd->bqghd', p_c, vc_blk)
        imp = jnp.einsum('bghqc,cs->bgqs', p_c, overlap)
        cur = (t // SEL_BLOCK)[:, None]
        js = blk_ids[None, :]
        forced = (js == 0) | (js == cur) | (js == cur - 1)
        imp = jnp.where(js > cur, -jnp.inf, jnp.where(forced, jnp.inf, imp))
        _, idx = lax.top_k(imp, n_sel)
        k_sel = gather_blocks(ks_blk, idx).astype(f32).reshape(b_sz, n_g, Q_BLOCK, n_sel * SEL_BLOCK, dh)
        v_sel = gather_blocks(vs_blk, idx).astype(f32).reshape(b_sz, n_g, Q_BLOCK, n_sel * SEL_BLOCK, dh)
        kpos = (idx[..., None] * SEL_BLOCK + in_blk).reshape(b_sz, n_g, Q_BLOCK, n_sel * SEL_BLOCK)
        p_s = masked_softmax(jnp.einsum('bqghd,bgqkd->bghqk', qr, k_sel), (kpos <= t[:, None])[:, :, None])
        o_s = jnp.einsum('bghqk,bgqkd->bqghd', p_s, v_sel)
        spos = q0 - WINDOW + win_off
        dist = t[:, None] - spos[None, :]
        m_w = (dist >= 0) & (dist < WINDOW) & (spos[None, :] >= 0)
        kwin = lax.dynamic_slice_in_dim(kw_pad, q0, Q_BLOCK + WINDOW, axis=1).astype(f32)
        vwin = lax.dynamic_slice_in_dim(vw_pad, q0, Q_BLOCK + WINDOW, axis=1).astype(f32)
        p_w = masked_softmax(jnp.einsum('bqghd,bkgd->bghqk', qr, kwin), m_w)
        o_w = jnp.einsum('bghqk,bkgd->bqghd', p_w, vwin)
        g = take(gates)
        o = g[..., 0:1] * o_c + g[..., 1:2] * o_s + g[..., 2:3] * o_w
        return o.reshape(b_sz, Q_BLOCK, NSA_HEADS * dh).astype(h.dtype)

    out = lax.map(query_block, jnp.arange(t_len // Q_BLOCK))
    out = jnp.moveaxis(out, 0, 1).reshape(b_sz, t_len, NSA_HEADS * dh)
    return out @ w_out

def first_inputs(seed: int = 0) -> dict:
    key = jax.random.key(seed)
    ks = jax.random.split(key, 24)
    f32 = jnp.float32

    def nrm(k, shape, scale):
        return jax.random.normal(k, shape, f32) * scale

    def gain(k, shape):
        return 1.0 + 0.01 * jax.random.normal(k, shape, f32)

    dt = jnp.exp(jax.random.uniform(ks[9], (N_EVEN, GDN_HEADS), f32, math.log(1e-3), math.log(0.1)))
    return {
        'x': nrm(ks[0], (BATCH, SEQ, D_MODEL), 1.0),
        'mix_norm': gain(ks[1], (DEPTH, D_MODEL)),
        'mlp_norm': gain(ks[2], (DEPTH, D_MODEL)),
        'w_up': nrm(ks[3], (DEPTH, D_MODEL, D_FF), D_MODEL ** -0.5),
        'w_down': nrm(ks[4], (DEPTH, D_FF, D_MODEL), D_FF ** -0.5),
        'final_norm': gain(ks[5], (D_MODEL,)),
        'ev_w_in': nrm(ks[6], (N_EVEN, D_MODEL, EVEN_IN), D_MODEL ** -0.5),
        'ev_qkv_conv': nrm(ks[7], (N_EVEN, GDN_CONV, 3 * GDN_WIDTH), GDN_CONV ** -0.5),
        'ev_a_log': jnp.log(jax.random.uniform(ks[8], (N_EVEN, GDN_HEADS), f32, 1.0, 16.0)),
        'ev_dt_bias': dt + jnp.log(-jnp.expm1(-dt)),
        'ev_o_norm': gain(ks[10], (N_EVEN, GDN_HEAD_DIM)),
        'ev_sc_conv': nrm(ks[11], (N_EVEN, SC_CONV, SC_WIDTH), SC_CONV ** -0.5),
        'ev_w_out': nrm(ks[12], (N_EVEN, GDN_WIDTH + SC_WIDTH, D_MODEL), D_MODEL ** -0.5),
        'od_w_in': nrm(ks[13], (N_ODD, D_MODEL, ODD_IN), D_MODEL ** -0.5),
        'od_cmp_pos': nrm(ks[14], (N_ODD, CMP_BLOCK, NSA_HEAD_DIM), 0.1),
        'od_cmp_k_w1': nrm(ks[15], (N_ODD, CMP_BLOCK * NSA_HEAD_DIM, CMP_HIDDEN), (CMP_BLOCK * NSA_HEAD_DIM) ** -0.5),
        'od_cmp_k_w2': nrm(ks[16], (N_ODD, CMP_HIDDEN, NSA_HEAD_DIM), CMP_HIDDEN ** -0.5),
        'od_cmp_v_w1': nrm(ks[17], (N_ODD, CMP_BLOCK * NSA_HEAD_DIM, CMP_HIDDEN), (CMP_BLOCK * NSA_HEAD_DIM) ** -0.5),
        'od_cmp_v_w2': nrm(ks[18], (N_ODD, CMP_HIDDEN, NSA_HEAD_DIM), CMP_HIDDEN ** -0.5),
        'od_w_out': nrm(ks[19], (N_ODD, NSA_HEADS * NSA_HEAD_DIM, D_MODEL), D_MODEL ** -0.5),
    }

def first_block(x, mix_norm, mlp_norm, w_up, w_down, final_norm,
              ev_w_in, ev_qkv_conv, ev_a_log, ev_dt_bias, ev_o_norm, ev_sc_conv, ev_w_out,
              od_w_in, od_cmp_pos, od_cmp_k_w1, od_cmp_k_w2, od_cmp_v_w1, od_cmp_v_w2, od_w_out):
    for layer in range(DEPTH):
        h = rms_norm(x, mix_norm[layer])
        i = layer // 2
        if layer % 2 == 0:
            x = x + gdn_shortconv_mixer(h, ev_w_in[i], ev_qkv_conv[i], ev_a_log[i], ev_dt_bias[i],
                                        ev_o_norm[i], ev_sc_conv[i], ev_w_out[i])
        else:
            x = x + nsa_mixer(h, od_w_in[i], od_cmp_pos[i], od_cmp_k_w1[i], od_cmp_k_w2[i],
                              od_cmp_v_w1[i], od_cmp_v_w2[i], od_w_out[i])
        x = x + squared_relu_mlp(rms_norm(x, mlp_norm[layer]), w_up[layer], w_down[layer])
    return rms_norm(x, final_norm)


N_A = DEPTH // 2
N_B = DEPTH - N_A

D_FF_2 = ((8 * D_MODEL // 3 + 127) // 128) * 128
FFN_RES_SCALE = 0.5

D_A = 2 * D_MODEL
CHUNK = 128
SGU_GROUPS = 8
SGU_GROUP_DIM = D_A // SGU_GROUPS

SB_HEADS = 16
SB_HEAD_DIM = D_MODEL // SB_HEADS
SB_KV_HEADS = 4
SB_GROUP = SB_HEADS // SB_KV_HEADS

LN_EPS = 1e-5


def rms_norm_2(x, g):
    xf = x.astype(jnp.float32)
    y = xf * lax.rsqrt(jnp.mean(xf * xf, axis=-1, keepdims=True) + NORM_EPS)
    return (y * g.astype(jnp.float32)).astype(x.dtype)

def layer_norm(x, g, b):
    xf = x.astype(jnp.float32)
    mu = jnp.mean(xf, axis=-1, keepdims=True)
    xc = xf - mu
    var = jnp.mean(xc * xc, axis=-1, keepdims=True)
    y = xc * lax.rsqrt(var + LN_EPS) * g.astype(jnp.float32) + b.astype(jnp.float32)
    return y.astype(x.dtype)

def swiglu(h, w_in, w_out):
    gu = h @ w_in
    gate, up = jnp.split(gu, 2, axis=-1)
    return (jax.nn.silu(gate) * up) @ w_out

def chunked_sgu(h, w_in, ln_g, ln_b, w_s, b_s, w_out):
    B, S, _ = h.shape
    z = jax.nn.gelu(h @ w_in)
    u, v = jnp.split(z, 2, axis=-1)
    v = layer_norm(v, ln_g, ln_b)
    v = v.reshape(B, S // CHUNK, CHUNK, SGU_GROUPS, SGU_GROUP_DIM)
    causal = jnp.tril(jnp.ones((CHUNK, CHUNK), dtype=w_s.dtype))
    ws = w_s * causal[None]
    v = jnp.einsum('gts,bnsgc->bntgc', ws, v) + b_s.T[None, None, :, :, None]
    v = v.reshape(B, S, D_A)
    return (u * v) @ w_out

def stick_breaking_attention(q, k, v):
    B, S = q.shape[0], q.shape[1]
    nb = S // Q_BLOCK
    scale = 1.0 / math.sqrt(SB_HEAD_DIM)
    qf = (q.astype(jnp.float32) * scale).reshape(B, nb, Q_BLOCK, SB_KV_HEADS, SB_GROUP, SB_HEAD_DIM)
    qf = jnp.moveaxis(qf, 1, 0)
    kf = k.astype(jnp.float32)
    vf = v.astype(jnp.float32)
    key_pos = jnp.arange(S)

    def one_block(args):
        qb, bi = args
        q_pos = bi * Q_BLOCK + jnp.arange(Q_BLOCK)
        mask = key_pos[None, :] < q_pos[:, None]
        z = jnp.einsum('bqkgd,bskd->bkgqs', qb, kf)
        log_1m_beta = jnp.where(mask, jax.nn.log_sigmoid(-z), 0.0)
        rev = lax.cumsum(log_1m_beta, axis=4, reverse=True)
        excl = jnp.concatenate([rev[..., 1:], jnp.zeros_like(rev[..., :1])], axis=-1)
        a = jnp.where(mask, jnp.exp(jax.nn.log_sigmoid(z) + excl), 0.0)
        o = jnp.einsum('bkgqs,bskd->bqkgd', a, vf)
        return o.reshape(B, Q_BLOCK, SB_HEADS * SB_HEAD_DIM)

    o = lax.map(one_block, (qf, jnp.arange(nb)))
    o = jnp.moveaxis(o, 0, 1).reshape(B, S, SB_HEADS * SB_HEAD_DIM)
    return o.astype(q.dtype)

def second_inputs(seed: int = 0) -> dict:
    key = jax.random.key(seed)
    ks = jax.random.split(key, 20)
    f32 = jnp.float32
    nrm = lambda k, shape, fan_in: jax.random.normal(k, shape, f32) * (fan_in ** -0.5)
    gain = lambda k, shape: 1.0 + 0.02 * jax.random.normal(k, shape, f32)
    HD = SB_HEADS * SB_HEAD_DIM
    KVD = SB_KV_HEADS * SB_HEAD_DIM
    return {
        "x": jax.random.normal(ks[0], (BATCH, SEQ, D_MODEL), f32),
        "ffn_norm": gain(ks[1], (DEPTH, 2, D_MODEL)),
        "ffn_w_in": nrm(ks[2], (DEPTH, 2, D_MODEL, 2 * D_FF_2), D_MODEL),
        "ffn_w_out": nrm(ks[3], (DEPTH, 2, D_FF_2, D_MODEL), D_FF_2),
        "mix_norm": gain(ks[4], (DEPTH, D_MODEL)),
        "a_w_in": nrm(ks[5], (N_A, D_MODEL, 2 * D_A), D_MODEL),
        "a_ln_g": gain(ks[6], (N_A, D_A)),
        "a_ln_b": 0.02 * jax.random.normal(ks[7], (N_A, D_A), f32),
        "a_w_s": 0.5 * nrm(ks[8], (N_A, SGU_GROUPS, CHUNK, CHUNK), CHUNK),
        "a_b_s": gain(ks[9], (N_A, SGU_GROUPS, CHUNK)),
        "a_w_out": nrm(ks[10], (N_A, D_A, D_MODEL), D_A),
        "kv_norm": gain(ks[11], (D_MODEL,)),
        "w_kv": nrm(ks[12], (D_MODEL, 2 * KVD), D_MODEL),
        "b_w_q": nrm(ks[13], (N_B, D_MODEL, HD), D_MODEL),
        "b_w_o": nrm(ks[14], (N_B, HD, D_MODEL), HD),
        "final_norm": gain(ks[15], (D_MODEL,)),
    }

def second_block(x, ffn_norm, ffn_w_in, ffn_w_out, mix_norm, a_w_in, a_ln_g, a_ln_b, a_w_s,
              a_b_s, a_w_out, kv_norm, w_kv, b_w_q, b_w_o, final_norm):
    B, S, _ = x.shape
    k_shared = None
    v_shared = None
    for i in range(DEPTH):
        if i == N_A:
            kv = rms_norm_2(x, kv_norm) @ w_kv
            k_flat, v_flat = jnp.split(kv, 2, axis=-1)
            k_shared = k_flat.reshape(B, S, SB_KV_HEADS, SB_HEAD_DIM)
            v_shared = v_flat.reshape(B, S, SB_KV_HEADS, SB_HEAD_DIM)
        x = x + FFN_RES_SCALE * swiglu(rms_norm_2(x, ffn_norm[i, 0]), ffn_w_in[i, 0], ffn_w_out[i, 0])
        h = rms_norm_2(x, mix_norm[i])
        if i < N_A:
            x = x + chunked_sgu(h, a_w_in[i], a_ln_g[i], a_ln_b[i], a_w_s[i], a_b_s[i], a_w_out[i])
        else:
            j = i - N_A
            q = (h @ b_w_q[j]).reshape(B, S, SB_HEADS, SB_HEAD_DIM)
            x = x + stick_breaking_attention(q, k_shared, v_shared) @ b_w_o[j]
        x = x + FFN_RES_SCALE * swiglu(rms_norm_2(x, ffn_norm[i, 1]), ffn_w_in[i, 1], ffn_w_out[i, 1])
    return rms_norm_2(x, final_norm)


def setup_inputs(seed=0):
    out = dict(first_inputs(seed))
    for name, value in second_inputs(seed + 1).items():
        if name != "x":
            out[name + "_2"] = value
    return out


def reference(
    x, mix_norm, mlp_norm, w_up, w_down, final_norm, ev_w_in, ev_qkv_conv, ev_a_log, ev_dt_bias,
    ev_o_norm, ev_sc_conv, ev_w_out, od_w_in, od_cmp_pos, od_cmp_k_w1, od_cmp_k_w2, od_cmp_v_w1,
    od_cmp_v_w2, od_w_out, ffn_norm_2, ffn_w_in_2, ffn_w_out_2, mix_norm_2, a_w_in_2, a_ln_g_2,
    a_ln_b_2, a_w_s_2, a_b_s_2, a_w_out_2, kv_norm_2, w_kv_2, b_w_q_2, b_w_o_2, final_norm_2,
):
    x = first_block(
        x, mix_norm, mlp_norm, w_up, w_down, final_norm, ev_w_in, ev_qkv_conv, ev_a_log,
        ev_dt_bias, ev_o_norm, ev_sc_conv, ev_w_out, od_w_in, od_cmp_pos, od_cmp_k_w1,
        od_cmp_k_w2, od_cmp_v_w1, od_cmp_v_w2, od_w_out,
    )
    return second_block(
        x, ffn_norm_2, ffn_w_in_2, ffn_w_out_2, mix_norm_2, a_w_in_2, a_ln_g_2, a_ln_b_2,
        a_w_s_2, a_b_s_2, a_w_out_2, kv_norm_2, w_kv_2, b_w_q_2, b_w_o_2, final_norm_2,
    )


_drawn_inputs = setup_inputs


def setup_inputs(seed=0):
    import zlib

    import numpy as np

    out = dict(_drawn_inputs(seed))
    spreads = {}
    factors = {'mix_norm': 3.625,
     'mlp_norm': 12.65,
     'final_norm': 4.569,
     'ev_o_norm': 41.98,
     'od_cmp_pos': 17.961,
     'ffn_norm_2': 3.967,
     'mix_norm_2': 4.007,
     'a_ln_g_2': 35.484,
     'a_ln_b_2': 34.894,
     'a_b_s_2': 4.92,
     'kv_norm_2': 21.305,
     'final_norm_2': 8.404}
    for name, (base, spread) in spreads.items():
        noise = np.random.default_rng([zlib.crc32(name.encode()), seed]).standard_normal(out[name].shape)
        drawn = base * np.exp(spread * noise) if base else spread * noise
        out[name] = jnp.asarray(drawn.astype(out[name].dtype))
    for name, factor in factors.items():
        out[name] = (out[name] * factor).astype(out[name].dtype)
    return out
```

```python
from contextlib import ExitStack

import concourse.bass as bass
from concourse import mybir

F32 = mybir.dt.float32
F32R = mybir.dt.float32r
ACT = mybir.ActivationFunctionType
ALU = mybir.AluOpType
AXX = mybir.AxisListType.X

P = 128
T = 256
TT = T // P
D = 1024
DK = D // P
NB = 512
PK = 4
PANEL = PK * NB
RING = 4
FF = 4 * D
FF2 = 2816
EPS = 1e-6
LN_EPS = 1e-5
KB = 1024
BIG = 1.0e30

PRODUCTS = [
    ("ev_in", DK, 7), ("ev_out", DK, 2),
    ("mlp0_up", DK, FF // NB), ("mlp0_down", FF // P, 2),
    ("od_in", DK, 5), ("od_out", DK, 2),
    ("mlp1_up", DK, FF // NB), ("mlp1_down", FF // P, 2),
    ("ffn00_up", DK, FF2 // 256), ("ffn00_down", FF2 // P, 2),
    ("sgu_in", DK, 8), ("sgu_out", 2 * DK, 2),
    ("ffn01_up", DK, FF2 // 256), ("ffn01_down", FF2 // P, 2),
    ("kv", DK, 1),
    ("ffn10_up", DK, FF2 // 256), ("ffn10_down", FF2 // P, 2),
    ("sb_q", DK, 2), ("sb_out", DK, 2),
    ("ffn11_up", DK, FF2 // 256), ("ffn11_down", FF2 // P, 2),
]
NORMS = ["mix0", "mlp0", "mix1", "mlp1", "ffn00", "ffn01", "ffn10", "ffn11", "sgu", "sb", "kv"]

LAYERS = ["mix0", "mlp0", "mix1", "mlp1", "fin1", "ffn00", "sgu", "ffn01", "kv", "ffn10", "sb", "ffn11", "fin2"]


class Product:

    def __init__(self, name, kt, blocks, panel, block):
        self.name, self.kt, self.blocks = name, kt, blocks
        self.per = -(-kt // PK)
        self.panel, self.block = panel, block


def lay_out_products(layers):
    owner = {"ev": "mix0", "od": "mix1"}
    out, panel, block = {}, 0, 0
    for name, kt, blocks in PRODUCTS:
        head = name.split("_")[0]
        if owner.get(head, head) not in layers:
            continue
        out[name] = Product(name, kt, blocks, panel, block)
        panel += out[name].per * blocks
        block += blocks
    return out, panel


def const_table():
    import numpy as np

    c, cols = {}, []

    def put(name, a):
        a = np.asarray(a, np.float32).reshape(P, -1)
        start = sum(x.shape[1] for x in cols)
        c[name] = (start, start + a.shape[1])
        cols.append(a)

    p = np.arange(P)[:, None]
    f = np.arange(P)[None, :]
    put("ident", p == f)
    same = p // 64 == f // 64
    put("cum", same & (p <= f))
    put("chunk", same)
    put("even", np.broadcast_to(p < 64, (P, P)))
    put("odd", np.broadcast_to(p >= 64, (P, P)))
    put("not_later", np.where(same & (p <= f), 0, -BIG))
    for level in range(1, 7):
        half = 1 << (level - 1)
        put(f"level{level}", (p // (2 * half) == f // (2 * half)) & (p // half % 2 == 0) & (f // half % 2 == 1))
    put("causal_wide", np.concatenate([np.zeros((P, P)), np.where(f <= p, 0, -BIG)], 1))
    put("group", p // 16 == np.arange(4)[None, :])
    tok = p[:, :, None] + P * np.arange(TT)[None, :, None]
    ends = np.arange(16)[None, None, :] * 16 + 31
    seen = (ends <= tok) & (np.arange(16)[None, None, :] < 15)
    put("cmp_add", np.where(seen, 0, -BIG))
    put("cmp_mul", seen)
    inv = np.float32(500000.0) ** (-np.arange(0, 16, 2, dtype=np.float32) / np.float32(16))
    ang = tok.astype(np.float32) * inv.astype(np.float32)[None, None, :]
    put("cos", np.cos(ang, dtype=np.float32))
    put("sin", np.sin(ang, dtype=np.float32))
    put("earlier", p < f)
    put("not_earlier", np.where(p < f, 0, -BIG))
    put("suffix", p >= f)
    put("ones", np.ones((P, P)))
    put("upto", p <= f)
    put("neg_half", np.full((P, 16), -0.5))
    return np.concatenate(cols, axis=1), c


CONST_AT = const_table()[1]
CONST_WIDTH = max(b for _, b in CONST_AT.values())


def build(nc, dram, layers=LAYERS):
    prod, panels = lay_out_products(layers)

    at, t, x, r = {}, 0, 0, 0
    hidden_batches = {"mlp": FF // NB, "ffn": FF2 // 256}
    for layer in layers:
        at[layer] = (t, x, r)
        kind = layer[:3]
        if layer == "kv":
            t, r = t + 2, r + 1
        elif layer in ("fin1", "fin2"):
            x, r = x + 2, r + 1
        elif kind in hidden_batches:
            t, x, r = t + 2 + hidden_batches[kind], x + 4, r + 1
        else:
            t, x, r = t + 2 + {"sgu": 4}.get(layer, 0), x + 4, r + 1
    hidden_before, count = {}, 0
    for layer in layers:
        hidden_before[layer] = count
        count += hidden_batches.get(layer[:3], 0)
    following = dict(zip(layers, layers[1:]))

    def early_norm(layer):
        nxt = following.get(layer)
        return nxt if layer[:3] in ("mlp", "ffn") and nxt in NORMS else None

    early = {early_norm(a) for a in layers}

    with ExitStack() as ctx:
        def sb(name, shape, dt=F32):
            return ctx.enter_context(nc.sbuf_tensor(name, shape, dt))

        def sem(name):
            return ctx.enter_context(nc.semaphore(name))

        raw = sb("raw", [P, RING, PANEL])
        w_hi = sb("w_hi", [P, 2, PANEL], F32R)
        w_lo = sb("w_lo", [P, 2, PANEL], F32R)
        x_sb = sb("x_sb", [P, TT, D])
        h_hi = sb("h_hi", [P, DK, T], F32R)
        h_lo = sb("h_lo", [P, DK, T], F32R)
        tm = sb("tm", [P, TT, NB])
        row = sb("row", [P, D])
        junk = sb("junk", [P, D], mybir.dt.bfloat16)
        const = sb("const", [P, CONST_WIDTH])
        norm_t = sb("norm_t", [P, len(NORMS), DK])
        ss = sb("ss", [P, TT])
        ms = sb("ms", [P, TT])
        rstd = sb("rstd", [P, TT])
        arena_bytes = 2 * (FF // P) * T * 4 + 34 * KB
        arena = sb("arena", [P, arena_bytes // 4])
        arena_at = nc.lookup_mloc(arena).addr

        def view(name, shape, at_byte, dt=F32):
            return nc.alloc_sbuf_tensor_at(name, shape, dt, offset=arena_at + at_byte)

        hid_hi = view("hid_hi", [P, FF // P, T], 0, F32R)
        hid_lo = view("hid_lo", [P, FF // P, T], (FF // P) * T * 4, F32R)
        hid_hi2 = hid_hi[:].rearrange("p k t -> p (k t)")
        hid_lo2 = hid_lo[:].rearrange("p k t -> p (k t)")

        sgu_z = view("sgu_z", [P, TT, 4 * D], 16 * KB)
        sgu_lo = hid_lo[:, 2 * DK:, :]
        ln_rows = view("ln_rows", [P, 2, 2 * D], 64 * KB)
        ws_raw = view("ws_raw", [P, 8, P], 80 * KB)
        ws_t = view("ws_t", [P, 8, P], 84 * KB)
        bs_t = view("bs_t", [P, 8], 88 * KB)
        v_sums = view("v_sums", [P, TT, 4], 88 * KB + 64)
        v_sq = view("v_sq", [P, TT, 2], 88 * KB + 192)
        v_stat = view("v_stat", [P, 3, TT], 88 * KB + 128)
        gd_x = view("gd_x", [P, 12, 3 + T], 0)
        gd_ch = view("gd_ch", [P, 4, 2 + T], 13 * KB)
        gd_b = view("gd_b", [P, 4, T], 18 * KB)
        gd_z = view("gd_z", [P, TT, NB], 22 * KB)
        gd_c = view("gd_c", [P, 12, T], 26 * KB)
        gd_sc = view("gd_sc", [P, 4, T], 38 * KB)
        gd_wab = view("gd_wab", [P, 8 * 16], 42 * KB)
        gd_wab_hi = view("gd_wab_hi", [P, 8 * 16], 42 * KB + 512, F32R)
        gd_wab_lo = view("gd_wab_lo", [P, 8 * 16], 43 * KB, F32R)
        gd_tm = view("gd_tm", [P, 8, NB], 44 * KB)
        gd_t = view("gd_t", [P, 4, 4, P], 60 * KB)
        gd_dt = view("gd_dt", [P, 8, P], 68 * KB)
        gd_mt = view("gd_mt", [P, 8, P], 72 * KB)
        gd_ml = view("gd_ml", [P, 2, 8, P], 76 * KB)
        gd_inv = view("gd_inv", [P, 8, P], 84 * KB)
        gd_invt = view("gd_invt", [P, 8, P], 88 * KB)
        gd_p = view("gd_p", [P, 8, P], 92 * KB)
        gd_gb = view("gd_gb", [P, 8, P], 92 * KB)
        gd_sq = view("gd_sq", [P, 2, NB], 84 * KB)
        gd_at = view("gd_at", [P, 8, P], 0)
        gd_u = view("gd_u", [P, NB], 4 * KB)
        gd_wt = view("gd_wt", [P, 4, P], 6 * KB)
        gd_vn = view("gd_vn", [P, NB], 8 * KB)
        gd_s = view("gd_s", [P, 4, P], 10 * KB)
        gd_o = view("gd_o", [P, NB], 14 * KB)
        gd_osq = view("gd_osq", [P, NB], 16 * KB)
        par_at = 96 * KB
        gd_cw = view("gd_cw", [P, 12, 4], par_at)
        gd_scw = view("gd_scw", [P, 4, 3], par_at + 192)
        gd_dt_bias = view("gd_dt_bias", [P, 8], par_at + 256)
        gd_a_log = view("gd_a_log", [P, 8], par_at + 288)
        gd_onorm = view("gd_onorm", [P, 64], par_at + 320)
        gd_g = view("gd_g", [P, 8, TT, 8], par_at + 576)
        gd_sum = view("gd_sum", [P, 4, TT, 8], par_at + 1088)
        gd_exp = view("gd_exp", [P, 4, TT, 8], par_at + 1344)
        gd_dec = view("gd_dec", [P, 2, TT, 4], par_at + 1600)
        gd_ez = view("gd_ez", [P, 2, TT, 8], par_at + 1664)
        gd_rs = view("gd_rs", [P, 3, 2, 8], par_at + 1792)

        ns_tm = view("ns_tm", [P, TT, 5 * NB], 0)
        ns_w1 = view("ns_w1", [P, 2, 16, 256], 20 * KB)
        ns_qt = view("ns_qt", [P, 8, T], 52 * KB)
        ns_qrt = view("ns_qrt", [P, 8, T], 60 * KB)
        ns_kt = view("ns_kt", [P, 2, 4, T], 68 * KB)
        ns_xp = view("ns_xp", [P, 2, 2, 8, 64], 76 * KB)
        ns_w2k = view("ns_w2k", [P, 2, P], 84 * KB)
        ns_w2v = view("ns_w2v", [P, 2, 64], 85 * KB)
        ns_h = view("ns_h", [64, 2, 256], 86 * KB)
        ns_ht = view("ns_ht", [P, 2, 2, 64], 88 * KB)
        ns_kct = view("ns_kct", [P, 64], 89 * KB)
        ns_vc = view("ns_vc", [64, 4, 64], 89 * KB + 256)
        ns_wg = view("ns_wg", [P, 8 * 48], 91 * KB)
        ns_wg_hi = view("ns_wg_hi", [P, 8 * 48], 92 * KB + 512, F32R)
        ns_wg_lo = view("ns_wg_lo", [P, 8 * 48], 94 * KB, F32R)
        ns_gate = view("ns_gate", [P, TT, 48], 95 * KB + 512)
        ns_pos = view("ns_pos", [P, 2, 8], 90 * KB + 256)
        ns_rot = view("ns_rot", [P, 4, TT, 16, 8], 76 * KB)
        ns_p = view("ns_p", [P, 2, 4, T], 20 * KB)
        ns_pt = view("ns_pt", [P, 2, 8, P], 28 * KB)
        ns_o = view("ns_o", [P, TT, D], 36 * KB)
        ns_c = view("ns_c", [P, 256], 44 * KB)
        ns_cpt = view("ns_cpt", [64, 4, P], 45 * KB)
        ns_st = view("ns_st", [P, 8, 16], 47 * KB)
        ns_cst = view("ns_cst", [P, 4, 16], 47 * KB + 512)
        ns_krot = view("ns_krot", [P, 4, TT, 4, 8], 48 * KB)
        kv_tm = view("kv_tm", [P, TT, NB], 92 * KB)
        sb_q = view("sb_q", [P, TT, D], 0)
        sb_qt = view("sb_qt", [P, 8, T], 8 * KB)
        sb_kt = view("sb_kt", [P, 4, T], 16 * KB)
        sb_s = view("sb_s", [P, 3, 2, 2, 256], 20 * KB)
        sb_o = view("sb_o", [P, TT, D], 32 * KB)

        ps = ctx.enter_context(nc.psum_tensor("ps", [P, 8, NB], F32))
        acc = [[ps[:, 2 * b + t, :] for t in range(TT)] for b in range(2)]
        tps = ps[:, 4:6, :].rearrange("p b n -> p (b n)").rearrange("p (f t) -> p f t", t=T)

        def cst(name):
            a, b = CONST_AT[name]
            return const[:, a:b]

        ident = cst("ident")
        two = {b: ps[:, b:b + 2, :] for b in range(0, 8, 2)}

        raw_full = [sem(f"raw_full{i}") for i in range(RING)]
        hi_ready = sem("hi_ready")
        lo_ready = sem("lo_ready")
        w_used = sem("w_used")
        act_tm = sem("act_tm")
        tm_ready = sem("tm_ready")
        tps_ready = sem("tps_ready")
        t_hi = sem("t_hi")
        t_lo = sem("t_lo")
        x_ready = sem("x_ready")
        ss_ready = sem("ss_ready")
        ms_ready = sem("ms_ready")
        rstd_ready = sem("rstd_ready")
        x_loaded = sem("x_loaded")
        params_loaded = sem("params_loaded")
        out_stored = sem("out_stored")
        row_loaded = sem("row_loaded")
        row2_loaded = sem("row2_loaded")
        y_tps = sem("y_tps")
        y_hi = sem("y_hi")
        y_lo = sem("y_lo")
        y_tm = sem("y_tm")
        sgu_params = sem("sgu_params")
        sgu_in = sem("sgu_in")
        sgu_mean = sem("sgu_mean")
        sgu_sq = sem("sgu_sq")
        sgu_rs = sem("sgu_rs")
        sgu_v = sem("sgu_v")
        sgu_ws = sem("sgu_ws")
        sgu_mix = sem("sgu_mix")
        sgu_s = sem("sgu_s")
        dve_step = sem("dve_step")
        pool_step = sem("pool_step")
        gd_params = sem("gd_params")
        gd_split = sem("gd_split")
        gd_in = sem("gd_in")
        gd_tp = sem("gd_tp")
        gd_ts = sem("gd_ts")
        gd_pad = sem("gd_pad")
        gd_cv = sem("gd_cv")
        gd_cs = sem("gd_cs")
        gd_abp = sem("gd_abp")
        gd_yb = sem("gd_yb")
        gd_ybh = sem("gd_ybh")
        gd_ybl = sem("gd_ybl")
        gd_ga = sem("gd_ga")
        gd_ge = sem("gd_ge")
        gd_gg = sem("gd_gg")
        gd_gp = sem("gd_gp")
        gd_gs = sem("gd_gs")
        gd_gx = sem("gd_gx")
        gd_gt = sem("gd_gt")
        gd_q = sem("gd_q")
        gd_qq = sem("gd_qq")
        gd_qs = sem("gd_qs")
        gd_qr = sem("gd_qr")
        gd_kn = sem("gd_kn")
        gd_kz = sem("gd_kz")
        gd_gbr = sem("gd_gbr")
        gd_bc = sem("gd_bc")
        gd_da = sem("gd_da")
        gd_de = sem("gd_de")
        gd_ft = sem("gd_ft")
        gd_fa = sem("gd_fa")
        gd_fv = sem("gd_fv")
        gd_kk = sem("gd_kk")
        gd_m = sem("gd_m")
        gd_a = sem("gd_a")
        gd_x1 = sem("gd_x1")
        gd_xp = sem("gd_xp")
        gd_xs = sem("gd_xs")
        gd_mlr = sem("gd_mlr")
        gd_pp = sem("gd_pp")
        gd_ps = sem("gd_ps")
        gd_qp = sem("gd_qp")
        gd_iv = sem("gd_iv")
        gd_up = sem("gd_up")
        gd_us = sem("gd_us")
        gd_ws = sem("gd_ws")
        gd_sp = sem("gd_sp")
        gd_vs = sem("gd_vs")
        gd_os = sem("gd_os")
        gd_dp = sem("gd_dp")
        gd_st = sem("gd_st")
        gd_op = sem("gd_op")
        gd_of = sem("gd_of")
        gd_oq = sem("gd_oq")
        gd_or = sem("gd_or")
        gd_on = sem("gd_on")
        gd_zn = sem("gd_zn")
        gd_z0 = sem("gd_z0")
        ns_params = sem("ns_params")
        ns_split = sem("ns_split")
        ns_in = sem("ns_in")
        ns_cvt = sem("ns_cvt")
        ns_x = sem("ns_x")
        ns_hp = sem("ns_hp")
        ns_hs = sem("ns_hs")
        ns_htp = sem("ns_htp")
        ns_hts = sem("ns_hts")
        ns_kvp = sem("ns_kvp")
        ns_kvs = sem("ns_kvs")
        ns_qtp = sem("ns_qtp")
        ns_qts = sem("ns_qts")
        ns_rope = sem("ns_rope")
        ns_krope = sem("ns_krope")
        ns_rtp = sem("ns_rtp")
        ns_rts = sem("ns_rts")
        ns_gp = sem("ns_gp")
        ns_gs = sem("ns_gs")
        ns_cs = sem("ns_cs")
        ns_cd = sem("ns_cd")
        ns_cg = sem("ns_cg")
        ns_ce = sem("ns_ce")
        ns_ctp = sem("ns_ctp")
        ns_cts = sem("ns_cts")
        ns_s = sem("ns_s")
        ns_m = sem("ns_m")
        ns_nm = sem("ns_nm")
        ns_e = sem("ns_e")
        ns_d = sem("ns_d")
        ns_w = sem("ns_w")
        ns_tp = sem("ns_tp")
        ns_ts = sem("ns_ts")
        ns_pv = sem("ns_pv")
        kv_in = sem("kv_in")
        sb_in = sem("sb_in")
        sb_tp = sem("sb_tp")
        sb_ts = sem("sb_ts")
        sb_z = sem("sb_z")
        sb_zm = sem("sb_zm")
        sb_abs = sem("sb_abs")
        sb_ln = sem("sb_ln")
        sb_sp = sem("sb_sp")
        sb_rev = sem("sb_rev")
        sb_arg = sem("sb_arg")
        sb_a = sem("sb_a")
        sb_av = sem("sb_av")

        read = {}
        for layer in layers:
            t0, x0, _ = at[layer]
            if layer[:3] in hidden_batches:
                h0 = hidden_before[layer]
                read[layer + "_up"] = (act_tm, 2 * h0, 2) if layer[:3] == "mlp" else (tm_ready, h0, 1)
                read[layer + "_down"] = (x_ready, x0, TT)
        if "sgu" in layers:
            read["sgu_in"], read["sgu_out"] = (sgu_in, 0, TT), (x_ready, at["sgu"][1], TT)
        if "mix0" in layers:
            read["ev_in"], read["ev_out"] = (gd_in, 0, TT), (x_ready, at["mix0"][1], TT)
        if "mix1" in layers:
            read["od_in"], read["od_out"] = (ns_in, 0, TT), (x_ready, at["mix1"][1], TT)
        if "kv" in layers:
            read["kv"] = (kv_in, 0, TT)
        if "sb" in layers:
            read["sb_q"], read["sb_out"] = (sb_in, 0, TT), (x_ready, at["sb"][1], TT)
        readers = [(read[q.name][0], read[q.name][1] + read[q.name][2] * (b + 1))
                   for q in prod.values() for b in range(q.blocks)]

        block = ctx.enter_context(nc.Block())

        mixers = [a for a in layers if a in ("mix0", "mix1", "sb")]

        def y_before(layer):
            return TT * mixers.index(layer)

        sb_rows = [(g, qt) for qt in range(TT) for g in range(4)]
        sb_units = [(g, qt, kt) for g, qt in sb_rows for kt in range(qt, -1, -1)]

        ns_units = [(tt, br, g) for tt in range(TT) for br in range(2) for g in range(4)]
        NS_COL = {"kc": 0, "vc": 256, "q": 512, "ks": 1536, "vs": 1792, "kw": 2048, "vw": 2304}

        def steps(first, blocks):
            pairs = (blocks - first) // 2
            return pairs, first + 2 * pairs

        @block.sync
        def _(sp):
            sp.dma_start(x_sb[:, :, :], dram["x"]).then_inc(x_loaded, 16)
            sp.dma_start(const[:, :], dram["const"]).then_inc(params_loaded, 16)
            sp.dma_start(norm_t[:, :, :], dram["norm_t"]).then_inc(params_loaded, 16)
            first_row = 0 if "fin1" in layers else 1
            sp.dma_start(row[:, :], dram["fin_rows"][first_row:first_row + 1, :].partition_broadcast(P)).then_inc(row_loaded, 16)

            def load(slot, panel, wait_lo):
                if wait_lo is not None:
                    sp.wait_ge(lo_ready, wait_lo)
                sp.dma_start(raw[:, slot, :], dram["stream"][panel, :, :]).then_inc(raw_full[slot], 16)

            for q in range(min(RING, panels)):
                load(q, q, None)
            turns = (panels - RING) // RING
            if turns > 0:
                with sp.Fori(0, turns) as i:
                    for q in range(RING):
                        load(q, RING + RING * i + q, RING * 2 * i + 2 * q + 2)
            for q in range(RING + RING * max(turns, 0), panels):
                load(q % RING, q, 2 * (q - RING) + 2)
            if "fin2" in layers:
                n = at["fin2"][1]
                for tt in range(TT):
                    sp.wait_ge(x_ready, n + tt + 1)
                    sp.dma_start(dram["out"][:, tt, :], x_sb[:, tt, :]).then_inc(out_stored, 16)
            else:
                t0, x0, _ = at[layers[-1]]
                sp.wait_ge(x_ready, x)
                for tt in range(TT):
                    sp.dma_start(dram["out"][:, tt, :], x_sb[:, tt, :]).then_inc(out_stored, 16)
            sp.wait_ge(out_stored, 16 * TT)

        @block.tensor
        def _(pe):
            def multiply(q, b, bs, i, j, a_hi, a_lo, k_at=0, halves=(0, 1)):
                panel = q.panel + q.per * b + j
                slot = (q.panel + q.per * bs + j) % 2
                nk = min(PK, q.kt - PK * j)
                half = nk // 2
                bank = acc[(q.block + bs) % 2]
                last = j == q.per - 1
                for s in halves:
                    if j == 0 and s == 0 and q.block + bs >= 2:
                        if bs >= 2:
                            free, before, each = read[q.name]
                            pe.wait_ge(free, before + each * (b - 1))
                        else:
                            free, count = readers[q.block + bs - 2]
                            pe.wait_ge(free, count)
                    pe.wait_ge(lo_ready, 2 * panel + s + 1)
                    for kk in range(s * half, (s + 1) * half):
                        k = PK * j + kk
                        hi = w_hi[:, slot, kk * NB:(kk + 1) * NB]
                        lo = w_lo[:, slot, kk * NB:(kk + 1) * NB]
                        for tt in range(TT):
                            rows = slice(tt * P, (tt + 1) * P)
                            pe.matmul(bank[tt], a_hi[:, k_at + k, rows], hi, start=(k == 0), stop=False)
                            pe.matmul(bank[tt], a_hi[:, k_at + k, rows], lo, start=False, stop=False)
                            done = pe.matmul(bank[tt], a_lo[:, k_at + k, rows], hi, start=False,
                                             stop=(k == q.kt - 1))
                if 1 in halves:
                    done.then_inc(w_used, 1)

            def transpose_batch(t, src, f_count, wait_for, count):
                pe.wait_ge(wait_for, count)
                if not (isinstance(t, int) and t == 0):
                    pe.wait_ge(t_lo, t)
                for tt in range(TT):
                    for f in range(f_count):
                        done = pe.transpose(tps[:, f, tt * P:(tt + 1) * P], src(tt, f), ident)
                done.then_inc(tps_ready, 1)

            def norm_batch(layer, half):
                t0, x0, _ = at[layer]
                if x0 == 0:
                    pe.wait_ge(params_loaded, 32)
                    transpose_batch(t0 + half, lambda tt, f: x_sb[:, tt, (4 * half + f) * P:(4 * half + f + 1) * P],
                                    4, x_loaded, 16)
                    return
                need = x0 if half or layer not in early else x0 - TT
                transpose_batch(t0 + half, lambda tt, f: x_sb[:, tt, (4 * half + f) * P:(4 * half + f + 1) * P],
                                4, x_ready, need)

            def enter(layer, q, b_hi=h_hi, b_lo=h_lo):
                t0 = at[layer][0]
                if layer not in early:
                    norm_batch(layer, 0)
                pe.wait_ge(t_lo, t0 + 1)
                multiply(q, 0, 0, 0, 0, h_hi, h_lo, halves=(0,))
                norm_batch(layer, 1)
                multiply(q, 0, 0, 0, 0, h_hi, h_lo, halves=(1,))
                pe.wait_ge(t_lo, t0 + 2)
                multiply(q, 0, 0, 0, 1, h_hi, h_lo)

            def hidden_layer(layer, f_count):
                up, down = prod[layer + "_up"], prod[layer + "_down"]
                t0 = at[layer][0] + 2
                tm_at = hidden_before[layer]

                def hidden_t(b):
                    transpose_batch(t0 + b, lambda tt, f: tm[:, tt, f * P:(f + 1) * P], f_count,
                                    tm_ready, tm_at + b + 1)

                enter(layer, up)

                def body(b, bs, i):
                    multiply(up, b, bs, i, 0, h_hi, h_lo)
                    hidden_t(b - 1)
                    multiply(up, b, bs, i, 1, h_hi, h_lo)

                body(1, 1, 0)
                pairs, rest = steps(2, up.blocks)
                with pe.Fori(0, pairs) as i:
                    for k in range(2):
                        body(2 + 2 * i + k, 2 + k, i)
                for b in range(rest, up.blocks):
                    body(b, b, 0)
                for b in range(down.blocks):
                    for j in range(down.per):
                        if b == 0 and j == 1:
                            hidden_t(up.blocks - 1)
                        if b == 0:
                            pe.wait_ge(t_lo, t0 + min(up.blocks, -(-min(PK * (j + 1), down.kt) // f_count)))
                        if b == 1 and j == 3 and early_norm(layer):
                            norm_batch(early_norm(layer), 0)
                        multiply(down, b, b, 0, j, hid_hi, hid_lo)

            def in_product(layer, q, between={}):
                enter(layer, q)
                for b in range(1, q.blocks):
                    multiply(q, b, b, 0, 0, h_hi, h_lo)
                    if b in between:
                        between[b]()
                    multiply(q, b, b, 0, 1, h_hi, h_lo)

            def out_product(layer, q):
                pe.wait_ge(y_lo, y_before(layer) + TT)
                for b in range(q.blocks):
                    for j in range(q.per):
                        multiply(q, b, b, 0, j, h_hi, h_lo)

            def transpose_y(layer, tt, src, tiles=8):
                n = y_before(layer) + tt
                pe.wait_ge(y_tm, n + 1)
                if n:
                    pe.wait_ge(y_lo, n)
                for f in range(tiles):
                    done = pe.transpose(two[4].rearrange("p b n -> p (b n)")[:, f * P:(f + 1) * P],
                                        src[:, f * P:(f + 1) * P], ident)
                done.then_inc(y_tps, 1)

            def spatial_gating():
                q, out = prod["sgu_in"], prod["sgu_out"]
                t0 = at["sgu"][0] + 2
                in_product("sgu", q)
                pe.wait_ge(sgu_ws, 1)
                pe.wait_ge(sgu_v, 3 * TT)

                def mix(pair):
                    if pair:
                        pe.wait_ge(sgu_s, TT * pair)
                    for tt in range(TT):
                        for g in range(2):
                            at_col = (2 * pair + g) * 256
                            done = pe.matmul(ps[:, 6 + tt, g * 256:(g + 1) * 256], ws_t[:, 2 * pair + g, :],
                                             sgu_z[:, tt, at_col:at_col + 256], start=True, stop=True)
                        done.then_inc(sgu_mix, 1)

                def gated_t(pair):
                    transpose_batch(t0 + pair, lambda tt, f: sgu_z[:, tt, 2 * D + (4 * pair + f) * P:2 * D + (4 * pair + f + 1) * P],
                                    4, sgu_s, TT * (pair + 1))

                mix(0)
                mix(1)
                gated_t(0)
                mix(2)
                gated_t(1)
                for b in range(out.blocks):
                    for j in range(out.per):
                        if b == 0:
                            pe.wait_ge(t_lo, t0 + j + 1)
                        multiply(out, b, b, 0, j, hid_hi, sgu_lo)
                        if b == 0 and j == 0:
                            mix(3)
                        if b == 0 and j < 2:
                            gated_t(j + 2)

            def stick_breaking():
                q, out = prod["sb_q"], prod["sb_out"]
                in_product("sb", q)
                pe.wait_ge(sb_in, TT * q.blocks)
                for n in range(4):
                    if n >= 2:
                        pe.wait_ge(sb_ts, n - 1)
                    for f in range(2):
                        for tt in range(TT):
                            done = pe.transpose(ps[:, 4 + n % 2, f * T + tt * P:f * T + (tt + 1) * P],
                                                sb_q[:, tt, (2 * n + f) * P:(2 * n + f + 1) * P], ident)
                    done.then_inc(sb_tp, 1)
                for n in range(2):
                    pe.wait_ge(sb_ts, n + 3)
                    for f in range(2):
                        for tt in range(TT):
                            for half in range(2):
                                done = pe.matmul(ps[64 * half:64 * half + 64, 4 + n % 2, f * T + tt * P:f * T + (tt + 1) * P],
                                                 kv_tm[:, tt, (2 * n + f) * 64:(2 * n + f + 1) * 64], ident,
                                                 start=(f == 0 and tt == 0), stop=True, skip_group_check=True)
                    done.then_inc(sb_tp, 1)
                pe.wait_ge(sb_ts, 6)

                def scores(u):
                    g, qt, kt = sb_units[u]
                    if u >= 2:
                        pe.wait_ge(sb_zm, u - 1)
                    for par in range(2):
                        rows = slice(64 * par, 64 * par + 64)
                        done = pe.matmul(ps[:, 2 * (u % 2) + par, 0:256], sb_kt[rows, g, kt * P:(kt + 1) * P],
                                         sb_qt[rows, 2 * g:2 * g + 2, qt * P:(qt + 1) * P], start=True, stop=True)
                    done.then_inc(sb_z, 1)

                def suffix_sums(u):
                    g, qt, kt = sb_units[u]
                    pe.wait_ge(sb_sp, u + 1)
                    if u:
                        pe.wait_ge(sb_arg, u)
                    carry = kt < qt
                    slot = u % 3
                    done = pe.matmul(ps[:, 4, :], cst("suffix"), sb_s[:, slot, 1, :, :], start=True, stop=not carry)
                    if carry:
                        done = pe.matmul(ps[:, 4, :], cst("ones"), sb_s[:, (u - 1) % 3, 1, :, :], start=False, stop=True)
                    done.then_inc(sb_rev, 1)

                def values(u):
                    g, qt, kt = sb_units[u]
                    pe.wait_ge(sb_a, u + 1)
                    if g == 0 and kt == qt and qt:
                        pe.wait_ge(y_tm, y_before("sb") + qt)
                    for j in range(4):
                        h = 4 * g + j
                        first = kt == qt and h % 8 == 0
                        done = pe.matmul(ps[:, 6 + h // 8, (h % 8) * 64:(h % 8 + 1) * 64],
                                         sb_s[:, u % 3, 0, j % 2, (j // 2) * P:(j // 2 + 1) * P],
                                         kv_tm[:, kt, 256 + g * 64:256 + (g + 1) * 64],
                                         start=first, stop=True, skip_group_check=True)
                    done.then_inc(sb_av, 1)

                n = len(sb_units)
                scores(0)
                for u in range(n):
                    if u + 1 < n:
                        scores(u + 1)
                    suffix_sums(u)
                    if u:
                        values(u - 1)
                values(n - 1)
                for tt in range(TT):
                    transpose_y("sb", tt, sb_o[:, tt, :])
                out_product("sb", out)

            def delta_rule():
                q, out = prod["ev_in"], prod["ev_out"]

                def block_t(n):
                    pe.wait_ge(gd_in, TT * (n + 1))
                    if n == 0:
                        pe.wait_ge(t_lo, at["mix0"][0] + 2)
                    else:
                        pe.wait_ge(gd_ts, n)
                    for tt in range(TT):
                        for f in range(4):
                            done = pe.transpose(tps[:, f, tt * P:(tt + 1) * P], tm[:, tt, f * P:(f + 1) * P], ident)
                    done.then_inc(gd_tp, 1)

                in_product("mix0", q, {b: (lambda b=b: block_t(b - 1)) for b in range(1, 7)})
                pe.wait_ge(gd_split, 2)
                for tt in range(TT):
                    rows = slice(tt * P, (tt + 1) * P)
                    for k in range(DK):
                        hi, lo = gd_wab_hi[:, k * 16:(k + 1) * 16], gd_wab_lo[:, k * 16:(k + 1) * 16]
                        dst = ps[:, 6, tt * 16:(tt + 1) * 16]
                        pe.matmul(dst, h_hi[:, k, rows], hi, start=(k == 0 and tt == 0), stop=False, skip_group_check=True)
                        pe.matmul(dst, h_hi[:, k, rows], lo, start=False, stop=False, skip_group_check=True)
                        done = pe.matmul(dst, h_lo[:, k, rows], hi, start=False, stop=True, skip_group_check=True)
                done.then_inc(gd_abp, 1)
                pe.wait_ge(gd_gg, 1)
                g = gd_g[:, 5, :, :].rearrange("p t h -> p (t h)")
                for n, name in enumerate(("cum", "chunk", "even", "odd")):
                    done = pe.matmul(ps[:, 7, n * 16:(n + 1) * 16], cst(name), g, start=(n == 0), stop=True,
                                     skip_group_check=True)
                done.then_inc(gd_gp, 1)

                for tt in range(TT):
                    one = 1 + tt
                    pe.wait_ge(gd_cs, 3)
                    if tt == 0:
                        pe.wait_ge(gd_in, TT * 7)
                        pe.wait_ge(gd_ts, 6)
                    else:
                        pe.wait_ge(gd_of, tt)
                    for n in range(3):
                        for f in range(4):
                            done = pe.transpose(ps[:, n, f * P:(f + 1) * P], gd_c[:, 4 * n + f, tt * P:(tt + 1) * P], ident)
                        done.then_inc(gd_q, 1)
                    pe.wait_ge(gd_gs, 1)
                    pe.wait_ge(gd_gbr, one)
                    for par in range(2):
                        for pair in range(4):
                            done = pe.matmul(ps[:, 6 + par, pair * P:(pair + 1) * P], gd_gb[:, 2 * pair + par, :],
                                             cst("cum"), start=True, stop=True)
                        done.then_inc(gd_bc, 1)
                    for n in range(4):
                        pe.wait_ge(gd_kn, 5 * tt + n + 1)
                        bank = (3, 4, 5, 0)[n]
                        if n == 3:
                            pe.wait_ge(gd_kn, 5 * tt + 5)
                        if n == 1 and tt:
                            pe.wait_ge(y_lo, y_before("mix0") + tt)
                        for f in range(4):
                            done = pe.transpose(ps[:, bank, f * P:(f + 1) * P], gd_tm[:, n, f * P:(f + 1) * P], ident)
                        done.then_inc(gd_ft, 1)
                    pe.wait_ge(gd_fa, 2 * one)
                    pe.wait_ge(gd_fv, 2 * one)
                    for bank, n in ((1, 1), (3, 2)):
                        for par in range(2):
                            rows = slice(64 * par, 64 * par + 64)
                            for pair in range(4):
                                done = pe.matmul(ps[:, bank + par, pair * P:(pair + 1) * P], gd_t[rows, 0, pair, :],
                                                 gd_t[rows, n, pair, :], start=(pair == 0), stop=True, skip_group_check=True)
                            done.then_inc(gd_kk, 1)

                    def units(par):
                        return range(4 * par, 4 * par + 4)

                    def bank_of(b, u):
                        return ps[:, b + u // 4, u % 4 * P:(u % 4 + 1) * P]

                    for par in range(2):
                        pe.wait_ge(gd_x1, 2 * tt + par + 1)
                        pe.wait_ge(gd_de, 2 * one)
                        for u in units(par):
                            done = pe.transpose(bank_of(6, u), gd_invt[:, u, :], ident)
                        done.then_inc(gd_xp, 1)
                    for level in range(2, 7):
                        n = 10 * tt + 2 * (level - 2)
                        for par in range(2):
                            pe.wait_ge(gd_mlr, 5 * tt + level - 1)
                            if level == 2:
                                pe.wait_ge(gd_xs, 2 * tt + par + 1)
                                pe.wait_ge(gd_m, 2 * one)
                            else:
                                pe.wait_ge(gd_iv, n - 2 + par + 1)
                            for u in units(par):
                                done = pe.matmul(bank_of(0, u), gd_ml[:, level % 2, u, :], gd_inv[:, u, :],
                                                 start=(u % 4 == 0), stop=True, skip_group_check=True)
                            done.then_inc(gd_pp, 1)
                        for par in range(2):
                            pe.wait_ge(gd_ps, n + par + 1)
                            pe.wait_ge(gd_a, 2 * one)
                            if level < 6:
                                for u in units(par):
                                    pe.matmul(bank_of(2, u), gd_invt[:, u, :], gd_p[:, u, :], start=(u % 4 == 0),
                                              stop=True, skip_group_check=True)
                            for u in units(par):
                                done = pe.matmul(bank_of(4, u), gd_p[:, u, :], gd_invt[:, u, :], start=(u % 4 == 0),
                                                 stop=True, skip_group_check=True)
                            done.then_inc(gd_qp, 1)
                    pe.wait_ge(gd_iv, 10 * one)
                    pe.wait_ge(gd_kz, 3 * one)
                    for u in range(8):
                        h = 2 * (u % 4) + u // 4
                        done = pe.matmul(ps[:, 0, h * 64:(h + 1) * 64], gd_invt[:, u, :], gd_tm[:, 4, h * 64:(h + 1) * 64],
                                         start=(u == 0), stop=True, skip_group_check=True)
                    done.then_inc(gd_up, 1)
                    for u in range(8):
                        par, pair = u // 4, u % 4
                        h = 2 * pair + par
                        done = pe.matmul(ps[64 * par:64 * par + 64, 1, pair * P:(pair + 1) * P],
                                         gd_tm[:, 5, h * 64:(h + 1) * 64], gd_invt[:, u, :],
                                         start=(pair == 0), stop=True, skip_group_check=True)
                    done.then_inc(gd_up, 1)
                    pe.wait_ge(gd_ws, one)
                    if tt == 0:
                        pe.wait_ge(gd_z0, 2)
                    for c in range(2):
                        n = 2 * tt + c
                        if n:
                            pe.wait_ge(gd_st, n)
                            pe.wait_ge(gd_os, n)
                        for bank, lhs in ((2, gd_wt), (3, None)):
                            for pair in range(4):
                                a = lhs[:, pair, :] if lhs is not None else gd_t[:, 3, pair, :]
                                done = pe.matmul(ps[:, bank, pair * P:(pair + 1) * P], a, gd_s[:, pair, :],
                                                 start=(pair == 0), stop=True, skip_group_check=True)
                            done.then_inc(gd_sp, 1)
                        pe.wait_ge(gd_vs, n + 1)
                        for pair in range(4):
                            cols = slice(pair * P, (pair + 1) * P)
                            done = pe.matmul(ps[:, 4, cols], gd_tm[:, 6 + c, cols], gd_vn[:, cols],
                                             start=(pair == 0), stop=True, skip_group_check=True)
                        done.then_inc(gd_dp, 1)
                    for u in range(8):
                        h = 2 * (u % 4) + u // 4
                        done = pe.matmul(ps[:, 5, h * 64:(h + 1) * 64], gd_at[:, u, :], gd_vn[:, h * 64:(h + 1) * 64],
                                         start=(u == 0), stop=True, skip_group_check=True)
                    done.then_inc(gd_op, 1)
                    pe.wait_ge(gd_st, 2 * one)
                    transpose_y("mix0", tt, gd_o[:, :], tiles=4)
                pe.wait_ge(gd_ybl, 1)
                out_product("mix0", out)

            def sparse_attention():
                q, out = prod["od_in"], prod["od_out"]

                def twice_t(bank, col, done_sem):
                    for g in range(4):
                        for tt in range(TT):
                            for half in range(2):
                                done = pe.matmul(ps[64 * half:64 * half + 64, bank + g // 2, g % 2 * T + tt * P:g % 2 * T + (tt + 1) * P],
                                                 ns_tm[:, tt, col + g * 64:col + (g + 1) * 64], ident,
                                                 start=(g % 2 == 0 and tt == 0), stop=True, skip_group_check=True)
                    done.then_inc(done_sem, 1)

                def query_t(n, bank, done_sem):
                    for f in range(2):
                        for tt in range(TT):
                            at_col = NS_COL["q"] + (2 * n + f) * P
                            done = pe.transpose(ps[:, bank, f * T + tt * P:f * T + (tt + 1) * P],
                                                ns_tm[:, tt, at_col:at_col + P], ident)
                    done.then_inc(done_sem, 1)

                def compressed_inputs():
                    pe.wait_ge(ns_in, TT)
                    pe.wait_ge(t_lo, at["mix1"][0] + 2)
                    twice_t(4, NS_COL["kc"], ns_cvt)
                    twice_t(6, NS_COL["vc"], ns_cvt)

                def compressed_hidden():
                    pe.wait_ge(ns_params, 16 * 5)
                    for kv in range(2):
                        pe.wait_ge(ns_x, 5 * (kv + 1))
                        for n in range(16):
                            done = pe.matmul(ps[0:64, 4 + kv, 0:256], ns_xp[:, kv, n // 8, n % 8, :], ns_w1[:, kv, n, :],
                                             start=(n == 0), stop=(n == 15))
                        done.then_inc(ns_hp, 1)

                def compressed_t():
                    pe.wait_ge(ns_hs, 2)
                    for kv in range(2):
                        for c in range(2):
                            done = pe.transpose(ps[:, 6, (2 * kv + c) * 64:(2 * kv + c + 1) * 64],
                                                ns_h[:, kv, c * P:(c + 1) * P], ident[0:64, 0:64])
                    done.then_inc(ns_htp, 1)
                    pe.wait_ge(ns_in, TT * 3)
                    query_t(0, 4, ns_qtp)
                    query_t(1, 5, ns_qtp)

                def compressed_kv():
                    pe.wait_ge(ns_hts, 1)
                    for c in range(2):
                        pe.matmul(ps[:, 6, 0:64], ns_w2k[:, c, :], ns_ht[:, 0, c, :], start=(c == 0), stop=(c == 1))
                    for c in range(2):
                        done = pe.matmul(ps[0:64, 7, 0:64], ns_ht[:, 1, c, :], ns_w2v[:, c, :],
                                         start=(c == 0), stop=(c == 1))
                    done.then_inc(ns_kvp, 1)
                    for n in range(2, 4):
                        pe.wait_ge(ns_qts, n - 1)
                        query_t(n, 2 + n, ns_qtp)

                in_product("mix1", q, {1: compressed_inputs, 2: compressed_hidden, 3: compressed_t, 4: compressed_kv})
                pe.wait_ge(ns_kvs, 3)
                pe.wait_ge(ns_split, 2)
                for tt in range(TT):
                    rows = slice(tt * P, (tt + 1) * P)
                    for k in range(DK):
                        hi, lo = ns_wg_hi[:, k * 48:(k + 1) * 48], ns_wg_lo[:, k * 48:(k + 1) * 48]
                        dst = ps[:, 7, tt * 48:(tt + 1) * 48]
                        first = k == 0 and tt == 0
                        pe.matmul(dst, h_hi[:, k, rows], hi, start=first, stop=False, skip_group_check=True)
                        pe.matmul(dst, h_hi[:, k, rows], lo, start=False, stop=False, skip_group_check=True)
                        done = pe.matmul(dst, h_lo[:, k, rows], hi, start=False, stop=True, skip_group_check=True)
                done.then_inc(ns_gp, 1)
                pe.wait_ge(ns_qts, 4)
                pe.wait_ge(ns_in, TT * 5)
                pe.wait_ge(ns_krope, 24)
                twice_t(4, NS_COL["ks"], ns_rtp)
                pe.wait_ge(ns_rope, 6)
                for n in range(4):
                    query_t(n, n, ns_rtp)
                pe.wait_ge(ns_gs, 1)
                twice_t(6, NS_COL["kw"], ns_rtp)
                pe.wait_ge(ns_rts, 6)

                def group_scores(u):
                    tt, br, g = ns_units[u]
                    if u >= 2:
                        pe.wait_ge(ns_m, 4 * (u - 1))
                    keys = (tt + 1) * P
                    for jh in range(2):
                        for par in range(2):
                            rows = slice(64 * par, 64 * par + 64)
                            done = pe.matmul(ps[:, 2 * (u % 2) + par, jh * keys:(jh + 1) * keys],
                                             ns_qrt[rows, 2 * g + jh, tt * P:(tt + 1) * P], ns_kt[rows, br, g, 0:keys],
                                             start=(jh == 0), stop=True, skip_group_check=True)
                    done.then_inc(ns_s, 1)

                def weights_t(u):
                    tt, br, g = ns_units[u]
                    pe.wait_ge(ns_w, u + 1)
                    if u:
                        pe.wait_ge(ns_ts, u)
                    for j in range(4):
                        for kt in range(tt + 1):
                            n = j * (tt + 1) + kt
                            done = pe.transpose(ps[:, 4 + n // 4, n % 4 * P:(n % 4 + 1) * P],
                                                ns_p[:, u % 2, j, kt * P:(kt + 1) * P], ident)
                    done.then_inc(ns_tp, 1)

                def values(u):
                    tt, br, g = ns_units[u]
                    pe.wait_ge(ns_ts, u + 1)
                    col = (NS_COL["vs"], NS_COL["vw"])[br] + g * 64
                    for j in range(4):
                        h = 4 * g + j
                        for kt in range(tt + 1):
                            done = pe.matmul(ps[:, 6 + h // 8, h % 8 * 64:(h % 8 + 1) * 64],
                                             ns_pt[:, u % 2, j * (tt + 1) + kt, :], ns_tm[:, kt, col:col + 64],
                                             start=False, stop=True, skip_group_check=True)
                    done.then_inc(ns_pv, 1)

                def compressed_scores(tt):
                    for h in range(16):
                        par, pair = h % 2, h // 2
                        rows = slice(64 * par, 64 * par + 64)
                        done = pe.matmul(ps[:, 4 + par, pair * 16:(pair + 1) * 16], ns_qt[rows, pair, tt * P:(tt + 1) * P],
                                         ns_kct[rows, h // 4 * 16:(h // 4 + 1) * 16],
                                         start=(pair == 0), stop=True, skip_group_check=True)
                    done.then_inc(ns_cs, 1)

                def compressed_values(tt):
                    pe.wait_ge(ns_cd, 9 * (tt + 1))
                    for j in range(4):
                        done = pe.transpose(ps[0:64, 4, j * P:(j + 1) * P], ns_c[:, j * 64:(j + 1) * 64], ident)
                    done.then_inc(ns_ctp, 1)
                    pe.wait_ge(ns_cts, tt + 1)
                    if tt:
                        pe.wait_ge(y_tm, y_before("mix1") + tt)
                    for gb in range(2):
                        for j in range(4):
                            dst = ps[:, 6 + gb, :].rearrange("p (g j d) -> p g j d", g=2, j=4)[:, :, j, :]
                            pe.matmul(dst, ns_cpt[:, j, :], ns_vc[:, 2 * gb:2 * gb + 2, :], start=(j == 0), stop=True,
                                      skip_group_check=True)

                n = len(ns_units)
                for tt in range(TT):
                    first = tt * n // TT
                    if tt:
                        pe.wait_ge(ns_ts, first)
                    compressed_scores(tt)
                    group_scores(first)
                    if tt:
                        values(first - 1)
                    compressed_values(tt)
                    for u in range(first, first + n // TT):
                        if u + 1 < first + n // TT:
                            group_scores(u + 1)
                        weights_t(u)
                        if u > first:
                            values(u - 1)
                values(n - 1)
                for tt in range(TT):
                    transpose_y("mix1", tt, ns_o[:, tt, :])
                out_product("mix1", out)

            for layer in layers:
                if layer[:3] == "mlp":
                    hidden_layer(layer, 4)
                elif layer[:3] == "ffn":
                    hidden_layer(layer, 2)
                elif layer == "mix0":
                    delta_rule()
                elif layer == "mix1":
                    sparse_attention()
                elif layer == "sgu":
                    spatial_gating()
                elif layer == "kv":
                    in_product("kv", prod["kv"])
                elif layer == "sb":
                    stick_breaking()

        @block.scalar
        def _(act):
            def split(q, b, bs, i, j):
                static = q.panel + q.per * bs + j
                panel = q.panel + q.per * b + j
                half = min(PK, q.kt - PK * j) // 2 * NB
                act.wait_ge(raw_full[static % RING], 16 * (static // RING + 1) + 16 * i)
                if static >= 2:
                    act.wait_ge(w_used, panel - 1)
                for s in range(2):
                    part = slice(s * half, (s + 1) * half)
                    act.activation(w_hi[:, static % 2, part], raw[:, static % RING, part],
                                   ACT.Copy).then_inc(hi_ready, 1)

            def norm_store(layer, half):
                t0 = at[layer][0]
                n = NORMS.index(layer)
                act.wait_ge(tps_ready, t0 + half + 1)
                for f in range(4):
                    k = 4 * half + f
                    done = act.activation(h_hi[:, k, :], tps[:, f, :], ACT.Copy, scale=norm_t[:, n, k:k + 1])
                done.then_inc(t_hi, 1)

            def square_sums(layer):
                _, x0, r0 = at[layer]
                if x0:
                    act.wait_ge(x_ready, x0)
                for tt in range(TT):
                    if tt:
                        act.wait_ge(ss_ready, TT * r0 + tt)
                    act.activation(junk[:, :], x_sb[:, tt, :], ACT.Square,
                                   accum_out=ss[:, tt:tt + 1]).then_inc(ss_ready, 1)

            def enter(layer, q):
                if at[layer][1] == 0:
                    act.wait_ge(params_loaded, 32)
                split(q, 0, 0, 0, 0)
                if layer not in early:
                    norm_store(layer, 0)
                norm_store(layer, 1)
                split(q, 0, 0, 0, 1)
                square_sums(layer)
                act.wait_ge(rstd_ready, at[layer][2] + 1)

            def hidden_layer(layer, f_count):
                up, down = prod[layer + "_up"], prod[layer + "_down"]
                t0 = at[layer][0] + 2

                def evacuate(b, bs):
                    act.wait_ge(w_used, up.panel + up.per * (b + 1))
                    bank = acc[(up.block + bs) % 2]
                    for tt in range(TT):
                        if f_count == 4:
                            done = act.activation(tm[:, tt, :], bank[tt], ACT.Relu, scale=rstd[:, tt:tt + 1])
                        else:
                            done = act.activation(tm[:, tt, 0:256], bank[tt][:, 0:256], ACT.Silu,
                                                  scale=rstd[:, tt:tt + 1])
                        done.then_inc(act_tm, 1)

                def store_t(b):
                    act.wait_ge(tps_ready, t0 + b + 1)
                    act.activation(hid_hi2[:, bass.ds(b * (f_count * T), f_count * T)],
                                   tps[:, 0:f_count, :].rearrange("p f t -> p (f t)"), ACT.Copy).then_inc(t_hi, 1)

                enter(layer, up)

                def body(b, bs, i):
                    split(up, b, bs, i, 0)
                    split(up, b, bs, i, 1)
                    evacuate(b - 1, bs - 1)
                    store_t(b - 1)

                body(1, 1, 0)
                pairs, rest = steps(2, up.blocks)
                with act.Fori(0, pairs) as i:
                    for k in range(2):
                        body(2 + 2 * i + k, 2 + k, i)
                for b in range(rest, up.blocks):
                    body(b, b, 0)
                for b in range(down.blocks):
                    for j in range(down.per):
                        if b == 0 and j == 2:
                            evacuate(up.blocks - 1, up.blocks - 1)
                            store_t(up.blocks - 1)
                        if b == 1 and j == 4 and early_norm(layer):
                            norm_store(early_norm(layer), 0)
                        split(down, b, b, 0, j)

            def in_product(layer, q, out, evacuate, between={}):
                enter(layer, q)
                for b in range(1, q.blocks):
                    for j in range(q.per):
                        split(q, b, b, 0, j)
                    evacuate(b - 1)
                    if b in between:
                        between[b]()
                if out:
                    split(out, 0, 0, 0, 0)
                    split(out, 0, 0, 0, 1)
                evacuate(q.blocks - 1)

            def copy_block(q, dst, done_sem, func=ACT.Copy):
                def evacuate(b):
                    act.wait_ge(w_used, q.panel + q.per * (b + 1))
                    for tt in range(TT):
                        act.activation(dst(tt, b), acc[(q.block + b) % 2][tt], func,
                                       scale=rstd[:, tt:tt + 1]).then_inc(done_sem, 1)
                return evacuate

            def out_product(q):
                for b in range(q.blocks):
                    for j in range(q.per):
                        if b or j >= 2:
                            split(q, b, b, 0, j)

            def store_y(layer, tt, tiles=8, first=0):
                n = y_before(layer) + tt
                act.wait_ge(y_tps, n + 1)
                act.activation(h_hi[:, first:first + tiles, tt * P:(tt + 1) * P],
                               two[4].rearrange("p b n -> p (b n)").rearrange("p (f t) -> p f t", t=P)[:, 0:tiles, :],
                               ACT.Copy).then_inc(y_hi, 1)

            def spatial_gating():
                q, out = prod["sgu_in"], prod["sgu_out"]
                t0 = at["sgu"][0] + 2
                enter("sgu", q)

                def evacuate(b):
                    act.wait_ge(w_used, q.panel + q.per * (b + 1))
                    for tt in range(TT):
                        sums = {"accum_out": v_sums[:, tt, b:b + 1]} if b < 4 else {}
                        act.activation(sgu_z[:, tt, b * NB:(b + 1) * NB], acc[(q.block + b) % 2][tt],
                                       ACT.Gelu_apprx_tanh, scale=rstd[:, tt:tt + 1], **sums).then_inc(sgu_in, 1)

                for b in range(1, q.blocks):
                    for j in range(q.per):
                        split(q, b, b, 0, j)
                    evacuate(b - 1)
                    if b == 5:
                        act.wait_ge(sgu_mean, 2)
                        for tt in range(TT):
                            for half in range(2):
                                if tt or half:
                                    act.wait_ge(sgu_sq, 2 * tt + half)
                                act.activation(junk[:, :], sgu_z[:, tt, half * D:(half + 1) * D], ACT.Square,
                                               bias=v_stat[:, 0, tt:tt + 1],
                                               accum_out=v_sq[:, tt, half:half + 1]).then_inc(sgu_sq, 1)
                split(out, 0, 0, 0, 0)
                split(out, 0, 0, 0, 1)
                evacuate(q.blocks - 1)
                for b in range(out.blocks):
                    for j in range(out.per):
                        if b == 0:
                            act.wait_ge(tps_ready, t0 + j + 1)
                            act.activation(hid_hi2[:, 4 * j * T:4 * (j + 1) * T], tps.rearrange("p f t -> p (f t)"),
                                           ACT.Copy).then_inc(t_hi, 1)
                            if j >= 1 and j + 1 < out.per:
                                split(out, b, b, 0, j + 1)
                        else:
                            split(out, b, b, 0, j)

            def stick_breaking():
                q, out = prod["sb_q"], prod["sb_out"]
                in_product("sb", q, out, copy_block(q, lambda tt, b: sb_q[:, tt, b * NB:(b + 1) * NB], sb_in))
                for n in range(6):
                    dst = sb_qt[:, 2 * n:2 * n + 2, :] if n < 4 else sb_kt[:, 2 * (n - 4):2 * (n - 4) + 2, :]
                    act.wait_ge(sb_tp, n + 1)
                    act.activation(dst.rearrange("p f t -> p (f t)"), ps[:, 4 + n % 2, :], ACT.Copy).then_inc(sb_ts, 1)
                for u in range(len(sb_units)):
                    soft = sb_s[:, u % 3, 1, :, :].rearrange("p a b -> p (a b)")
                    act.wait_ge(sb_abs, u + 1)
                    act.activation(soft, soft, ACT.Exp, scale=-1.0).then_inc(sb_ln, 1)
                    act.wait_ge(sb_ln, 2 * u + 1)
                    act.activation(soft, soft, ACT.Ln, bias=1.0).then_inc(sb_ln, 1)
                    if u:
                        weights(u - 1)
                weights(len(sb_units) - 1)
                for tt in range(TT):
                    store_y("sb", tt)
                out_product(out)

            def weights(u):
                z = sb_s[:, u % 3, 0, :, :].rearrange("p a b -> p (a b)")
                act.wait_ge(sb_arg, u + 1)
                act.activation(z, z, ACT.Exp).then_inc(sb_a, 1)
                g, qt, kt = sb_units[u]
                if g == 3 and kt == 0:
                    act.wait_ge(sb_av, u + 1)
                    act.activation(sb_o[:, qt, :], two[6].rearrange("p b n -> p (b n)"), ACT.Copy).then_inc(y_tm, 1)

            def delta_rule():
                q, out = prod["ev_in"], prod["ev_out"]

                def evacuate(b):
                    act.wait_ge(w_used, q.panel + q.per * (b + 1))
                    if 0 < b < 6:
                        act.wait_ge(gd_tp, b)
                    for tt in range(TT):
                        dst, func = (tm[:, tt, :], ACT.Copy) if b < 6 else (gd_z[:, tt, :], ACT.Silu)
                        act.activation(dst, acc[(q.block + b) % 2][tt], func, scale=rstd[:, tt:tt + 1]).then_inc(gd_in, 1)

                def store(n):
                    if n == 4:
                        return
                    dst = (gd_x[:, 0:4, 3:], gd_x[:, 4:8, 3:], gd_x[:, 8:12, 3:], gd_ch[:, :, 2:], None, gd_b[:, :, :])[n]
                    act.wait_ge(gd_tp, n + 1)
                    if n == 5:
                        act.wait_ge(gd_ts, 5)
                    act.activation(dst, tps, ACT.Copy).then_inc(gd_ts, 1)

                def silu(n):
                    c = gd_c[:, 4 * n:4 * n + 4, :].rearrange("p f t -> p (f t)")
                    act.wait_ge(gd_cv, n + 1)
                    act.activation(c, c, ACT.Silu).then_inc(gd_cs, 1)

                def between(b):
                    store(b - 1)
                    if 3 <= b <= 5:
                        silu(b - 3)
                    if b == 1:
                        act.wait_ge(gd_params, 16 * 6)
                        act.activation(gd_wab_hi[:, :], gd_wab[:, :], ACT.Copy).then_inc(gd_split, 1)

                in_product("mix0", q, out, evacuate, {b: (lambda b=b: between(b)) for b in range(1, 7)})
                act.activation(gd_a_log[:, :], gd_a_log[:, :], ACT.Exp).then_inc(gd_ge, 1)
                act.wait_ge(gd_ga, 1)
                act.activation(gd_g[:, 2, :, :], gd_g[:, 2, :, :], ACT.Exp, scale=-1.0).then_inc(gd_ge, 1)
                act.activation(gd_g[:, 3, :, :], gd_g[:, 1, :, :], ACT.Exp, scale=-1.0).then_inc(gd_ge, 1)
                act.wait_ge(gd_ge, 2)
                act.activation(gd_g[:, 4, :, :], gd_g[:, 2, :, :], ACT.Ln, bias=1.0).then_inc(gd_ge, 1)
                act.wait_ge(gd_gs, 1)
                act.activation(gd_exp[:, :, :, :], gd_sum[:, :, :, :], ACT.Exp).then_inc(gd_gx, 1)
                act.wait_ge(gd_yb, 1)
                act.wait_ge(gd_abp, 1)
                act.activation(h_hi[:, 4:8, :], gd_sc[:, :, :], ACT.Copy).then_inc(gd_ybh, 1)

                for tt in range(TT):
                    one = 1 + tt
                    for n in range(2):
                        act.wait_ge(gd_q, 3 * tt + n + 1)
                        act.activation(gd_sq[:, n, :], ps[:, n, :], ACT.Square).then_inc(gd_qq, 1)
                    for par in range(2):
                        act.wait_ge(gd_da, 2 * tt + par + 1)
                        d = gd_dt[:, 4 * par:4 * par + 4, :]
                        act.activation(d, d, ACT.Exp).then_inc(gd_de, 1)
                    for n, bank in ((0, 3), (2, 5)):
                        act.wait_ge(gd_ft, 4 * tt + n + 1)
                        act.activation(gd_t[:, n, :, :].rearrange("p f t -> p (f t)"), ps[:, bank, :],
                                       ACT.Copy).then_inc(gd_fa, 1)
                    for par in range(2):
                        act.wait_ge(gd_xp, 2 * tt + par + 1)
                        act.activation(gd_inv[:, 4 * par:4 * par + 4, :].rearrange("p u t -> p (u t)"), ps[:, 6 + par, :],
                                       ACT.Copy).then_inc(gd_xs, 1)
                    for n in range(10):
                        par = n % 2
                        act.wait_ge(gd_pp, 10 * tt + n + 1)
                        act.activation(gd_p[:, 4 * par:4 * par + 4, :].rearrange("p u t -> p (u t)"), ps[:, par, :],
                                       ACT.Copy).then_inc(gd_ps, 1)
                    act.wait_ge(gd_up, 2 * tt + 1)
                    act.activation(gd_u[:, :], ps[:, 0, :], ACT.Copy).then_inc(gd_us, 1)
                    for c in range(2):
                        rows = slice(64 * c, 64 * c + 64)
                        act.wait_ge(gd_sp, 4 * tt + 2 * c + 2)
                        act.activation(gd_o[rows, :], ps[rows, 3, :], ACT.Copy).then_inc(gd_os, 1)
                    act.wait_ge(gd_of, one)
                    act.activation(gd_osq[:, :], gd_o[:, :], ACT.Square).then_inc(gd_oq, 1)
                    store_y("mix0", tt, tiles=4)
                out_product(out)

            def sparse_attention():
                q, out = prod["od_in"], prod["od_out"]

                def split_gate_weights():
                    act.wait_ge(ns_params, 16 * 5)
                    act.activation(ns_wg_hi[:, :], ns_wg[:, :], ACT.Copy).then_inc(ns_split, 1)

                def compressed_silu():
                    for kv in range(2):
                        act.wait_ge(ns_hp, kv + 1)
                        act.activation(ns_h[:, kv, :], ps[0:64, 4 + kv, 0:256], ACT.Silu).then_inc(ns_hs, 1)

                def store_query(n, bank):
                    act.wait_ge(ns_qtp, n + 1)
                    act.activation(ns_qt[:, 2 * n:2 * n + 2, :].rearrange("p f t -> p (f t)"), ps[:, bank, :],
                                   ACT.Copy).then_inc(ns_qts, 1)

                def queries(first):
                    for n in range(first, first + 2):
                        store_query(n, 4 + n % 2)

                in_product("mix1", q, out, copy_block(q, lambda tt, b: ns_tm[:, tt, b * NB:(b + 1) * NB], ns_in),
                           {1: split_gate_weights, 2: compressed_silu, 3: lambda: queries(0), 4: lambda: queries(2)})
                act.wait_ge(ns_gp, 1)
                for tt in range(TT):
                    done = act.activation(ns_gate[:, tt, :], ps[:, 7, tt * 48:(tt + 1) * 48], ACT.Sigmoid,
                                          scale=rstd[:, tt:tt + 1])
                done.then_inc(ns_gs, 1)

                act.wait_ge(ns_rtp, 1)
                act.activation(ns_kt[:, 0, :, :].rearrange("p g t -> p (g t)"), two[4].rearrange("p b n -> p (b n)"),
                               ACT.Copy).then_inc(ns_rts, 1)
                for n in range(4):
                    act.wait_ge(ns_rtp, n + 2)
                    act.activation(ns_qrt[:, 2 * n:2 * n + 2, :].rearrange("p f t -> p (f t)"), ps[:, n, :],
                                   ACT.Copy).then_inc(ns_rts, 1)
                act.wait_ge(ns_rtp, 6)
                act.activation(ns_kt[:, 1, :, :].rearrange("p g t -> p (g t)"), two[6].rearrange("p b n -> p (b n)"),
                               ACT.Copy).then_inc(ns_rts, 1)

                n = len(ns_units)

                def exps(u):
                    tt, br, g = ns_units[u]
                    keys = (tt + 1) * P
                    act.wait_ge(ns_nm, u + 1)
                    for j in range(4):
                        act.activation(ns_p[:, u % 2, j, 0:keys], ns_p[:, u % 2, j, 0:keys], ACT.Exp, scale=0.125,
                                       bias=ns_st[:, 1 + 4 * (u % 2), j:j + 1],
                                       accum_out=ns_st[:, 2 + 4 * (u % 2), j:j + 1]).then_inc(ns_e, 1)

                def store_weights(u):
                    tt, br, g = ns_units[u]
                    if u >= 2:
                        act.wait_ge(ns_pv, u - 1)
                    act.wait_ge(ns_tp, u + 1)
                    act.activation(ns_pt[:, u % 2, 0:4 * (tt + 1), :].rearrange("p n t -> p (n t)"),
                                   two[4].rearrange("p b n -> p (b n)")[:, 0:4 * (tt + 1) * P], ACT.Copy).then_inc(ns_ts, 1)

                for tt in range(TT):
                    first = tt * n // TT
                    act.wait_ge(ns_cd, 9 * tt + 4)
                    act.activation(ns_c[:, :], ns_c[:, :], ACT.Exp, scale=0.125).then_inc(ns_ce, 1)
                    exps(first)
                    act.wait_ge(ns_ctp, tt + 1)
                    act.activation(ns_cpt[:, :, :].rearrange("p j t -> p (j t)"), ps[0:64, 4, :], ACT.Copy).then_inc(ns_cts, 1)
                    for u in range(first, first + n // TT):
                        if u + 1 < first + n // TT:
                            exps(u + 1)
                        store_weights(u)
                    act.wait_ge(ns_pv, first + n // TT)
                    act.activation(ns_o[:, tt, :], two[6].rearrange("p b n -> p (b n)"), ACT.Copy).then_inc(y_tm, 1)
                for tt in range(TT):
                    store_y("mix1", tt)
                out_product(out)

            for layer in layers:
                if layer[:3] == "mlp":
                    hidden_layer(layer, 4)
                elif layer[:3] == "ffn":
                    hidden_layer(layer, 2)
                elif layer[:3] == "fin":
                    square_sums(layer)
                elif layer == "mix0":
                    delta_rule()
                elif layer == "mix1":
                    sparse_attention()
                elif layer == "sgu":
                    spatial_gating()
                elif layer == "kv":
                    in_product("kv", prod["kv"], None, copy_block(prod["kv"], lambda tt, b: kv_tm[:, tt, :], kv_in))
                elif layer == "sb":
                    stick_breaking()

        @block.vector
        def _(dve):
            def split(q, b, bs, i, j):
                static = q.panel + q.per * bs + j
                panel = q.panel + q.per * b + j
                half = min(PK, q.kt - PK * j) // 2 * NB
                for s in range(2):
                    part = slice(s * half, (s + 1) * half)
                    dve.wait_ge(hi_ready, 2 * panel + s + 1)
                    dve.tensor_tensor(w_lo[:, static % 2, part], raw[:, static % RING, part],
                                      w_hi[:, static % 2, part].bitcast(F32), ALU.subtract).then_inc(lo_ready, 1)

            def norm_store(layer, half):
                t0 = at[layer][0]
                n = NORMS.index(layer)
                dve.wait_ge(t_hi, t0 + half + 1)
                for f in range(4):
                    k = 4 * half + f
                    done = dve.scalar_tensor_tensor(h_lo[:, k, :], tps[:, f, :], norm_t[:, n, k:k + 1],
                                                    h_hi[:, k, :].bitcast(F32), ALU.mult, ALU.subtract)
                done.then_inc(t_lo, 1)

            pending = []

            def residual():
                if not pending:
                    return
                q, b, scale = pending.pop()
                dve.wait_ge(w_used, q.panel + q.per * (b + 1))
                bank = acc[(q.block + b) % 2]
                for tt in range(TT):
                    cols = x_sb[:, tt, b * NB:(b + 1) * NB]
                    dve.scalar_tensor_tensor(cols, bank[tt], scale, cols, ALU.mult, ALU.add).then_inc(x_ready, 1)

            def enter(layer, q):
                if at[layer][1] == 0:
                    dve.wait_ge(params_loaded, 32)
                split(q, 0, 0, 0, 0)
                residual()
                if layer not in early:
                    norm_store(layer, 0)
                norm_store(layer, 1)
                split(q, 0, 0, 0, 1)

            def hidden_layer(layer, f_count, scale):
                up, down = prod[layer + "_up"], prod[layer + "_down"]
                t0 = at[layer][0] + 2
                h0 = hidden_before[layer]

                def evacuate(b, bs):
                    bank = acc[(up.block + bs) % 2]
                    if f_count == 4:
                        dve.wait_ge(act_tm, 2 * (h0 + b + 1))
                        dve.tensor_tensor(tm[:, :, :], tm[:, :, :], tm[:, :, :], ALU.mult).then_inc(tm_ready, 1)
                        return
                    if b is not None:
                        dve.wait_ge(act_tm, 2 * (h0 + b + 1))
                    for tt in range(TT):
                        gate = tm[:, tt, 0:256]
                        done = dve.scalar_tensor_tensor(gate, bank[tt][:, 256:512], rstd[:, tt:tt + 1], gate,
                                                        ALU.mult, ALU.mult)
                    done.then_inc(tm_ready, 1)

                def store_t(b):
                    dve.wait_ge(t_hi, t0 + b + 1)
                    cols = bass.ds(b * (f_count * T), f_count * T)
                    dve.tensor_tensor(hid_lo2[:, cols], tps[:, 0:f_count, :].rearrange("p f t -> p (f t)"),
                                      hid_hi2[:, cols].bitcast(F32), ALU.subtract).then_inc(t_lo, 1)

                enter(layer, up)

                def body(b, bs, i):
                    split(up, b, bs, i, 0)
                    split(up, b, bs, i, 1)
                    evacuate(b - 1, bs - 1)
                    store_t(b - 1)

                body(1, 1, 0)
                pairs, rest = steps(2, up.blocks)
                with dve.Fori(0, pairs) as i:
                    for k in range(2):
                        body(2 + 2 * i + k, 2 + k, i)
                for b in range(rest, up.blocks):
                    body(b, b, 0)
                for b in range(down.blocks):
                    for j in range(down.per):
                        if b == 0 and j == 2:
                            evacuate(up.blocks - 1, up.blocks - 1)
                            store_t(up.blocks - 1)
                        if b == 1 and j == 2:
                            residual()
                        if b == 1 and j == 4 and early_norm(layer):
                            norm_store(early_norm(layer), 0)
                        split(down, b, b, 0, j)
                    pending.append((down, b, scale))

            def final_norm(layer):
                _, x0, r0 = at[layer]
                residual()
                dve.wait_ge(rstd_ready, r0 + 1)
                dve.wait_ge(row_loaded if layer == "fin1" or "fin1" not in layers else row2_loaded, 16)
                for tt in range(TT):
                    dve.scalar_tensor_tensor(x_sb[:, tt, :], x_sb[:, tt, :], rstd[:, tt:tt + 1], row[:, :],
                                             ALU.mult, ALU.mult).then_inc(x_ready, 1)

            def in_product(layer, q, out, between={}):
                enter(layer, q)
                for b in range(1, q.blocks):
                    for j in range(q.per):
                        split(q, b, b, 0, j)
                    if b in between:
                        between[b]()
                if out:
                    split(out, 0, 0, 0, 0)
                    split(out, 0, 0, 0, 1)

            def out_product(q, wait_first=2):
                for b in range(q.blocks):
                    for j in range(q.per):
                        if b or j >= wait_first:
                            split(q, b, b, 0, j)
                        if b == 1 and j == 1:
                            residual()
                    pending.append((q, b, 1.0))

            def store_y(layer, tt, tiles=8, first=0):
                n = y_before(layer) + tt
                dve.wait_ge(y_hi, n + 1)
                cols = (slice(None), slice(first, first + tiles), slice(tt * P, (tt + 1) * P))
                dve.tensor_tensor(h_lo[cols],
                                  two[4].rearrange("p b n -> p (b n)").rearrange("p (f t) -> p f t", t=P)[:, 0:tiles, :],
                                  h_hi[cols].bitcast(F32), ALU.subtract).then_inc(y_lo, 1)

            def spatial_gating():
                q, out = prod["sgu_in"], prod["sgu_out"]
                t0 = at["sgu"][0] + 2
                enter("sgu", q)
                for b in range(1, q.blocks):
                    for j in range(q.per):
                        if (b, j) != (7, 0):
                            split(q, b, b, 0, j)
                    if b == 4:
                        dve.wait_ge(sgu_in, TT * 4)
                        dve.tensor_reduce(v_stat[:, 1, :], v_sums[:, :, :], AXX, ALU.add).then_inc(sgu_mean, 1)
                        dve.wait_ge(sgu_mean, 1)
                        dve.tensor_scalar(v_stat[:, 0, :], v_stat[:, 1, :], -1.0 / (2 * D), None,
                                          ALU.mult).then_inc(sgu_mean, 1)
                    if b == 6:
                        dve.wait_ge(sgu_rs, 3)
                        dve.wait_ge(sgu_params, 64)
                        for tt in range(TT):
                            v = sgu_z[:, tt, 0:2 * D]
                            dve.tensor_scalar(v, v, v_stat[:, 0, tt:tt + 1], v_stat[:, 2, tt:tt + 1], ALU.add,
                                              ALU.mult).then_inc(sgu_v, 1)
                            dve.wait_ge(sgu_v, 3 * tt + 1)
                            dve.tensor_tensor(v, v, ln_rows[:, 0, :], ALU.mult).then_inc(sgu_v, 1)
                            dve.wait_ge(sgu_v, 3 * tt + 2)
                            dve.tensor_tensor(v, v, ln_rows[:, 1, :], ALU.add).then_inc(sgu_v, 1)
                            if tt == 0:
                                split(q, 7, 7, 0, 0)
                split(out, 0, 0, 0, 0)
                split(out, 0, 0, 0, 1)
                dve.wait_ge(sgu_in, TT * 8)

                def gate(pair):
                    for tt in range(TT):
                        dve.wait_ge(sgu_mix, TT * pair + tt + 1)
                        for g in range(2):
                            u = sgu_z[:, tt, 2 * D + (2 * pair + g) * 256:2 * D + (2 * pair + g + 1) * 256]
                            done = dve.scalar_tensor_tensor(u, ps[:, 6 + tt, g * 256:(g + 1) * 256],
                                                            bs_t[:, 2 * pair + g:2 * pair + g + 1], u, ALU.add, ALU.mult)
                        done.then_inc(sgu_s, 1)

                def store(j):
                    dve.wait_ge(t_hi, t0 + j + 1)
                    dve.tensor_tensor(sgu_lo[:, 4 * j:4 * (j + 1), :], tps, hid_hi[:, 4 * j:4 * (j + 1), :].bitcast(F32),
                                      ALU.subtract).then_inc(t_lo, 1)

                gate(0)
                gate(1)
                store(0)
                gate(2)
                store(1)
                split(out, 0, 0, 0, 2)
                gate(3)
                store(2)
                split(out, 0, 0, 0, 3)
                store(3)
                out_product(out, wait_first=4)

            def stick_breaking():
                q, out = prod["sb_q"], prod["sb_out"]
                in_product("sb", q, out)
                n = len(sb_units)

                def masked_scores(u):
                    g, qt, kt = sb_units[u]
                    z, soft = sb_s[:, u % 3, 0, :, :], sb_s[:, u % 3, 1, :, :]
                    dve.wait_ge(sb_z, u + 1)
                    if u >= 3:
                        dve.wait_ge(sb_av, u - 2)
                    src = ps[:, 2 * (u % 2):2 * (u % 2) + 2, 0:256]
                    if kt == qt:
                        for par in range(2):
                            done = dve.scalar_tensor_tensor(
                                z[:, par, :].rearrange("p (h t) -> p h t", t=P), src[:, par, :].rearrange("p (h t) -> p h t", t=P), 0.125,
                                cst("not_earlier").unsqueeze(1).broadcast_to([P, 2, P]), ALU.mult, ALU.add)
                    else:
                        done = dve.tensor_scalar(z, src, 0.125, None, ALU.mult)
                    done.then_inc(sb_zm, 1)
                    dve.wait_ge(sb_zm, u + 1)
                    dve.scalar_tensor_tensor(soft, z, -1.0, z, ALU.mult, ALU.max).then_inc(sb_abs, 1)

                def softplus(u):
                    z = sb_s[:, u % 3, 0, :, :].rearrange("p a b -> p (a b)")
                    soft = sb_s[:, u % 3, 1, :, :].rearrange("p a b -> p (a b)")
                    dve.wait_ge(sb_ln, 2 * u + 2)
                    dve.scalar_tensor_tensor(soft, z, 0.0, soft, ALU.max, ALU.add).then_inc(sb_sp, 1)

                def log_weights(u):
                    z = sb_s[:, u % 3, 0, :, :].rearrange("p a b -> p (a b)")
                    dve.wait_ge(sb_rev, u + 1)
                    dve.tensor_tensor(z, z, ps[:, 4, :], ALU.subtract).then_inc(sb_arg, 1)

                masked_scores(0)
                for u in range(n):
                    softplus(u)
                    if u + 1 < n:
                        masked_scores(u + 1)
                    log_weights(u)
                for tt in range(TT):
                    store_y("sb", tt)
                out_product(out)

            taken = [0]

            def step(ins):
                taken[0] += 1
                ins.then_inc(dve_step, 1)
                dve.wait_ge(dve_step, taken[0])

            def each_head(ap):
                return ap.rearrange("p (h d) -> p h d", d=64)

            def of_heads(ap):
                return ap.unsqueeze(2).broadcast_to([P, 8, 64])

            def delta_rule():
                q, out = prod["ev_in"], prod["ev_out"]

                def convolve(n):
                    dve.wait_ge(gd_ts, n + 1)
                    if n == 0:
                        dve.wait_ge(gd_params, 16 * 6)
                        dve.wait_ge(gd_pad, 2)
                    for tap in range(4):
                        for f in range(4 * n, 4 * n + 4):
                            src, dst, w = gd_x[:, f, tap:tap + T], gd_c[:, f, :], gd_cw[:, f, tap:tap + 1]
                            if tap == 0:
                                done = dve.tensor_scalar(dst, src, w, None, ALU.mult)
                            else:
                                done = dve.scalar_tensor_tensor(dst, src, w, dst, ALU.mult, ALU.add)
                        if tap < 3:
                            step(done)
                    done.then_inc(gd_cv, 1)

                def between(b):
                    if 2 <= b <= 4:
                        convolve(b - 2)
                    if b == 1:
                        dve.wait_ge(gd_split, 1)
                        dve.tensor_tensor(gd_wab_lo[:, :], gd_wab[:, :], gd_wab_hi[:, :].bitcast(F32),
                                          ALU.subtract).then_inc(gd_split, 1)
                    if b == 5:
                        dve.wait_ge(gd_tp, 5)
                        dve.tensor_tensor(gd_ch[:, :, 2:], gd_ch[:, :, 2:], tps, ALU.mult).then_inc(gd_ts, 1)
                    if b == 6:
                        dve.wait_ge(gd_ts, 5)
                        for tap in range(3):
                            for f in range(4):
                                src, dst, w = gd_ch[:, f, tap:tap + T], gd_sc[:, f, :], gd_scw[:, f, tap:tap + 1]
                                if tap == 0:
                                    done = dve.tensor_scalar(dst, src, w, None, ALU.mult)
                                else:
                                    done = dve.scalar_tensor_tensor(dst, src, w, dst, ALU.mult, ALU.add)
                            step(done)

                in_product("mix0", q, out, {b: (lambda b=b: between(b)) for b in range(1, 7)})
                dve.wait_ge(gd_ts, 6)
                dve.tensor_tensor(gd_sc[:, :, :], gd_sc[:, :, :], gd_b[:, :, :], ALU.mult).then_inc(gd_yb, 1)
                dve.wait_ge(gd_abp, 1)
                dve.wait_ge(rstd_ready, at["mix0"][2] + 1)
                for tt in range(TT):
                    r = rstd[:, tt:tt + 1]
                    dve.scalar_tensor_tensor(gd_g[:, 0, tt, :], ps[:, 6, tt * 16:tt * 16 + 8], r, gd_dt_bias[:, :],
                                             ALU.mult, ALU.add)
                    done = dve.tensor_scalar(gd_g[:, 1, tt, :], ps[:, 6, tt * 16 + 8:tt * 16 + 16], r, None, ALU.mult)
                step(done)
                dve.scalar_tensor_tensor(gd_g[:, 2, :, :], gd_g[:, 0, :, :], -1.0, gd_g[:, 0, :, :],
                                         ALU.mult, ALU.max).then_inc(gd_ga, 1)
                dve.wait_ge(gd_ge, 4)
                step(dve.scalar_tensor_tensor(gd_g[:, 4, :, :], gd_g[:, 0, :, :], 0.0, gd_g[:, 4, :, :], ALU.max, ALU.add))
                for tt in range(TT):
                    dve.scalar_tensor_tensor(gd_g[:, 5, tt, :], gd_g[:, 4, tt, :], -1.0, gd_a_log[:, :], ALU.mult, ALU.mult)
                step(dve.tensor_scalar(gd_g[:, 3, :, :], gd_g[:, 3, :, :], 1.0, None, ALU.add))
                dve.reciprocal(gd_g[:, 6, :, :], gd_g[:, 3, :, :]).then_inc(gd_gg, 1)
                dve.wait_ge(gd_gp, 1)
                sums = ps[:, 7, 0:64].rearrange("p (n t h) -> p n t h", n=4, t=TT)
                step(dve.tensor_copy(gd_sum[:, :, :, :], sums))
                dve.tensor_tensor(gd_sum[:, 1, :, :], gd_sum[:, 1, :, :], gd_sum[:, 0, :, :], ALU.subtract).then_inc(gd_gs, 1)
                dve.wait_ge(gd_gx, 1)
                dve.wait_ge(gd_gg, 1)
                dve.tensor_tensor(gd_g[:, 7, :, :], gd_g[:, 6, :, :], gd_exp[:, 0, :, :], ALU.mult)
                for par in range(2):
                    rows = slice(64 * par, 64 * par + 64)
                    dve.tensor_copy(gd_dec[rows, :, :, :].rearrange("p c t h -> p (c t) h"),
                                    gd_exp[rows, 2:4, :, :].rearrange("p c t (h r) -> p r (c t) h", r=2)[:, par])
                for c, name in enumerate(("even", "odd")):
                    done = dve.tensor_scalar(gd_ez[:, c, :, :], gd_exp[:, 1, :, :], cst(name)[:, 0:1], None, ALU.mult)
                done.then_inc(gd_gt, 1)
                dve.wait_ge(gd_ybh, 1)
                dve.tensor_tensor(h_lo[:, 4:8, :], gd_sc[:, :, :], h_hi[:, 4:8, :].bitcast(F32), ALU.subtract).then_inc(gd_ybl, 1)
                dve.wait_ge(gd_gt, 1)

                for tt in range(TT):
                    one = 1 + tt
                    dve.wait_ge(gd_qq, 2 * one)
                    dve.tensor_reduce(gd_rs[:, 0, :, :], gd_sq[:, :, :].rearrange("p n (h d) -> p n h d", d=64), AXX,
                                      ALU.add).then_inc(gd_qs, 1)
                    for par in range(2):
                        dve.wait_ge(gd_bc, 2 * tt + par + 1)
                        for pair in range(4):
                            h = 2 * pair + par
                            done = dve.scalar_tensor_tensor(gd_dt[:, 4 * par + pair, :], ps[:, 6 + par, pair * P:(pair + 1) * P],
                                                            gd_sum[:, 0, tt, h:h + 1], cst("not_later"), ALU.subtract, ALU.add)
                        done.then_inc(gd_da, 1)
                    beta, eg = of_heads(gd_g[:, 6, tt, :]), of_heads(gd_exp[:, 0, tt, :])
                    dve.wait_ge(gd_qr, one)
                    k, kb, qn, qe, vb = [each_head(gd_tm[:, n, :]) for n in range(5)]
                    dve.wait_ge(gd_q, 3 * one)
                    dve.tensor_tensor(k, each_head(ps[:, 1, :]), of_heads(gd_rs[:, 2, 1, :]), ALU.mult).then_inc(gd_kn, 1)
                    dve.wait_ge(gd_kn, 5 * tt + 1)
                    dve.tensor_tensor(kb, k, beta, ALU.mult).then_inc(gd_kn, 1)
                    dve.scalar_tensor_tensor(qn, each_head(ps[:, 0, :]), 0.125, of_heads(gd_rs[:, 2, 0, :]), ALU.mult,
                                             ALU.mult).then_inc(gd_kn, 1)
                    dve.wait_ge(gd_kn, 5 * tt + 3)
                    dve.tensor_tensor(qe, qn, eg, ALU.mult).then_inc(gd_kn, 1)
                    dve.tensor_tensor(vb, each_head(ps[:, 2, :]), beta, ALU.mult).then_inc(gd_kn, 1)
                    for n, bank in ((1, 4), (3, 0)):
                        dve.wait_ge(gd_ft, 4 * tt + n + 1)
                        dve.tensor_copy(gd_t[:, n, :, :].rearrange("p f t -> p (f t)"), ps[:, bank, :]).then_inc(gd_fv, 1)

                    def units(ap, par):
                        return ap[:, 4 * par:4 * par + 4, :]

                    def bank4(b):
                        return ps[:, b, :].rearrange("p (u t) -> p u t", t=P)

                    level1 = cst("level1").unsqueeze(1).broadcast_to([P, 4, P])
                    eye = ident.unsqueeze(1).broadcast_to([P, 4, P])
                    dve.wait_ge(gd_de, 2 * one)
                    for par in range(2):
                        dve.wait_ge(gd_kk, 4 * tt + par + 1)
                        dve.tensor_tensor(units(gd_mt, par), bank4(1 + par), units(gd_dt, par), ALU.mult).then_inc(gd_m, 1)
                    for par in range(2):
                        dve.wait_ge(gd_m, 2 * tt + par + 1)
                        step(dve.tensor_tensor(units(gd_invt, par), units(gd_mt, par), level1, ALU.mult))
                        dve.tensor_tensor(units(gd_invt, par), eye, units(gd_invt, par), ALU.subtract).then_inc(gd_x1, 1)
                    for par in range(2):
                        dve.wait_ge(gd_kk, 4 * tt + par + 3)
                        dve.tensor_tensor(units(gd_at, par), bank4(3 + par), units(gd_dt, par), ALU.mult).then_inc(gd_a, 1)
                    for level in range(2, 7):
                        for par in range(2):
                            n = 10 * tt + 2 * (level - 2) + par
                            dve.wait_ge(gd_qp, n + 1)
                            if level < 6:
                                dve.tensor_tensor(units(gd_inv, par), units(gd_inv, par), bank4(2 + par), ALU.subtract)
                            dve.tensor_tensor(units(gd_invt, par), units(gd_invt, par), bank4(4 + par),
                                              ALU.subtract).then_inc(gd_iv, 1)
                    dve.wait_ge(gd_up, 2 * one)
                    dve.tensor_copy(gd_wt[:, :, :].rearrange("p f t -> p (f t)"), ps[:, 1, :]).then_inc(gd_ws, 1)
                    dve.wait_ge(gd_us, one)
                    for c in range(2):
                        n = 2 * tt + c
                        rows = slice(64 * c, 64 * c + 64)
                        dve.wait_ge(gd_sp, 2 * n + 1)
                        if n == 0:
                            dve.wait_ge(gd_z0, 2)
                        dve.tensor_tensor(gd_vn[rows, :], gd_u[rows, :], ps[rows, 2, :], ALU.subtract).then_inc(gd_vs, 1)
                        dve.wait_ge(gd_sp, 2 * n + 2)
                        step(dve.tensor_tensor(gd_s[:, :, :], gd_s[:, :, :],
                                               gd_dec[:, c, tt, :].unsqueeze(2).broadcast_to([P, 4, P]), ALU.mult))
                        dve.wait_ge(gd_dp, n + 1)
                        for par in range(2):
                            r, cols = slice(64 * par, 64 * par + 64), slice(64 * par, 64 * par + 64)
                            done = dve.tensor_tensor(gd_s[r, :, cols], gd_s[r, :, cols], bank4(4)[r, :, cols], ALU.add)
                        done.then_inc(gd_st, 1)
                    dve.wait_ge(gd_op, one)
                    dve.wait_ge(gd_os, 2 * one)
                    dve.tensor_tensor(gd_o[:, :], gd_o[:, :], ps[:, 5, :], ALU.add).then_inc(gd_of, 1)
                    dve.wait_ge(gd_oq, one)
                    dve.tensor_reduce(gd_rs[:, 0, 0, :], each_head(gd_osq[:, :]), AXX, ALU.add).then_inc(gd_or, 1)
                    dve.wait_ge(gd_on, one)
                    step(dve.tensor_tensor(each_head(gd_o[:, :]), each_head(gd_o[:, :]), of_heads(gd_rs[:, 2, 0, :]), ALU.mult))
                    dve.wait_ge(gd_zn, 2)
                    dve.tensor_tensor(gd_o[:, :], gd_o[:, :], gd_z[:, tt, :], ALU.mult).then_inc(y_tm, 1)
                    store_y("mix0", tt, tiles=4)
                out_product(out)

            def sparse_attention():
                q, out = prod["od_in"], prod["od_out"]

                def compression_input():
                    dve.wait_ge(ns_split, 1)
                    dve.tensor_tensor(ns_wg_lo[:, :], ns_wg[:, :], ns_wg_hi[:, :].bitcast(F32),
                                      ALU.subtract).then_inc(ns_split, 1)
                    for kv in range(2):
                        dve.memset(ns_xp[:, kv, :, :, :].rearrange("p h u (g n) -> p (h u g) n", n=16)[:, :, 15:16],
                                   0.0).then_inc(ns_x, 1)
                        dve.wait_ge(ns_cvt, kv + 1)
                        src = two[4 + 2 * kv].rearrange("p b n -> p (b n)").rearrange("p (g t) -> p g t", t=T)
                        for half in range(2):
                            for par in range(2):
                                rows = slice(64 * par, 64 * par + 64)
                                taps = src[rows, :, 16 * half + par:16 * half + par + 239:2]
                                taps = taps.rearrange("p g (n u) -> p g n u", u=8)
                                pos = ns_pos[rows, half, :].unsqueeze(1).unsqueeze(1).broadcast_to([64, 4, 15, 8])
                                dst = ns_xp[rows, kv, half, :, :].rearrange("p u (g n) -> p g n u", n=16)[:, :, 0:15, :]
                                dve.tensor_tensor(dst, taps, pos, ALU.add).then_inc(ns_x, 1)

                def store_hidden():
                    dve.wait_ge(ns_htp, 1)
                    dve.tensor_copy(ns_ht[:, :, :, :].rearrange("p k c n -> p (k c n)"), ps[:, 6, 0:256]).then_inc(ns_hts, 1)

                def store_compressed():
                    dve.wait_ge(ns_kvp, 1)
                    dve.tensor_copy(ns_kct[:, :], ps[:, 6, 0:64]).then_inc(ns_kvs, 1)
                    a = CONST_AT["group"][0]
                    for g in range(4):
                        done = dve.tensor_scalar(ns_vc[:, g, :], ps[0:64, 7, 0:64], const[0:64, a + g:a + g + 1], None, ALU.mult)
                    done.then_inc(ns_kvs, 2)
                    dve.wait_ge(ns_qtp, 4)
                    heads = ns_tm[:, :, NS_COL["q"]:NS_COL["q"] + D].rearrange("p t (h d) -> p t h d", d=64)
                    x1, x2 = heads[:, :, :, 0:8], heads[:, :, :, 8:16]
                    cos, sin = [cst(n).rearrange("p (t f) -> p t f", f=8).unsqueeze(2).broadcast_to([P, TT, 16, 8])
                                for n in ("cos", "sin")]
                    for n, (a, b) in enumerate([(x1, cos), (x2, sin), (x2, cos), (x1, sin)]):
                        for tt in range(TT):
                            done = dve.tensor_tensor(ns_rot[:, n, tt], a[:, tt], b[:, tt], ALU.mult)
                        done.then_inc(ns_rope, 1)
                    dve.wait_ge(ns_rope, 4)
                    for tt in range(TT):
                        dve.tensor_tensor(x1[:, tt], ns_rot[:, 0, tt], ns_rot[:, 1, tt], ALU.subtract)
                        done = dve.tensor_tensor(x2[:, tt], ns_rot[:, 2, tt], ns_rot[:, 3, tt], ALU.add)
                        done.then_inc(ns_rope, 1)

                in_product("mix1", q, out, {1: compression_input, 3: store_hidden, 4: store_compressed})
                n = len(ns_units)

                def maxima(u):
                    tt, br, g = ns_units[u]
                    keys = (tt + 1) * P
                    wide = cst("causal_wide")[:, 2 * P - keys:2 * P]
                    st = 4 * (u % 2)
                    dve.wait_ge(ns_s, u + 1)
                    if u >= 2:
                        dve.wait_ge(ns_tp, u - 1)
                    for j in range(4):
                        dve.tensor_tensor_reduce(out=ns_p[:, u % 2, j, 0:keys],
                                                 in0=ps[:, 2 * (u % 2) + j % 2, j // 2 * keys:(j // 2 + 1) * keys],
                                                 in1=wide, scale=1.0, scalar=-3.0e38, op0=ALU.add, op1=ALU.max,
                                                 accum_out=ns_st[:, st, j:j + 1]).then_inc(ns_m, 1)
                    dve.wait_ge(ns_m, 4 * u + 4)
                    dve.tensor_scalar(ns_st[:, st + 1, 0:4], ns_st[:, st, 0:4], -0.125, None, ALU.mult).then_inc(ns_nm, 1)

                def weigh(u):
                    tt, br, g = ns_units[u]
                    keys = (tt + 1) * P
                    st = 4 * (u % 2)
                    dve.wait_ge(ns_e, 4 * u + 4)
                    dve.reciprocal(ns_st[:, st + 3, 0:4], ns_st[:, st + 2, 0:4]).then_inc(ns_d, 1)
                    dve.wait_ge(ns_d, 2 * u + 1)
                    dve.tensor_tensor(ns_st[:, st + 3, 4:8], ns_st[:, st + 3, 0:4],
                                      ns_gate[:, tt, 12 * g + 1 + br:12 * g + 11 + br:3], ALU.mult).then_inc(ns_d, 1)
                    dve.wait_ge(ns_d, 2 * u + 2)
                    for j in range(4):
                        done = dve.tensor_scalar(ns_p[:, u % 2, j, 0:keys], ns_p[:, u % 2, j, 0:keys],
                                                 ns_st[:, st + 3, 4 + j:5 + j], None, ALU.mult)
                    done.then_inc(ns_w, 1)

                for tt in range(TT):
                    first = tt * n // TT
                    c0 = 9 * tt
                    c = ns_c[:, :].rearrange("p (h n) -> p h n", n=16)
                    dve.wait_ge(ns_cs, tt + 1)
                    if tt:
                        dve.wait_ge(ns_ctp, tt)
                    add = cst("cmp_add")[:, 16 * tt:16 * tt + 16]
                    for par in range(2):
                        src = ps[:, 4 + par, 0:P].rearrange("p (g j n) -> p g j n", g=4, j=2)
                        dst = ns_c[:, :].rearrange("p (j r g n) -> p r g j n", j=2, r=2, g=4)[:, par]
                        dve.tensor_tensor(dst, src, add.unsqueeze(1).unsqueeze(1).broadcast_to([P, 4, 2, 16]),
                                          ALU.add).then_inc(ns_cd, 1)
                    dve.wait_ge(ns_cd, c0 + 2)
                    dve.tensor_reduce(ns_cst[:, 0, :], c, AXX, ALU.max).then_inc(ns_cd, 1)
                    dve.wait_ge(ns_cd, c0 + 3)
                    dve.tensor_tensor(c, c, ns_cst[:, 0, :].unsqueeze(2).broadcast_to([P, 16, 16]),
                                      ALU.subtract).then_inc(ns_cd, 1)
                    maxima(first)
                    dve.wait_ge(ns_ce, tt + 1)
                    dve.tensor_tensor(c, c, cst("cmp_mul")[:, 16 * tt:16 * tt + 16].unsqueeze(1).broadcast_to([P, 16, 16]),
                                      ALU.mult).then_inc(ns_cd, 1)
                    dve.wait_ge(ns_cd, c0 + 5)
                    dve.tensor_reduce(ns_cst[:, 1, :], c, AXX, ALU.add).then_inc(ns_cd, 1)
                    dve.wait_ge(ns_cd, c0 + 6)
                    dve.tensor_scalar(ns_cst[:, 1, :], ns_cst[:, 1, :], 1.0, None, ALU.max).then_inc(ns_cd, 1)
                    dve.wait_ge(ns_cd, c0 + 7)
                    dve.reciprocal(ns_cst[:, 2, :], ns_cst[:, 1, :]).then_inc(ns_cd, 1)
                    dve.wait_ge(ns_gs, 1)
                    dve.wait_ge(ns_cd, c0 + 8)
                    gate = ns_gate[:, tt, :].rearrange("p (g j b) -> p j g b", g=4, j=4)[:, :, :, 0]
                    dve.tensor_tensor(ns_cst[:, 3, :].rearrange("p (j g) -> p j g", g=4),
                                      ns_cst[:, 2, :].rearrange("p (j g) -> p j g", g=4), gate, ALU.mult).then_inc(ns_cg, 1)
                    dve.wait_ge(ns_cg, tt + 1)
                    dve.tensor_tensor(c, c, ns_cst[:, 3, :].unsqueeze(2).broadcast_to([P, 16, 16]),
                                      ALU.mult).then_inc(ns_cd, 1)
                    for u in range(first, first + n // TT):
                        if u + 1 < first + n // TT:
                            maxima(u + 1)
                        weigh(u)
                for tt in range(TT):
                    store_y("mix1", tt)
                out_product(out)

            for layer in layers:
                if layer == "sgu":
                    spatial_gating()
                elif layer == "mix0":
                    delta_rule()
                elif layer == "mix1":
                    sparse_attention()
                elif layer == "kv":
                    in_product("kv", prod["kv"], None)
                elif layer == "sb":
                    stick_breaking()
                elif layer[:3] == "mlp":
                    hidden_layer(layer, 4, 1.0)
                elif layer[:3] == "ffn":
                    hidden_layer(layer, 2, 0.5)
                elif layer[:3] == "fin":
                    final_norm(layer)
            residual()

        @block.gpsimd
        def _(pool):
            pool.wait_ge(params_loaded, 32)

            def inverse_rms(layer):
                r0 = at[layer][2]
                pool.wait_ge(ss_ready, TT * (r0 + 1))
                pool.tensor_scalar(ms[:, :], ss[:, :], 1.0 / D, EPS, ALU.mult, ALU.add).then_inc(ms_ready, 1)
                pool.wait_ge(ms_ready, r0 + 1)
                pool.tensor_tensor(rstd[:, :], ms[:, :], cst("neg_half")[:, 0:TT], ALU.pow).then_inc(rstd_ready, 1)

            def spatial_gating():
                pool.wait_ge(x_ready, at["sgu"][1])
                pool.dma_start(ws_raw[:, :, :], dram["ws_t"]).then_inc(sgu_params, 16)
                pool.dma_start(bs_t[:, :], dram["bs_t"]).then_inc(sgu_params, 16)
                for k in range(2):
                    pool.dma_start(ln_rows[:, k, :], dram["ln_rows"][k:k + 1, :].partition_broadcast(P)).then_inc(sgu_params, 16)
                pool.wait_ge(sgu_params, 64)
                pool.tensor_tensor(ws_t[:, :, :], ws_raw[:, :, :], cst("upto").unsqueeze(1).broadcast_to([P, 8, P]),
                                   ALU.mult).then_inc(sgu_ws, 1)
                pool.wait_ge(sgu_sq, 4)
                pool.tensor_tensor(v_stat[:, 2, :], v_sq[:, :, 0], v_sq[:, :, 1], ALU.add).then_inc(sgu_rs, 1)
                pool.wait_ge(sgu_rs, 1)
                pool.tensor_scalar(v_stat[:, 1, :], v_stat[:, 2, :], 1.0 / (2 * D), LN_EPS, ALU.mult,
                                   ALU.add).then_inc(sgu_rs, 1)
                pool.wait_ge(sgu_rs, 2)
                pool.tensor_tensor(v_stat[:, 2, :], v_stat[:, 1, :], cst("neg_half")[:, 0:TT], ALU.pow).then_inc(sgu_rs, 1)

            taken = [0]

            def step(ins):
                taken[0] += 1
                ins.then_inc(pool_step, 1)
                pool.wait_ge(pool_step, taken[0])

            def delta_rule():
                for dst, name in ((gd_wab[:, :], "gd_wab"), (gd_cw[:, :, :], "gd_cw"), (gd_scw[:, :, :], "gd_scw")):
                    pool.dma_start(dst, dram[name]).then_inc(gd_params, 16)
                for dst, name in ((gd_dt_bias, "gd_dt_bias"), (gd_a_log, "gd_a_log"), (gd_onorm, "gd_onorm")):
                    pool.dma_start(dst[:, :], dram[name].partition_broadcast(P)).then_inc(gd_params, 16)
                pool.memset(gd_x[:, :, 0:3], 0.0).then_inc(gd_pad, 1)
                pool.memset(gd_ch[:, :, 0:2], 0.0).then_inc(gd_pad, 1)
                inverse_rms("mix0")
                pool.wait_ge(gd_params, 16 * 6)
                pool.wait_ge(gd_in, TT * 7)
                for tt in range(TT):
                    z = gd_z[:, tt, :].rearrange("p (h d) -> p h d", d=64)
                    pool.tensor_tensor(z, z, gd_onorm[:, :].unsqueeze(1).broadcast_to([P, 8, 64]), ALU.mult).then_inc(gd_zn, 1)
                pool.wait_ge(gd_cv, 3)
                pool.memset(gd_s[:, :, :], 0.0).then_inc(gd_z0, 1)
                pool.memset(gd_vn[:, :], 0.0).then_inc(gd_z0, 1)
                for tt in range(TT):
                    one = 1 + tt
                    pool.wait_ge(gd_gg, 1)
                    if tt:
                        pool.wait_ge(gd_qp, 10 * tt)
                    pool.tensor_copy(gd_gb[:, :, :], gd_g[:, 5, tt, :].unsqueeze(2).broadcast_to([P, 8, P])).then_inc(gd_gbr, 1)
                    pool.wait_ge(gd_qs, one)
                    step(pool.tensor_scalar(gd_rs[:, 1, :, :], gd_rs[:, 0, :, :], 1.0, EPS, ALU.mult, ALU.add))
                    half = cst("neg_half").rearrange("p (n h) -> p n h", h=8)
                    pool.tensor_tensor(gd_rs[:, 2, :, :], gd_rs[:, 1, :, :], half, ALU.pow).then_inc(gd_qr, 1)
                    pool.wait_ge(gd_kn, 5 * tt + 1)
                    pool.wait_ge(gd_gt, 1)
                    k = gd_tm[:, 0, :].rearrange("p (h d) -> p h d", d=64)
                    for n, f in ((5, gd_g[:, 7, tt, :]), (6, gd_ez[:, 0, tt, :]), (7, gd_ez[:, 1, tt, :])):
                        pool.tensor_tensor(gd_tm[:, n, :].rearrange("p (h d) -> p h d", d=64), k,
                                           f.unsqueeze(2).broadcast_to([P, 8, 64]), ALU.mult).then_inc(gd_kz, 1)
                    pool.wait_ge(gd_m, 2 * one)
                    for level in range(2, 7):
                        if level >= 4:
                            pool.wait_ge(gd_pp, 10 * tt + 2 * (level - 3))
                        pool.tensor_tensor(gd_ml[:, level % 2, :, :], gd_mt[:, :, :],
                                           cst(f"level{level}").unsqueeze(1).broadcast_to([P, 8, P]),
                                           ALU.mult).then_inc(gd_mlr, 1)
                    pool.wait_ge(gd_or, one)
                    step(pool.tensor_scalar(gd_rs[:, 1, 0, :], gd_rs[:, 0, 0, :], 1.0 / 64, EPS, ALU.mult, ALU.add))
                    pool.tensor_tensor(gd_rs[:, 2, 0, :], gd_rs[:, 1, 0, :], cst("neg_half")[:, 0:8],
                                       ALU.pow).then_inc(gd_on, 1)

            def sparse_attention():
                if at["mix1"][1]:
                    pool.wait_ge(x_ready, at["mix1"][1])
                for dst, name in ((ns_w1[:, :, :, :], "ns_w1"), (ns_w2k[:, :, :], "ns_w2k"), (ns_w2v[:, :, :], "ns_w2v"),
                                  (ns_wg[:, :], "ns_wg"), (ns_pos[:, :, :], "ns_pos")):
                    pool.dma_start(dst, dram[name]).then_inc(ns_params, 16)
                inverse_rms("mix1")
                pool.wait_ge(ns_in, TT * 5)
                cos, sin = [cst(n).rearrange("p (t f) -> p t f", f=8).unsqueeze(2).broadcast_to([P, TT, 4, 8])
                            for n in ("cos", "sin")]
                for k, col in enumerate((NS_COL["ks"], NS_COL["kw"])):
                    heads = ns_tm[:, :, col:col + 256].rearrange("p t (h d) -> p t h d", d=64)
                    x1, x2 = heads[:, :, :, 0:8], heads[:, :, :, 8:16]
                    if k:
                        pool.wait_ge(ns_krope, 12)
                    for n, (a, b) in enumerate([(x1, cos), (x2, sin), (x2, cos), (x1, sin)]):
                        for tt in range(TT):
                            pool.tensor_tensor(ns_krot[:, n, tt], a[:, tt], b[:, tt], ALU.mult).then_inc(ns_krope, 1)
                    pool.wait_ge(ns_krope, 12 * k + 8)
                    for tt in range(TT):
                        pool.tensor_tensor(x1[:, tt], ns_krot[:, 0, tt], ns_krot[:, 1, tt], ALU.subtract).then_inc(ns_krope, 1)
                        pool.tensor_tensor(x2[:, tt], ns_krot[:, 2, tt], ns_krot[:, 3, tt], ALU.add).then_inc(ns_krope, 1)

            for layer in layers:
                if layer == "mix0":
                    delta_rule()
                    continue
                if layer == "mix1":
                    sparse_attention()
                    continue
                inverse_rms(layer)
                if layer == "sgu":
                    spatial_gating()
                if layer == "fin1":
                    pool.wait_ge(x_ready, at[layer][1] + TT)
                    if "fin2" in layers:
                        pool.dma_start(row[:, :], dram["fin_rows"][1:2, :].partition_broadcast(P)).then_inc(row2_loaded, 16)


def lay_out(a, layers=LAYERS):
    import numpy as np

    def panels(w, gated=False):
        w = np.asarray(w)
        k, n = w.shape
        if gated:
            w = w.reshape(k, 2, n // 512, 256).transpose(0, 2, 1, 3).reshape(k, n)
        kt, blocks = k // P, n // NB
        per = -(-kt // PK)
        out = np.zeros((blocks, per * PK, P, NB), np.float32)
        out[:, :kt] = w.reshape(kt, P, blocks, NB).transpose(2, 0, 1, 3)
        return out.reshape(blocks, per, PK, P, NB).transpose(0, 1, 3, 2, 4).reshape(blocks * per, P, PANEL)

    prod, _ = lay_out_products(layers)
    ev = np.asarray(a["ev_w_in"])[0]
    od = np.asarray(a["od_w_in"])[0]
    od_main = np.concatenate([od[:, 1024:1536], od[:, 0:1024], od[:, 1536:2560]], 1)
    ev_main = np.concatenate([ev[:, 0:1536], ev[:, 2576:3088], ev[:, 3088:3600], ev[:, 2064:2576], ev[:, 1536:2048]], 1)
    sgu = np.asarray(a["a_w_in_2"])[0]
    weights = {
        "ev_in": ev_main, "ev_out": a["ev_w_out"][0],
        "mlp0_up": a["w_up"][0], "mlp0_down": a["w_down"][0],
        "od_in": od_main, "od_out": a["od_w_out"][0],
        "mlp1_up": a["w_up"][1], "mlp1_down": a["w_down"][1],
        "sgu_in": np.concatenate([sgu[:, 2048:], sgu[:, :2048]], 1), "sgu_out": a["a_w_out_2"][0],
        "kv": a["w_kv_2"], "sb_q": a["b_w_q_2"][0], "sb_out": a["b_w_o_2"][0],
    }
    for i in range(2):
        for j in range(2):
            weights[f"ffn{i}{j}_up"] = a["ffn_w_in_2"][i][j]
            weights[f"ffn{i}{j}_down"] = a["ffn_w_out_2"][i][j]
    stream = np.concatenate([panels(weights[n], n.startswith("ffn") and n.endswith("up")) for n in prod])
    norms = {
        "mix0": a["mix_norm"][0], "mlp0": a["mlp_norm"][0], "mix1": a["mix_norm"][1], "mlp1": a["mlp_norm"][1],
        "ffn00": a["ffn_norm_2"][0][0], "ffn01": a["ffn_norm_2"][0][1], "ffn10": a["ffn_norm_2"][1][0],
        "ffn11": a["ffn_norm_2"][1][1], "sgu": a["mix_norm_2"][0], "sb": a["mix_norm_2"][1], "kv": a["kv_norm_2"],
    }
    norm_t = np.stack([np.asarray(norms[n]).reshape(DK, P).T for n in NORMS], 1)
    x = np.asarray(a["x"]).reshape(TT, P, D).transpose(1, 0, 2)
    out = {
        "x": x, "stream": stream, "norm_t": norm_t, "const": const_table()[0],
        "gd_wab": ev[:, 2048:2064].reshape(DK, P, 16).transpose(1, 0, 2).reshape(P, DK * 16),
        "gd_cw": np.asarray(a["ev_qkv_conv"])[0].reshape(4, 12, P).transpose(2, 1, 0),
        "gd_scw": np.asarray(a["ev_sc_conv"])[0].reshape(3, 4, P).transpose(2, 1, 0),
        "gd_dt_bias": np.asarray(a["ev_dt_bias"]), "gd_a_log": np.asarray(a["ev_a_log"]), "gd_onorm": np.asarray(a["ev_o_norm"]),
        "ns_w1": np.stack([np.asarray(a[n])[0].reshape(16, P, 256).transpose(1, 0, 2)
                           for n in ("od_cmp_k_w1", "od_cmp_v_w1")], 1),
        "ns_w2k": np.tile(np.asarray(a["od_cmp_k_w2"])[0].reshape(2, P, 64).transpose(1, 0, 2), (1, 1, 2)),
        "ns_w2v": np.asarray(a["od_cmp_v_w2"])[0].reshape(2, P, 64).transpose(1, 0, 2),
        "ns_wg": od[:, 2560:2608].reshape(DK, P, 48).transpose(1, 0, 2).reshape(P, DK * 48),
        "ns_pos": np.asarray(a["od_cmp_pos"])[0].reshape(2, 8, 2, 64).transpose(2, 3, 0, 1).reshape(P, 2, 8),
        "ws_t": np.asarray(a["a_w_s_2"])[0].transpose(2, 0, 1), "bs_t": np.asarray(a["a_b_s_2"])[0].T,
        "ln_rows": np.stack([np.asarray(a["a_ln_g_2"])[0], np.asarray(a["a_ln_b_2"])[0]]),
        "fin_rows": np.stack([np.asarray(a["final_norm"]), np.asarray(a["final_norm_2"])]),
    }
    return {k: np.ascontiguousarray(v) for k, v in out.items()}


def kernel(**inputs):
    import numpy as np
    import concourse.bacc as bacc
    from concourse.bass_utils import run_bass_kernel_spmd

    nc = bacc.Bacc("TRN2", target_bir_lowering=False, num_devices=1)
    arrays = lay_out({k: np.asarray(v) for k, v in inputs.items()})
    dram = {k: nc.dram_tensor(f"in_{k}", v.shape, F32, kind="ExternalInput").ap() for k, v in arrays.items()}
    dram["out"] = nc.dram_tensor("out", (P, TT, D), F32, kind="ExternalOutput").ap()
    build(nc, dram)
    r = run_bass_kernel_spmd(nc, [{f"in_{k}": v for k, v in arrays.items()}], core_ids=[0])
    return np.asarray(r.results[0]["out"]).transpose(1, 0, 2).reshape(1, T, D)
```

```python
from contextlib import ExitStack

import concourse.bass as bass
from concourse import mybir

F32 = mybir.dt.float32
F32R = mybir.dt.float32r
ACT = mybir.ActivationFunctionType
ALU = mybir.AluOpType
AXX = mybir.AxisListType.X

P = 128
T = 256
TT = T // P
D = 1024
DK = D // P
NB = 512
PK = 4
PANEL = PK * NB
RING = 4
FF = 4 * D
FF2 = 2816
EPS = 1e-6
LN_EPS = 1e-5
KB = 1024
BIG = 1.0e30

PRODUCTS = [
    ("ev_in", DK, 7), ("ev_out", DK, 2),
    ("mlp0_up", DK, FF // NB), ("mlp0_down", FF // P, 2),
    ("od_in", DK, 5), ("od_out", DK, 2),
    ("mlp1_up", DK, FF // NB), ("mlp1_down", FF // P, 2),
    ("ffn00_up", DK, FF2 // 256), ("ffn00_down", FF2 // P, 2),
    ("sgu_in", DK, 8), ("sgu_out", 2 * DK, 2),
    ("ffn01_up", DK, FF2 // 256), ("ffn01_down", FF2 // P, 2),
    ("kv", DK, 1),
    ("ffn10_up", DK, FF2 // 256), ("ffn10_down", FF2 // P, 2),
    ("sb_q", DK, 2), ("sb_out", DK, 2),
    ("ffn11_up", DK, FF2 // 256), ("ffn11_down", FF2 // P, 2),
]
NORMS = ["mix0", "mlp0", "mix1", "mlp1", "ffn00", "ffn01", "ffn10", "ffn11", "sgu", "sb", "kv"]

LAYERS = ["mix0", "mlp0", "mix1", "mlp1", "fin1", "ffn00", "sgu", "ffn01", "kv", "ffn10", "sb", "ffn11", "fin2"]


class Product:

    def __init__(self, name, kt, blocks, panel, block):
        self.name, self.kt, self.blocks = name, kt, blocks
        self.per = -(-kt // PK)
        self.panel, self.block = panel, block


def lay_out_products(layers):
    owner = {"ev": "mix0", "od": "mix1"}
    out, panel, block = {}, 0, 0
    for name, kt, blocks in PRODUCTS:
        head = name.split("_")[0]
        if owner.get(head, head) not in layers:
            continue
        out[name] = Product(name, kt, blocks, panel, block)
        panel += out[name].per * blocks
        block += blocks
    return out, panel


def const_table():
    import numpy as np

    c, cols = {}, []

    def put(name, a):
        a = np.asarray(a, np.float32).reshape(P, -1)
        start = sum(x.shape[1] for x in cols)
        c[name] = (start, start + a.shape[1])
        cols.append(a)

    p = np.arange(P)[:, None]
    f = np.arange(P)[None, :]
    put("ident", p == f)
    put("neg_half", np.full((P, 16), -0.5))
    same = p // 64 == f // 64
    put("cum", same & (p <= f))
    put("chunk", same)
    put("even", np.broadcast_to(p < 64, (P, P)))
    put("odd", np.broadcast_to(p >= 64, (P, P)))
    put("not_later", np.where(same & (p <= f), 0, -BIG))
    for level in range(1, 7):
        half = 1 << (level - 1)
        put(f"level{level}", (p // (2 * half) == f // (2 * half)) & (p // half % 2 == 0) & (f // half % 2 == 1))
    put("causal_wide", np.concatenate([np.zeros((P, P)), np.where(f <= p, 0, -BIG)], 1))
    put("group", p // 16 == np.arange(4)[None, :])
    tok = p[:, :, None] + P * np.arange(TT)[None, :, None]
    ends = np.arange(16)[None, None, :] * 16 + 31
    seen = (ends <= tok) & (np.arange(16)[None, None, :] < 15)
    put("cmp_add", np.where(seen, 0, -BIG))
    put("cmp_mul", seen)
    inv = np.float32(500000.0) ** (-np.arange(0, 16, 2, dtype=np.float32) / np.float32(16))
    ang = tok.astype(np.float32) * inv.astype(np.float32)[None, None, :]
    put("cos", np.cos(ang, dtype=np.float32))
    put("sin", np.sin(ang, dtype=np.float32))
    put("earlier", p < f)
    put("not_earlier", np.where(p < f, 0, -BIG))
    put("suffix", p >= f)
    put("ones", np.ones((P, P)))
    put("upto", p <= f)
    return np.concatenate(cols, axis=1), c


CONST_AT = const_table()[1]
CONST_WIDTH = max(b for _, b in CONST_AT.values())
CONST_FIRST = CONST_AT["neg_half"][1]


def build(nc, dram, layers=LAYERS):
    prod, panels = lay_out_products(layers)

    at, t, x, r = {}, 0, 0, 0
    hidden_batches = {"mlp": FF // NB, "ffn": FF2 // 256}
    for layer in layers:
        at[layer] = (t, x, r)
        kind = layer[:3]
        if layer == "kv":
            t, r = t + 2, r + 1
        elif layer in ("fin1", "fin2"):
            x, r = x + 2, r + 1
        elif kind in hidden_batches:
            t, x, r = t + 2 + hidden_batches[kind], x + 4, r + 1
        else:
            t, x, r = t + 2 + {"sgu": 4}.get(layer, 0), x + 4, r + 1
    hidden_before, count = {}, 0
    for layer in layers:
        hidden_before[layer] = count
        count += hidden_batches.get(layer[:3], 0)
    following = dict(zip(layers, layers[1:]))

    def early_norm(layer):
        nxt = following.get(layer)
        return nxt if layer[:3] != "fin" and nxt in NORMS else None

    early = {early_norm(a) for a in layers}

    def after_final(layer):
        return any(a[:3] == "fin" and following.get(a) == layer for a in layers)

    with ExitStack() as ctx:
        def sb(name, shape, dt=F32):
            return ctx.enter_context(nc.sbuf_tensor(name, shape, dt))

        def sem(name):
            return ctx.enter_context(nc.semaphore(name))

        raw = sb("raw", [P, RING, PANEL])
        w_hi = sb("w_hi", [P, 2, PANEL], F32R)
        w_lo = sb("w_lo", [P, 2, PANEL], F32R)
        x_sb = sb("x_sb", [P, TT, D])
        h_hi = sb("h_hi", [P, DK, T], F32R)
        h_lo = sb("h_lo", [P, DK, T], F32R)
        tm = sb("tm", [P, TT, NB])
        row = sb("row", [P, D])
        junk = sb("junk", [P, D], mybir.dt.bfloat16)
        const = sb("const", [P, CONST_WIDTH])
        norm_t = sb("norm_t", [P, len(NORMS), DK])
        ss = sb("ss", [P, TT])
        ms = sb("ms", [P, TT])
        rstd = sb("rstd", [P, TT])
        arena_bytes = 2 * (FF // P) * T * 4 + 34 * KB
        arena = sb("arena", [P, arena_bytes // 4])
        arena_at = nc.lookup_mloc(arena).addr

        def view(name, shape, at_byte, dt=F32):
            return nc.alloc_sbuf_tensor_at(name, shape, dt, offset=arena_at + at_byte)

        hid_hi = view("hid_hi", [P, FF // P, T], 0, F32R)
        hid_lo = view("hid_lo", [P, FF // P, T], (FF // P) * T * 4, F32R)
        hid_hi2 = hid_hi[:].rearrange("p k t -> p (k t)")
        hid_lo2 = hid_lo[:].rearrange("p k t -> p (k t)")

        sgu_z = view("sgu_z", [P, TT, 4 * D], 16 * KB)
        sgu_lo = hid_lo[:, 2 * DK:, :]
        ln_rows = view("ln_rows", [P, 2, 2 * D], 64 * KB)
        ws_raw = view("ws_raw", [P, 8, P], 80 * KB)
        ws_t = view("ws_t", [P, 8, P], 84 * KB)
        bs_t = view("bs_t", [P, 8], 88 * KB)
        v_sums = view("v_sums", [P, TT, 4], 88 * KB + 64)
        v_sq = view("v_sq", [P, TT, 2], 88 * KB + 192)
        v_stat = view("v_stat", [P, 3, TT], 88 * KB + 128)
        gd_x = view("gd_x", [P, 12, 3 + T], 0)
        gd_ch = view("gd_ch", [P, 4, 2 + T], 13 * KB)
        gd_b = view("gd_b", [P, 4, T], 18 * KB)
        gd_z = view("gd_z", [P, TT, NB], 22 * KB)
        gd_c = view("gd_c", [P, 12, T], 26 * KB)
        gd_sc = view("gd_sc", [P, 4, T], 38 * KB)
        gd_wab = view("gd_wab", [P, 8 * 16], 42 * KB)
        gd_wab_hi = view("gd_wab_hi", [P, 8 * 16], 42 * KB + 512, F32R)
        gd_wab_lo = view("gd_wab_lo", [P, 8 * 16], 43 * KB, F32R)
        gd_tm = view("gd_tm", [P, 8, NB], 44 * KB)
        gd_t = view("gd_t", [P, 4, 4, P], 60 * KB)
        gd_dt = view("gd_dt", [P, 8, P], 68 * KB)
        gd_mt = view("gd_mt", [P, 8, P], 72 * KB)
        gd_ml = view("gd_ml", [P, 2, 8, P], 76 * KB)
        gd_inv = view("gd_inv", [P, 8, P], 84 * KB)
        gd_invt = view("gd_invt", [P, 8, P], 88 * KB)
        gd_p = view("gd_p", [P, 8, P], 92 * KB)
        gd_gb = view("gd_gb", [P, 8, P], 92 * KB)
        gd_sq = view("gd_sq", [P, 2, NB], 84 * KB)
        gd_at = view("gd_at", [P, 8, P], 0)
        gd_u = view("gd_u", [P, NB], 4 * KB)
        gd_wt = view("gd_wt", [P, 4, P], 6 * KB)
        gd_vn = view("gd_vn", [P, NB], 8 * KB)
        gd_s = view("gd_s", [P, 4, P], 10 * KB)
        gd_o = view("gd_o", [P, NB], 14 * KB)
        gd_osq = view("gd_osq", [P, NB], 16 * KB)
        par_at = 96 * KB
        gd_cw = view("gd_cw", [P, 12, 4], par_at)
        gd_scw = view("gd_scw", [P, 4, 3], par_at + 192)
        gd_dt_bias = view("gd_dt_bias", [P, 8], par_at + 256)
        gd_a_log = view("gd_a_log", [P, 8], par_at + 288)
        gd_onorm = view("gd_onorm", [P, 64], par_at + 320)
        gd_g = view("gd_g", [P, 8, TT, 8], par_at + 576)
        gd_sum = view("gd_sum", [P, 4, TT, 8], par_at + 1088)
        gd_exp = view("gd_exp", [P, 4, TT, 8], par_at + 1344)
        gd_dec = view("gd_dec", [P, 2, TT, 4], par_at + 1600)
        gd_ez = view("gd_ez", [P, 2, TT, 8], par_at + 1664)
        gd_rs = view("gd_rs", [P, 3, 2, 8], par_at + 1792)
        gd_ro = view("gd_ro", [P, 2, 8], par_at + 1984)

        ns_tm = view("ns_tm", [P, TT, 5 * NB], 0)
        ns_w1 = view("ns_w1", [P, 2, 16, 256], 20 * KB)
        ns_qt = view("ns_qt", [P, 8, T], 52 * KB)
        ns_qrt = view("ns_qrt", [P, 8, T], 60 * KB)
        ns_kt = view("ns_kt", [P, 2, 2, 4, T], 68 * KB)
        ns_xp = view("ns_xp", [P, 2, 2, 8, 64], 76 * KB)
        ns_w2k = view("ns_w2k", [P, 2, P], 84 * KB)
        ns_w2v = view("ns_w2v", [P, 2, 64], 85 * KB)
        ns_ht = view("ns_ht", [P, 2, 2, 64], 88 * KB)
        ns_kct = view("ns_kct", [P, 4, 2, 16], 87 * KB)
        ns_vc = view("ns_vc", [64, 4, 64], 89 * KB + 256)
        ns_wg = view("ns_wg", [P, 8 * 48], 91 * KB)
        ns_wg_hi = view("ns_wg_hi", [P, 8 * 48], 92 * KB + 512, F32R)
        ns_wg_lo = view("ns_wg_lo", [P, 8 * 48], 94 * KB, F32R)
        ns_gate = view("ns_gate", [P, TT, 48], 95 * KB + 512)
        ns_pos = view("ns_pos", [P, 2, 8], 90 * KB + 256)
        ns_p = view("ns_p", [P, 3, 4, T], 20 * KB)
        ns_pt = view("ns_pt", [P, 2, 8, P], 32 * KB)
        ns_kd = view("ns_kd", [P, 2, TT, 4, 2, 64], 40 * KB)
        ns_c = view("ns_c", [P, TT, 256], 48 * KB)
        ns_krot = view("ns_krot", [P, 4, TT, 4, 8], 50 * KB)
        ns_rot = view("ns_rot", [P, 4, TT, 16, 8], 32 * KB)
        ns_cpt = view("ns_cpt", [64, TT, 4, P], 52 * KB)
        ns_st = view("ns_st", [P, 3, 4, 8], 86 * KB)
        ns_cst = view("ns_cst", [P, 4, TT * 16], 51 * KB)
        ns_kcv = view("ns_kcv", [P, TT, 8, 2, 64], 60 * KB)
        kv_tm = view("kv_tm", [P, TT, NB], 92 * KB)
        sb_q = view("sb_q", [P, TT, D], 0)
        sb_qt = view("sb_qt", [P, 8, T], 8 * KB)
        sb_kt = view("sb_kt", [P, 2, 4, T], 16 * KB)
        sb_s = view("sb_s", [P, 8, 2, 2, 256], 40 * KB)
        sb_kd = view("sb_kd", [P, TT, 4, 2, 64], 76 * KB)

        ps = ctx.enter_context(nc.psum_tensor("ps", [P, 8, NB], F32))
        acc = [[ps[:, 2 * b + t, :] for t in range(TT)] for b in range(2)]
        tps = ps[:, 4:6, :].rearrange("p b n -> p (b n)").rearrange("p (f t) -> p f t", t=T)

        def cst(name):
            a, b = CONST_AT[name]
            return const[:, a:b]

        ident = cst("ident")
        two = {b: ps[:, b:b + 2, :] for b in range(0, 8, 2)}

        raw_full = [sem(f"raw_full{i}") for i in range(RING)]
        hi_ready = sem("hi_ready")
        lo_ready = sem("lo_ready")
        w_used = sem("w_used")
        act_tm = sem("act_tm")
        tm_ready = sem("tm_ready")
        tps_ready = sem("tps_ready")
        t_hi = sem("t_hi")
        norm_hi = sem("norm_hi")
        t_lo = sem("t_lo")
        x_ready = sem("x_ready")
        ss_ready = sem("ss_ready")
        ms_ready = sem("ms_ready")
        rstd_ready = sem("rstd_ready")
        x_loaded = sem("x_loaded")
        x2_loaded = sem("x2_loaded")
        params_loaded = sem("params_loaded")
        const_loaded = sem("const_loaded")
        out_stored = sem("out_stored")
        row_loaded = sem("row_loaded")
        row2_loaded = sem("row2_loaded")
        y_tps = sem("y_tps")
        y_hi = sem("y_hi")
        y_lo = sem("y_lo")
        y_tm = sem("y_tm")
        sgu_params = sem("sgu_params")
        sgu_in = sem("sgu_in")
        sgu_mean = sem("sgu_mean")
        sgu_sq = sem("sgu_sq")
        sgu_rs = sem("sgu_rs")
        sgu_v = sem("sgu_v")
        sgu_ws = sem("sgu_ws")
        sgu_mix = sem("sgu_mix")
        sgu_s = sem("sgu_s")
        dve_step = sem("dve_step")
        pool_step = sem("pool_step")
        gd_params = sem("gd_params")
        gd_split = sem("gd_split")
        gd_in = sem("gd_in")
        gd_tp = sem("gd_tp")
        gd_ts = sem("gd_ts")
        gd_pad = sem("gd_pad")
        gd_cv = sem("gd_cv")
        gd_cs = sem("gd_cs")
        gd_abp = sem("gd_abp")
        gd_yb = sem("gd_yb")
        gd_ybh = sem("gd_ybh")
        gd_ybl = sem("gd_ybl")
        gd_ga = sem("gd_ga")
        gd_ge = sem("gd_ge")
        gd_gg = sem("gd_gg")
        gd_gp = sem("gd_gp")
        gd_gs = sem("gd_gs")
        gd_gx = sem("gd_gx")
        gd_gt = sem("gd_gt")
        gd_q = sem("gd_q")
        gd_qq = sem("gd_qq")
        gd_qs = sem("gd_qs")
        gd_qr = sem("gd_qr")
        gd_kn = sem("gd_kn")
        gd_kz = sem("gd_kz")
        gd_gbr = sem("gd_gbr")
        gd_bc = sem("gd_bc")
        gd_da = sem("gd_da")
        gd_de = sem("gd_de")
        gd_ft = sem("gd_ft")
        gd_fa = sem("gd_fa")
        gd_fv = sem("gd_fv")
        gd_kk = sem("gd_kk")
        gd_m = sem("gd_m")
        gd_a = sem("gd_a")
        gd_x1 = sem("gd_x1")
        gd_xp = sem("gd_xp")
        gd_xs = sem("gd_xs")
        gd_mlr = sem("gd_mlr")
        gd_pp = sem("gd_pp")
        gd_ps = sem("gd_ps")
        gd_qp = sem("gd_qp")
        gd_iv = sem("gd_iv")
        gd_up = sem("gd_up")
        gd_us = sem("gd_us")
        gd_ws = sem("gd_ws")
        gd_sp = sem("gd_sp")
        gd_vs = sem("gd_vs")
        gd_os = sem("gd_os")
        gd_dp = sem("gd_dp")
        gd_st = sem("gd_st")
        gd_op = sem("gd_op")
        gd_of = sem("gd_of")
        gd_oq = sem("gd_oq")
        gd_or = sem("gd_or")
        gd_on = sem("gd_on")
        gd_zn = sem("gd_zn")
        gd_z0 = sem("gd_z0")
        ns_params = sem("ns_params")
        ns_split = sem("ns_split")
        ns_in = sem("ns_in")
        ns_cvt = sem("ns_cvt")
        ns_x = sem("ns_x")
        ns_hp = sem("ns_hp")
        ns_hs = sem("ns_hs")
        ns_kvp = sem("ns_kvp")
        ns_kvs = sem("ns_kvs")
        ns_qtp = sem("ns_qtp")
        ns_qts = sem("ns_qts")
        ns_rope = sem("ns_rope")
        ns_krope = sem("ns_krope")
        ns_rtp = sem("ns_rtp")
        ns_kz = sem("ns_kz")
        ns_rts = sem("ns_rts")
        ns_gp = sem("ns_gp")
        ns_gs = sem("ns_gs")
        ns_cs = sem("ns_cs")
        ns_cd = sem("ns_cd")
        ns_cg = sem("ns_cg")
        ns_ce = sem("ns_ce")
        ns_ctp = sem("ns_ctp")
        ns_cts = sem("ns_cts")
        ns_s = sem("ns_s")
        ns_m = sem("ns_m")
        ns_nm = sem("ns_nm")
        ns_e = sem("ns_e")
        ns_d = sem("ns_d")
        ns_w = sem("ns_w")
        ns_tp = sem("ns_tp")
        ns_ts = sem("ns_ts")
        ns_pv = sem("ns_pv")
        kv_in = sem("kv_in")
        sb_copied = sem("sb_copied")
        sb_kz = sem("sb_kz")
        sb_in = sem("sb_in")
        sb_tp = sem("sb_tp")
        sb_ts = sem("sb_ts")
        sb_z = sem("sb_z")
        sb_zm = sem("sb_zm")
        sb_abs = sem("sb_abs")
        sb_ex = sem("sb_ex")
        sb_ln = sem("sb_ln")
        sb_sp = sem("sb_sp")
        sb_rev = sem("sb_rev")
        sb_arg = sem("sb_arg")
        sb_a = sem("sb_a")
        sb_av = sem("sb_av")

        read = {}
        for layer in layers:
            t0, x0, _ = at[layer]
            if layer[:3] in hidden_batches:
                h0 = hidden_before[layer]
                read[layer + "_up"] = (act_tm, 2 * h0, 2) if layer[:3] == "mlp" else (tm_ready, h0, 1)
                read[layer + "_down"] = (x_ready, x0, TT)
        if "sgu" in layers:
            read["sgu_in"], read["sgu_out"] = (sgu_in, 0, TT), (x_ready, at["sgu"][1], TT)
        if "mix0" in layers:
            read["ev_in"], read["ev_out"] = (gd_in, 0, TT), (x_ready, at["mix0"][1], TT)
        if "mix1" in layers:
            read["od_in"], read["od_out"] = (ns_in, 0, TT), (x_ready, at["mix1"][1], TT)
        if "kv" in layers:
            read["kv"] = (kv_in, 0, TT)
        if "sb" in layers:
            read["sb_q"], read["sb_out"] = (sb_in, 0, TT), (x_ready, at["sb"][1], TT)
        readers = [(read[q.name][0], read[q.name][1] + read[q.name][2] * (b + 1))
                   for q in prod.values() for b in range(q.blocks)]

        block = ctx.enter_context(nc.Block())

        mixers = [a for a in layers if a in ("mix0", "mix1", "sb")]
        normed = [a for a in layers if a in NORMS]

        def y_before(layer):
            return TT * mixers.index(layer)

        def y_banks(layer, tt=0):
            before = sum(TT * (1 if a == "mix0" else 2) for a in mixers[:mixers.index(layer)])
            return before + tt * (1 if layer == "mix0" else 2)

        sb_rows = [(g, qt) for qt in range(TT) for g in range(4)]
        sb_units = [(g, qt, kt) for g, qt in sb_rows for kt in range(qt, -1, -1)]

        ns_units = [(tt, br, g) for tt in range(TT) for br in range(2) for g in range(4)]
        NS_COL = {"kc": 0, "vc": 256, "q": 512, "ks": 1536, "vs": 1792, "kw": 2048, "vw": 2304}

        def steps(first, blocks):
            pairs = (blocks - first) // 2
            return pairs, first + 2 * pairs

        @block.sync
        def _(sp):
            def load(slot, panel, wait_lo):
                if wait_lo is not None:
                    sp.wait_ge(lo_ready, wait_lo)
                sp.dma_start(raw[:, slot, :], dram["stream"][panel, :, :]).then_inc(raw_full[slot], 16)

            sp.dma_start(const[:, 0:CONST_FIRST], dram["const"][:, 0:CONST_FIRST]).then_inc(params_loaded, 16)
            sp.dma_start(norm_t[:, :, :], dram["norm_t"]).then_inc(params_loaded, 16)
            sp.dma_start(x_sb[:, :, 0:NB], dram["x"][:, :, 0:NB]).then_inc(x_loaded, 16)
            load(0, 0, None)
            sp.dma_start(x_sb[:, :, NB:], dram["x"][:, :, NB:]).then_inc(x2_loaded, 16)
            load(1, 1, None)
            sp.dma_start(const[:, CONST_FIRST:], dram["const"][:, CONST_FIRST:]).then_inc(const_loaded, 16)
            for q in range(2, min(RING, panels)):
                load(q, q, None)
            first_row = 0 if "fin1" in layers else 1
            sp.dma_start(row[:, :], dram["fin_rows"][first_row:first_row + 1, :].partition_broadcast(P)).then_inc(row_loaded, 16)
            turns = (panels - RING) // RING
            if turns > 0:
                with sp.Fori(0, turns) as i:
                    for q in range(RING):
                        load(q, RING + RING * i + q, RING * 2 * i + 2 * q + 2)
            for q in range(RING + RING * max(turns, 0), panels):
                load(q % RING, q, 2 * (q - RING) + 2)
            if "fin2" in layers:
                n = at["fin2"][1]
                for half in range(2):
                    cols = slice(half * NB, (half + 1) * NB)
                    sp.wait_ge(x_ready, n + half + 1)
                    sp.dma_start(dram["out"][:, :, cols], x_sb[:, :, cols]).then_inc(out_stored, 16)
            else:
                t0, x0, _ = at[layers[-1]]
                sp.wait_ge(x_ready, x)
                for tt in range(TT):
                    sp.dma_start(dram["out"][:, tt, :], x_sb[:, tt, :]).then_inc(out_stored, 16)
            sp.wait_ge(out_stored, 16 * TT)

        @block.tensor
        def _(pe):
            def multiply(q, b, bs, i, j, a_hi, a_lo, k_at=0, halves=(0, 1)):
                panel = q.panel + q.per * b + j
                slot = (q.panel + q.per * bs + j) % 2
                nk = min(PK, q.kt - PK * j)
                half = nk // 2
                bank = acc[(q.block + bs) % 2]
                last = j == q.per - 1
                for s in halves:
                    if j == 0 and s == 0 and q.block + bs >= 2:
                        if bs >= 2:
                            free, before, each = read[q.name]
                            pe.wait_ge(free, before + each * (b - 1))
                        else:
                            free, count = readers[q.block + bs - 2]
                            pe.wait_ge(free, count)
                    pe.wait_ge(lo_ready, 2 * panel + s + 1)
                    for kk in range(s * half, (s + 1) * half):
                        k = PK * j + kk
                        hi = w_hi[:, slot, kk * NB:(kk + 1) * NB]
                        lo = w_lo[:, slot, kk * NB:(kk + 1) * NB]
                        for tt in range(TT):
                            rows = slice(tt * P, (tt + 1) * P)
                            pe.matmul(bank[tt], a_hi[:, k_at + k, rows], hi, start=(k == 0), stop=False)
                            pe.matmul(bank[tt], a_hi[:, k_at + k, rows], lo, start=False, stop=False)
                            done = pe.matmul(bank[tt], a_lo[:, k_at + k, rows], hi, start=False,
                                             stop=(k == q.kt - 1))
                if 1 in halves:
                    done.then_inc(w_used, 1)

            def transpose_batch(t, src, f_count, wait_for, count):
                pe.wait_ge(wait_for, count)
                if not (isinstance(t, int) and t == 0):
                    pe.wait_ge(t_lo, t)
                for tt in range(TT):
                    for f in range(f_count):
                        done = pe.transpose(tps[:, f, tt * P:(tt + 1) * P], src(tt, f), ident)
                done.then_inc(tps_ready, 1)

            def norm_batch(layer, half):
                t0, x0, _ = at[layer]
                if x0 == 0:
                    pe.wait_ge(params_loaded, 32)
                    transpose_batch(t0 + half, lambda tt, f: x_sb[:, tt, (4 * half + f) * P:(4 * half + f + 1) * P],
                                    4, x2_loaded if half else x_loaded, 16)
                    return
                later = TT if layer in early else 1 if after_final(layer) else 0
                need = x0 if half else x0 - later
                transpose_batch(t0 + half, lambda tt, f: x_sb[:, tt, (4 * half + f) * P:(4 * half + f + 1) * P],
                                4, x_ready, need)

            def enter(layer, q, b_hi=h_hi, b_lo=h_lo):
                t0 = at[layer][0]
                if layer not in early:
                    norm_batch(layer, 0)
                pe.wait_ge(t_lo, t0 + 1)
                multiply(q, 0, 0, 0, 0, h_hi, h_lo, halves=(0,))
                norm_batch(layer, 1)
                multiply(q, 0, 0, 0, 0, h_hi, h_lo, halves=(1,))
                pe.wait_ge(t_lo, t0 + 2)
                if layer == "kv" and early_norm(layer):
                    norm_batch(early_norm(layer), 0)
                multiply(q, 0, 0, 0, 1, h_hi, h_lo)
                if at[layer][1] == 0:
                    pe.wait_ge(const_loaded, 16)

            def hidden_layer(layer, f_count):
                up, down = prod[layer + "_up"], prod[layer + "_down"]
                t0 = at[layer][0] + 2
                tm_at = hidden_before[layer]

                def hidden_t(b):
                    transpose_batch(t0 + b, lambda tt, f: tm[:, tt, f * P:(f + 1) * P], f_count,
                                    tm_ready, tm_at + b + 1)

                enter(layer, up)

                def body(b, bs, i):
                    multiply(up, b, bs, i, 0, h_hi, h_lo)
                    hidden_t(b - 1)
                    multiply(up, b, bs, i, 1, h_hi, h_lo)

                body(1, 1, 0)
                pairs, rest = steps(2, up.blocks)
                with pe.Fori(0, pairs) as i:
                    for k in range(2):
                        body(2 + 2 * i + k, 2 + k, i)
                for b in range(rest, up.blocks):
                    body(b, b, 0)
                for b in range(down.blocks):
                    for j in range(down.per):
                        if b == 0 and j == 1:
                            hidden_t(up.blocks - 1)
                        if b == 0:
                            pe.wait_ge(t_lo, t0 + min(up.blocks, -(-min(PK * (j + 1), down.kt) // f_count)))
                        if b == 1 and j == 3 and early_norm(layer):
                            norm_batch(early_norm(layer), 0)
                        multiply(down, b, b, 0, j, hid_hi, hid_lo)

            def in_product(layer, q, between={}):
                enter(layer, q)
                for b in range(1, q.blocks):
                    for j in range(q.per):
                        multiply(q, b, b, 0, j, h_hi, h_lo)
                        if b + 0.5 * j in between:
                            between[b + 0.5 * j]()

            def out_product(layer, q):
                for b in range(q.blocks):
                    for j in range(q.per):
                        if b == 1 and j == 1 and early_norm(layer):
                            norm_batch(early_norm(layer), 0)
                        if b == 0:
                            pe.wait_ge(y_lo, y_banks(layer, TT) - (1 if j == 0 and layer != "mix0" else 0))
                        multiply(q, b, b, 0, j, h_hi, h_lo)

            def transpose_y(layer, tt, src, tiles=8, bank=4):
                n = y_before(layer) + tt
                pe.wait_ge(y_tm, n + 1)
                if n:
                    pe.wait_ge(y_lo, y_banks(layer, tt))
                for f in range(tiles):
                    done = pe.transpose(ps[:, bank + f // 4, f % 4 * P:(f % 4 + 1) * P],
                                        src[:, f * P:(f + 1) * P], ident)
                done.then_inc(y_tps, 1)

            def spatial_gating():
                q, out = prod["sgu_in"], prod["sgu_out"]
                t0 = at["sgu"][0] + 2

                def mix(pair):
                    if pair:
                        pe.wait_ge(sgu_s, TT * pair)
                    for tt in range(TT):
                        for g in range(2):
                            at_col = (2 * pair + g) * 256
                            done = pe.matmul(ps[:, 6 + tt, g * 256:(g + 1) * 256], ws_t[:, 2 * pair + g, :],
                                             sgu_z[:, tt, at_col:at_col + 256], start=True, stop=True)
                        done.then_inc(sgu_mix, 1)

                def gated_t(pair):
                    transpose_batch(t0 + pair, lambda tt, f: sgu_z[:, tt, 2 * D + (4 * pair + f) * P:2 * D + (4 * pair + f + 1) * P],
                                    4, sgu_s, TT * (pair + 1))

                def first_mix():
                    pe.wait_ge(sgu_ws, 1)
                    pe.wait_ge(sgu_v, 3 * TT)
                    mix(0)

                in_product("sgu", q, {7: first_mix})
                gated_t(0)
                mix(1)
                mix(2)
                gated_t(1)
                for b in range(out.blocks):
                    for j in range(out.per):
                        if b == 0:
                            pe.wait_ge(t_lo, t0 + j + 1)
                        if b == 1 and j == 2 and early_norm("sgu"):
                            norm_batch(early_norm("sgu"), 0)
                        multiply(out, b, b, 0, j, hid_hi, sgu_lo)
                        if b == 0 and j == 0:
                            mix(3)
                        if b == 0 and j < 2:
                            gated_t(j + 2)

            def stick_breaking():
                q, out = prod["sb_q"], prod["sb_out"]

                def keys_t():
                    pe.wait_ge(sb_copied, 2)
                    pe.wait_ge(t_lo, at["sb"][0] + 2)
                    for n in range(2):
                        for f in range(2):
                            for tt in range(TT):
                                done = pe.transpose(ps[:, 4 + n, f * T + tt * P:f * T + (tt + 1) * P],
                                                    sb_kd[:, tt, 2 * n + f].rearrange("p r d -> p (r d)"), ident)
                        done.then_inc(sb_tp, 1)

                def query_t(block):
                    pe.wait_ge(sb_in, TT * (block + 1))
                    for n in (2 * block, 2 * block + 1):
                        pe.wait_ge(sb_ts, n + 1)
                        for f in range(2):
                            for tt in range(TT):
                                done = pe.transpose(ps[:, 4 + n % 2, f * T + tt * P:f * T + (tt + 1) * P],
                                                    sb_q[:, tt, (2 * n + f) * P:(2 * n + f + 1) * P], ident)
                        done.then_inc(sb_tp, 1)

                in_product("sb", q, {1: keys_t, 1.5: lambda: query_t(0)})
                query_t(1)

                def scores(u):
                    g, qt, kt = sb_units[u]
                    if u >= 2:
                        pe.wait_ge(sb_zm, u - 1)
                        pe.wait_ge(sb_ts, 6)
                    else:
                        pe.wait_ge(sb_ts, 4)
                    for par in range(2):
                        done = pe.matmul(ps[:, 2 * (u % 2) + par, 0:256], sb_kt[:, par, g, kt * P:(kt + 1) * P],
                                         sb_qt[:, 2 * g:2 * g + 2, qt * P:(qt + 1) * P], start=True, stop=True)
                    done.then_inc(sb_z, 1)

                def suffix_sums(u):
                    g, qt, kt = sb_units[u]
                    pe.wait_ge(sb_sp, u + 1)
                    if u >= 2:
                        pe.wait_ge(sb_arg, u - 1)
                    carry = kt < qt
                    done = pe.matmul(ps[:, 4 + u % 2, :], cst("suffix"), sb_s[:, u % 8, 1, :, :], start=True, stop=not carry)
                    if carry:
                        done = pe.matmul(ps[:, 4 + u % 2, :], cst("ones"), sb_s[:, (u - 1) % 8, 1, :, :], start=False, stop=True)
                    done.then_inc(sb_rev, 1)

                def values(u):
                    g, qt, kt = sb_units[u]
                    pe.wait_ge(sb_a, u + 1)
                    if g == 0 and kt == qt and qt:
                        pe.wait_ge(y_lo, y_banks("sb", qt))
                    for par in range(2):
                        done = pe.matmul(ps[64 * par:64 * par + 64, 6 + g // 2, g % 2 * 256:g % 2 * 256 + 256],
                                         kv_tm[:, kt, 256 + g * 64:256 + (g + 1) * 64], sb_s[:, u % 8, 0, par, :],
                                         start=(kt == qt and g % 2 == 0), stop=True, skip_group_check=True)
                    done.then_inc(sb_av, 1)

                n = len(sb_units)
                for u in range(4):
                    scores(u)
                for p in range(n // 2 + 1):
                    for u in (2 * p, 2 * p + 1):
                        if u < n:
                            suffix_sums(u)
                    for u in (2 * p, 2 * p + 1):
                        if u + 4 < n:
                            scores(u + 4)
                    if p:
                        values(2 * p - 2)
                        values(2 * p - 1)
                out_product("sb", out)

            def delta_rule():
                q, out = prod["ev_in"], prod["ev_out"]

                def block_t(n):
                    pe.wait_ge(gd_in, TT * (n + 1))
                    if n == 0:
                        pe.wait_ge(t_lo, at["mix0"][0] + 2)
                    else:
                        pe.wait_ge(gd_ts, n)
                    for tt in range(TT):
                        for f in range(4):
                            done = pe.transpose(tps[:, f, tt * P:(tt + 1) * P], tm[:, tt, f * P:(f + 1) * P], ident)
                    done.then_inc(gd_tp, 1)

                def gate_rows():
                    pe.wait_ge(gd_split, 2)
                    for tt in range(TT):
                        rows = slice(tt * P, (tt + 1) * P)
                        for k in range(DK):
                            hi, lo = gd_wab_hi[:, k * 16:(k + 1) * 16], gd_wab_lo[:, k * 16:(k + 1) * 16]
                            dst = ps[:, 6, tt * 16:(tt + 1) * 16]
                            pe.matmul(dst, h_hi[:, k, rows], hi, start=(k == 0 and tt == 0), stop=False, skip_group_check=True)
                            pe.matmul(dst, h_hi[:, k, rows], lo, start=False, stop=False, skip_group_check=True)
                            done = pe.matmul(dst, h_lo[:, k, rows], hi, start=False, stop=True, skip_group_check=True)
                    done.then_inc(gd_abp, 1)

                def gate_sums():
                    pe.wait_ge(gd_gg, 1)
                    g = gd_g[:, 5, :, :].rearrange("p t h -> p (t h)")
                    for n, name in enumerate(("cum", "chunk", "even", "odd")):
                        done = pe.matmul(ps[:, 7, n * 16:(n + 1) * 16], cst(name), g, start=(n == 0), stop=True,
                                         skip_group_check=True)
                    done.then_inc(gd_gp, 1)

                def between(b):
                    block_t(b - 1)
                    if b == 2:
                        gate_rows()
                    if b == 6:
                        gate_sums()

                in_product("mix0", q, {b: (lambda b=b: between(b)) for b in range(1, 7)})

                for tt in range(TT):
                    one = 1 + tt
                    pe.wait_ge(gd_cs, 3)
                    if tt == 0:
                        pe.wait_ge(gd_in, TT * 7)
                        pe.wait_ge(gd_ts, 6)
                    else:
                        pe.wait_ge(gd_of, tt)
                        pe.wait_ge(gd_st, 2 * tt)
                    for n in range(3):
                        for f in range(4):
                            done = pe.transpose(ps[:, n, f * P:(f + 1) * P], gd_c[:, 4 * n + f, tt * P:(tt + 1) * P], ident)
                        done.then_inc(gd_q, 1)
                    pe.wait_ge(gd_gs, 1)
                    pe.wait_ge(gd_gbr, one)
                    for par in range(2):
                        for pair in range(4):
                            done = pe.matmul(ps[:, 6 + par, pair * P:(pair + 1) * P], gd_gb[:, 2 * pair + par, :],
                                             cst("cum"), start=True, stop=True)
                        done.then_inc(gd_bc, 1)
                    for n in range(4):
                        pe.wait_ge(gd_kn, 5 * tt + n + 1)
                        bank = (3, 4, 5, 0)[n]
                        if n == 3:
                            pe.wait_ge(gd_kn, 5 * tt + 5)
                        for f in range(4):
                            done = pe.transpose(ps[:, bank, f * P:(f + 1) * P], gd_tm[:, n, f * P:(f + 1) * P], ident)
                        done.then_inc(gd_ft, 1)
                    pe.wait_ge(gd_fa, 2 * one)
                    pe.wait_ge(gd_fv, 2 * one)
                    for bank, n in ((1, 1), (3, 2)):
                        for par in range(2):
                            rows = slice(64 * par, 64 * par + 64)
                            for pair in range(4):
                                done = pe.matmul(ps[:, bank + par, pair * P:(pair + 1) * P], gd_t[rows, 0, pair, :],
                                                 gd_t[rows, n, pair, :], start=(pair == 0), stop=True, skip_group_check=True)
                            done.then_inc(gd_kk, 1)
                    if tt:
                        transpose_y("mix0", 0, gd_o[:, :], tiles=4, bank=5)

                    def units(par):
                        return range(4 * par, 4 * par + 4)

                    def bank_of(b, u):
                        return ps[:, b + u // 4, u % 4 * P:(u % 4 + 1) * P]

                    for par in range(2):
                        pe.wait_ge(gd_x1, 2 * tt + par + 1)
                        pe.wait_ge(gd_de, 2 * one)
                        for u in units(par):
                            done = pe.transpose(bank_of(6, u), gd_invt[:, u, :], ident)
                        done.then_inc(gd_xp, 1)
                    for level in range(2, 7):
                        n = 10 * tt + 2 * (level - 2)
                        for par in range(2):
                            pe.wait_ge(gd_mlr, 5 * tt + level - 1)
                            if level == 2:
                                pe.wait_ge(gd_xs, 2 * tt + par + 1)
                                pe.wait_ge(gd_m, 2 * one)
                            else:
                                pe.wait_ge(gd_iv, n - 2 + par + 1)
                            for u in units(par):
                                done = pe.matmul(bank_of(0, u), gd_ml[:, level % 2, u, :], gd_inv[:, u, :],
                                                 start=(u % 4 == 0), stop=True, skip_group_check=True)
                            done.then_inc(gd_pp, 1)
                        for par in range(2):
                            pe.wait_ge(gd_ps, n + par + 1)
                            pe.wait_ge(gd_a, 2 * one)
                            if tt:
                                pe.wait_ge(y_lo, y_before("mix0") + tt)
                            if level < 6:
                                for u in units(par):
                                    pe.matmul(bank_of(2, u), gd_invt[:, u, :], gd_p[:, u, :], start=(u % 4 == 0),
                                              stop=True, skip_group_check=True)
                            for u in units(par):
                                done = pe.matmul(bank_of(4, u), gd_p[:, u, :], gd_invt[:, u, :], start=(u % 4 == 0),
                                                 stop=True, skip_group_check=True)
                            done.then_inc(gd_qp, 1)
                    pe.wait_ge(gd_iv, 10 * one)
                    pe.wait_ge(gd_kz, 3 * one)
                    for u in range(8):
                        h = 2 * (u % 4) + u // 4
                        done = pe.matmul(ps[:, 0, h * 64:(h + 1) * 64], gd_invt[:, u, :], gd_tm[:, 4, h * 64:(h + 1) * 64],
                                         start=(u == 0), stop=True, skip_group_check=True)
                    done.then_inc(gd_up, 1)
                    for u in range(8):
                        par, pair = u // 4, u % 4
                        h = 2 * pair + par
                        done = pe.matmul(ps[64 * par:64 * par + 64, 1, pair * P:(pair + 1) * P],
                                         gd_tm[:, 5, h * 64:(h + 1) * 64], gd_invt[:, u, :],
                                         start=(pair == 0), stop=True, skip_group_check=True)
                    done.then_inc(gd_up, 1)
                    pe.wait_ge(gd_ws, one)
                    if tt == 0:
                        pe.wait_ge(gd_z0, 2)
                    for c in range(2):
                        n = 2 * tt + c
                        if n:
                            pe.wait_ge(gd_st, n)
                            pe.wait_ge(gd_os, n)
                        for bank, lhs in ((2, gd_wt), (3, None)):
                            for pair in range(4):
                                a = lhs[:, pair, :] if lhs is not None else gd_t[:, 3, pair, :]
                                done = pe.matmul(ps[:, bank, pair * P:(pair + 1) * P], a, gd_s[:, pair, :],
                                                 start=(pair == 0), stop=True, skip_group_check=True)
                            done.then_inc(gd_sp, 1)
                        pe.wait_ge(gd_vs, n + 1)
                        for pair in range(4):
                            cols = slice(pair * P, (pair + 1) * P)
                            done = pe.matmul(ps[:, 4, cols], gd_tm[:, 6 + c, cols], gd_vn[:, cols],
                                             start=(pair == 0), stop=True, skip_group_check=True)
                        done.then_inc(gd_dp, 1)
                    for u in range(8):
                        h = 2 * (u % 4) + u // 4
                        done = pe.matmul(ps[:, 5, h * 64:(h + 1) * 64], gd_at[:, u, :], gd_vn[:, h * 64:(h + 1) * 64],
                                         start=(u == 0), stop=True, skip_group_check=True)
                    done.then_inc(gd_op, 1)
                transpose_y("mix0", 1, gd_o[:, :], tiles=4, bank=5)
                pe.wait_ge(gd_ybl, 1)
                out_product("mix0", out)

            def sparse_attention():
                q, out = prod["od_in"], prod["od_out"]

                def twice_t(bank, heads, done_sem):
                    for g in range(4):
                        for tt in range(TT):
                            done = pe.transpose(ps[:, bank + g // 2, g % 2 * T + tt * P:g % 2 * T + (tt + 1) * P],
                                                heads(tt, g).rearrange("p r d -> p (r d)"), ident)
                    done.then_inc(done_sem, 1)

                def query_t(n, bank, done_sem):
                    for f in range(2):
                        for tt in range(TT):
                            at_col = NS_COL["q"] + (2 * n + f) * P
                            done = pe.transpose(ps[:, bank, f * T + tt * P:f * T + (tt + 1) * P],
                                                ns_tm[:, tt, at_col:at_col + P], ident)
                    done.then_inc(done_sem, 1)

                def compressed_inputs():
                    pe.wait_ge(ns_in, TT)
                    pe.wait_ge(t_lo, at["mix1"][0] + 2)
                    for kv in range(2):
                        twice_t(4 + 2 * kv, lambda tt, g: ns_kcv[:, tt, 4 * kv + g], ns_cvt)

                def compressed_hidden():
                    pe.wait_ge(ns_params, 16 * 5)
                    for kv in range(2):
                        pe.wait_ge(ns_x, 5 * (kv + 1))
                        for c in range(2):
                            at_col = (2 * kv + c) * 64
                            for n in range(16):
                                done = pe.matmul(ps[:, 4, at_col:at_col + 64], ns_w1[:, kv, n, c * P:(c + 1) * P],
                                                 ns_xp[:, kv, n // 8, n % 8, :], start=(at_col == 0 and n == 0),
                                                 stop=(n == 15), skip_group_check=True)
                    done.then_inc(ns_hp, 1)

                def gate_rows():
                    pe.wait_ge(ns_split, 2)
                    for tt in range(TT):
                        rows = slice(tt * P, (tt + 1) * P)
                        for k in range(DK):
                            hi, lo = ns_wg_hi[:, k * 48:(k + 1) * 48], ns_wg_lo[:, k * 48:(k + 1) * 48]
                            dst = ps[:, 7, tt * 48:(tt + 1) * 48]
                            first = k == 0 and tt == 0
                            pe.matmul(dst, h_hi[:, k, rows], hi, start=first, stop=False, skip_group_check=True)
                            pe.matmul(dst, h_hi[:, k, rows], lo, start=False, stop=False, skip_group_check=True)
                            done = pe.matmul(dst, h_lo[:, k, rows], hi, start=False, stop=True, skip_group_check=True)
                    done.then_inc(ns_gp, 1)

                def compressed_kv():
                    pe.wait_ge(ns_hs, 1)
                    for c in range(2):
                        pe.matmul(ps[:, 6, 0:64], ns_w2k[:, c, :], ns_ht[:, 0, c, :], start=(c == 0), stop=(c == 1))
                    for c in range(2):
                        done = pe.matmul(ps[0:64, 5, 0:64], ns_ht[:, 1, c, :], ns_w2v[:, c, :],
                                         start=(c == 0), stop=(c == 1))
                    done.then_inc(ns_kvp, 1)
                    pe.wait_ge(ns_in, TT * 3)
                    query_t(0, 4, ns_qtp)

                def queries_t():
                    pe.wait_ge(ns_kvs, 3)
                    pe.wait_ge(ns_gs, 1)
                    for n in range(1, 4):
                        query_t(n, 4 + n, ns_qtp)

                def compressed_scores():
                    pe.wait_ge(ns_qts, 4)
                    for tt in range(TT):
                        for pair in range(8):
                            at_col = tt * 256 + pair * 32
                            done = pe.matmul(ps[:, 4, at_col:at_col + 32], ns_qt[:, pair, tt * P:(tt + 1) * P],
                                             ns_kct[:, pair // 2, :, :].rearrange("p r n -> p (r n)"),
                                             start=(at_col == 0), stop=True, skip_group_check=True)
                    done.then_inc(ns_cs, 1)

                in_product("mix1", q, {1: compressed_inputs, 2: lambda: (compressed_hidden(), gate_rows()), 3: compressed_kv,
                                       3.5: queries_t, 4: compressed_scores})

                pe.wait_ge(ns_in, TT * 5)
                pe.wait_ge(ns_krope, 14)
                twice_t(0, lambda tt, g: ns_kd[:, 0, tt, g], ns_rtp)
                pe.wait_ge(ns_rope, 6)
                query_t(0, 2, ns_rtp)
                query_t(1, 3, ns_rtp)
                pe.wait_ge(ns_rts, 1)
                query_t(2, 0, ns_rtp)
                query_t(3, 1, ns_rtp)
                pe.wait_ge(ns_krope, 28)
                twice_t(6, lambda tt, g: ns_kd[:, 1, tt, g], ns_rtp)
                pe.wait_ge(ns_rts, 5)

                def group_scores(u):
                    tt, br, g = ns_units[u]
                    if u >= 2:
                        pe.wait_ge(ns_m, 4 * (u - 1))
                    if br:
                        pe.wait_ge(ns_rts, 6)
                    keys = (tt + 1) * P
                    for jh in range(2):
                        for par in range(2):
                            done = pe.matmul(ps[:, 2 * (u % 2) + par, jh * keys:(jh + 1) * keys],
                                             ns_qrt[:, 2 * g + jh, tt * P:(tt + 1) * P], ns_kt[:, par, br, g, 0:keys],
                                             start=(jh == 0), stop=True, skip_group_check=True)
                    done.then_inc(ns_s, 1)

                def weights_t(u):
                    tt, br, g = ns_units[u]
                    pe.wait_ge(ns_w, u + 1)
                    if u:
                        pe.wait_ge(ns_ts, u)
                    for j in range(4):
                        for kt in range(tt + 1):
                            n = j * (tt + 1) + kt
                            done = pe.transpose(ps[:, 4 + n // 4, n % 4 * P:(n % 4 + 1) * P],
                                                ns_p[:, u % 3, j, kt * P:(kt + 1) * P], ident)
                    done.then_inc(ns_tp, 1)

                def values(u):
                    tt, br, g = ns_units[u]
                    pe.wait_ge(ns_ts, u + 1)
                    col = (NS_COL["vs"], NS_COL["vw"])[br] + g * 64
                    for par in range(2):
                        for kt in range(tt + 1):
                            n = par * (tt + 1) + kt
                            done = pe.matmul(ps[64 * par:64 * par + 64, 6 + g // 2, g % 2 * 256:g % 2 * 256 + 256],
                                             ns_tm[:, kt, col:col + 64], ns_pt[:, u % 2, n:n + 2 * (tt + 1) + 1:2 * (tt + 1), :],
                                             start=False, stop=True, skip_group_check=True)
                    done.then_inc(ns_pv, 1)

                def compressed_values(tt):
                    if tt:
                        pe.wait_ge(y_lo, y_banks("mix1", tt))
                    else:
                        pe.wait_ge(ns_rts, 6)
                    for g in range(4):
                        for par in range(2):
                            pe.matmul(ps[64 * par:64 * par + 64, 6 + g // 2, g % 2 * 256:g % 2 * 256 + 256],
                                      ns_vc[:, g, :], ns_cpt[:, tt, par:par + 3:2, :], start=(g % 2 == 0), stop=True,
                                      skip_group_check=True)

                n = len(ns_units)
                group_scores(0)
                group_scores(1)
                pe.wait_ge(ns_cd, 12)
                for tt in range(TT):
                    for j in range(4):
                        done = pe.transpose(ps[0:64, 4 + tt, j * P:(j + 1) * P], ns_c[:, tt, j * 64:(j + 1) * 64], ident)
                done.then_inc(ns_ctp, 1)
                pe.wait_ge(ns_cts, 1)
                for u in range(n):
                    if u + 2 < n:
                        group_scores(u + 2)
                    weights_t(u)
                    if u:
                        values(u - 1)
                    if u % (n // TT) == 0:
                        compressed_values(u // (n // TT))
                values(n - 1)
                out_product("mix1", out)

            for layer in layers:
                if layer[:3] == "mlp":
                    hidden_layer(layer, 4)
                elif layer[:3] == "ffn":
                    hidden_layer(layer, 2)
                elif layer == "mix0":
                    delta_rule()
                elif layer == "mix1":
                    sparse_attention()
                elif layer == "sgu":
                    spatial_gating()
                elif layer == "kv":
                    in_product("kv", prod["kv"])
                elif layer == "sb":
                    stick_breaking()

        @block.scalar
        def _(act):
            def split(q, b, bs, i, j):
                static = q.panel + q.per * bs + j
                panel = q.panel + q.per * b + j
                half = min(PK, q.kt - PK * j) // 2 * NB
                act.wait_ge(raw_full[static % RING], 16 * (static // RING + 1) + 16 * i)
                if static >= 2:
                    act.wait_ge(w_used, panel - 1)
                for s in range(2):
                    part = slice(s * half, (s + 1) * half)
                    act.activation(w_hi[:, static % 2, part], raw[:, static % RING, part],
                                   ACT.Copy).then_inc(hi_ready, 1)

            def norm_store(layer, half):
                t0 = at[layer][0]
                n = NORMS.index(layer)
                act.wait_ge(tps_ready, t0 + half + 1)
                for f in range(4):
                    k = 4 * half + f
                    done = act.activation(h_hi[:, k, :], tps[:, f, :], ACT.Copy, scale=norm_t[:, n, k:k + 1])
                    if f == 1:
                        done.then_inc(norm_hi, 1)
                done.then_inc(t_hi, 1)

            def square_sums(layer):
                _, x0, r0 = at[layer]
                for tt in range(TT):
                    if x0:
                        act.wait_ge(x_ready, x0 if after_final(layer) else x0 - TT + tt + 1)
                    if tt:
                        act.wait_ge(ss_ready, TT * r0 + tt)
                    act.activation(junk[:, :], x_sb[:, tt, :], ACT.Square,
                                   accum_out=ss[:, tt:tt + 1]).then_inc(ss_ready, 1)

            def enter(layer, q):
                if at[layer][1] == 0:
                    act.wait_ge(params_loaded, 32)
                    norm_store(layer, 0)
                if following.get("kv") != layer:
                    split(q, 0, 0, 0, 0)
                if layer not in early and at[layer][1]:
                    norm_store(layer, 0)
                if at[layer][1]:
                    split(q, 0, 0, 0, 1)
                norm_store(layer, 1)
                if not at[layer][1]:
                    split(q, 0, 0, 0, 1)
                if layer == "kv" and early_norm(layer):
                    next_norm(layer, q.panel + 1)
                if at[layer][1] == 0:
                    act.wait_ge(const_loaded, 16)
                square_sums(layer)
                act.wait_ge(rstd_ready, at[layer][2] + 1)

            def hidden_layer(layer, f_count):
                up, down = prod[layer + "_up"], prod[layer + "_down"]
                t0 = at[layer][0] + 2

                def evacuate(b, bs):
                    act.wait_ge(w_used, up.panel + up.per * (b + 1))
                    bank = acc[(up.block + bs) % 2]
                    for tt in range(TT):
                        if f_count == 4:
                            done = act.activation(tm[:, tt, :], bank[tt], ACT.Relu, scale=rstd[:, tt:tt + 1])
                        else:
                            done = act.activation(tm[:, tt, 0:256], bank[tt][:, 0:256], ACT.Silu,
                                                  scale=rstd[:, tt:tt + 1])
                        done.then_inc(act_tm, 1)

                def store_t(b):
                    act.wait_ge(tps_ready, t0 + b + 1)
                    act.activation(hid_hi2[:, bass.ds(b * (f_count * T), f_count * T)],
                                   tps[:, 0:f_count, :].rearrange("p f t -> p (f t)"), ACT.Copy).then_inc(t_hi, 1)

                enter(layer, up)

                def body(b, bs, i):
                    split(up, b, bs, i, 0)
                    split(up, b, bs, i, 1)
                    evacuate(b - 1, bs - 1)
                    store_t(b - 1)

                body(1, 1, 0)
                pairs, rest = steps(2, up.blocks)
                with act.Fori(0, pairs) as i:
                    for k in range(2):
                        body(2 + 2 * i + k, 2 + k, i)
                for b in range(rest, up.blocks):
                    body(b, b, 0)
                for b in range(down.blocks):
                    for j in range(down.per):
                        if b == 0 and j == 2:
                            evacuate(up.blocks - 1, up.blocks - 1)
                            store_t(up.blocks - 1)
                        if b == 1 and j == 4 and early_norm(layer):
                            norm_store(early_norm(layer), 0)
                        split(down, b, b, 0, j)

            def in_product(layer, q, out, evacuate, between={}, before_last=None, ahead=1):
                enter(layer, q)
                for b in range(1, q.blocks):
                    for j in range(q.per):
                        split(q, b, b, 0, j)
                    if b == q.blocks - 1 and before_last:
                        before_last()
                    evacuate(b - 1)
                    if b in between:
                        between[b]()
                if out:
                    for j in range(ahead):
                        split(out, 0, 0, 0, j)
                elif "kv" in following:
                    split(prod[following["kv"] + "_up"], 0, 0, 0, 0)
                evacuate(q.blocks - 1)
                if out:
                    for j in range(ahead, 2):
                        split(out, 0, 0, 0, j)

            def copy_block(q, dst, done_sem, func=ACT.Copy):
                def evacuate(b):
                    act.wait_ge(w_used, q.panel + q.per * (b + 1))
                    for tt in range(TT):
                        act.activation(dst(tt, b), acc[(q.block + b) % 2][tt], func,
                                       scale=rstd[:, tt:tt + 1]).then_inc(done_sem, 1)
                return evacuate

            def out_product(layer, q):
                for b in range(q.blocks):
                    for j in range(q.per):
                        if b or j >= 2:
                            split(q, b, b, 0, j)
                next_norm(layer, q.panel + q.per + 1)

            def next_norm(layer, panels_used):
                if early_norm(layer):
                    act.wait_ge(w_used, panels_used)
                    norm_store(early_norm(layer), 0)

            def store_y(layer, tt, tiles=8, bank=4):
                n = y_before(layer) + tt
                if layer == "mix0":
                    act.wait_ge(y_tps, n + 1)
                for k in range(tiles // 4):
                    act.activation(h_hi[:, 4 * k:4 * k + 4, tt * P:(tt + 1) * P],
                                   ps[:, bank + k, :].rearrange("p (f t) -> p f t", t=P), ACT.Copy).then_inc(y_hi, 1)

            def spatial_gating():
                q, out = prod["sgu_in"], prod["sgu_out"]
                t0 = at["sgu"][0] + 2
                enter("sgu", q)

                def evacuate(b):
                    act.wait_ge(w_used, q.panel + q.per * (b + 1))
                    for tt in range(TT):
                        sums = {"accum_out": v_sums[:, tt, b:b + 1]} if b < 4 else {}
                        act.activation(sgu_z[:, tt, b * NB:(b + 1) * NB], acc[(q.block + b) % 2][tt],
                                       ACT.Gelu_apprx_tanh, scale=rstd[:, tt:tt + 1], **sums).then_inc(sgu_in, 1)

                for b in range(1, q.blocks):
                    for j in range(q.per):
                        split(q, b, b, 0, j)
                    evacuate(b - 1)
                    if b == 5:
                        act.wait_ge(sgu_mean, 2)
                        for tt in range(TT):
                            for half in range(2):
                                if tt or half:
                                    act.wait_ge(sgu_sq, 2 * tt + half)
                                act.activation(junk[:, :], sgu_z[:, tt, half * D:(half + 1) * D], ACT.Square,
                                               bias=v_stat[:, 0, tt:tt + 1],
                                               accum_out=v_sq[:, tt, half:half + 1]).then_inc(sgu_sq, 1)
                split(out, 0, 0, 0, 0)
                evacuate(q.blocks - 1)
                for b in range(out.blocks):
                    for j in range(out.per):
                        if b == 0:
                            act.wait_ge(tps_ready, t0 + j + 1)
                            act.activation(hid_hi2[:, 4 * j * T:4 * (j + 1) * T], tps.rearrange("p f t -> p (f t)"),
                                           ACT.Copy).then_inc(t_hi, 1)
                            if j + 1 < out.per:
                                split(out, b, b, 0, j + 1)
                        else:
                            if j == 3 and early_norm("sgu"):
                                norm_store(early_norm("sgu"), 0)
                            split(out, b, b, 0, j)

            def stick_breaking():
                q, out = prod["sb_q"], prod["sb_out"]

                def store_t(first):
                    act.wait_ge(sb_kz, 1)
                    for n in range(first, first + 2):
                        act.wait_ge(sb_tp, n + 1)
                        if n >= 2:
                            done = act.activation(sb_qt[:, 2 * n - 4:2 * n - 2, :].rearrange("p f t -> p (f t)"),
                                                  ps[:, 4 + n % 2, :], ACT.Copy)
                        else:
                            for par in range(2):
                                rows = slice(64 * par, 64 * par + 64)
                                done = act.activation(sb_kt[rows, par, 2 * n:2 * n + 2, :].rearrange("p f t -> p (f t)"),
                                                      ps[rows, 4 + n % 2, :], ACT.Copy)
                        done.then_inc(sb_ts, 1)

                in_product("sb", q, out, copy_block(q, lambda tt, b: sb_q[:, tt, b * NB:(b + 1) * NB], sb_in),
                           {1: lambda: store_t(2)}, lambda: store_t(0))
                store_t(4)
                n = len(sb_units)

                def soft_exp(u):
                    soft = sb_s[:, u % 8, 1, :, :].rearrange("p a b -> p (a b)")
                    act.wait_ge(sb_abs, u + 1)
                    act.activation(soft, soft, ACT.Exp, scale=-1.0).then_inc(sb_ex, 1)

                def soft_log(u):
                    soft = sb_s[:, u % 8, 1, :, :].rearrange("p a b -> p (a b)")
                    act.wait_ge(sb_ex, u + 1)
                    act.activation(soft, soft, ACT.Ln, bias=1.0).then_inc(sb_ln, 1)

                def weights(u):
                    z = sb_s[:, u % 8, 0, :, :].rearrange("p a b -> p (a b)")
                    act.wait_ge(sb_arg, u + 1)
                    act.activation(z, z, ACT.Exp).then_inc(sb_a, 1)

                for p in range(-1, n // 2 + 1):
                    for u in (2 * p + 2, 2 * p + 3):
                        if u < n:
                            soft_exp(u)
                    if p == 3:
                        act.wait_ge(sb_av, 4)
                        store_y("sb", 0, bank=6)
                    for u in (2 * p - 2, 2 * p - 1):
                        if u >= 0:
                            weights(u)
                    for u in (2 * p + 2, 2 * p + 3):
                        if u < n:
                            soft_log(u)
                act.wait_ge(sb_av, n)
                store_y("sb", 1, bank=6)
                out_product("sb", out)

            def delta_rule():
                q, out = prod["ev_in"], prod["ev_out"]

                def evacuate(b):
                    act.wait_ge(w_used, q.panel + q.per * (b + 1))
                    if 0 < b < 6:
                        act.wait_ge(gd_tp, b)
                    for tt in range(TT):
                        dst, func = (tm[:, tt, :], ACT.Copy) if b < 6 else (gd_z[:, tt, :], ACT.Silu)
                        act.activation(dst, acc[(q.block + b) % 2][tt], func, scale=rstd[:, tt:tt + 1]).then_inc(gd_in, 1)

                def store(n):
                    if n == 4:
                        return
                    dst = (gd_x[:, 0:4, 3:], gd_x[:, 4:8, 3:], gd_x[:, 8:12, 3:], gd_ch[:, :, 2:], None, gd_b[:, :, :])[n]
                    act.wait_ge(gd_tp, n + 1)
                    if n == 5:
                        act.wait_ge(gd_ts, 5)
                    act.activation(dst, tps, ACT.Copy).then_inc(gd_ts, 1)

                def silu(n):
                    c = gd_c[:, 4 * n:4 * n + 4, :].rearrange("p f t -> p (f t)")
                    act.wait_ge(gd_cv, n + 1)
                    act.activation(c, c, ACT.Silu).then_inc(gd_cs, 1)

                def between(b):
                    store(b - 1)
                    if 3 <= b <= 5:
                        silu(b - 3)
                    if b == 1:
                        act.wait_ge(gd_params, 16 * 6)
                        act.activation(gd_wab_hi[:, :], gd_wab[:, :], ACT.Copy).then_inc(gd_split, 1)
                    if b == 4:
                        act.activation(gd_a_log[:, :], gd_a_log[:, :], ACT.Exp).then_inc(gd_ge, 1)
                        act.wait_ge(gd_ga, 1)
                        act.activation(gd_g[:, 2, :, :], gd_g[:, 2, :, :], ACT.Exp, scale=-1.0).then_inc(gd_ge, 1)
                        act.activation(gd_g[:, 3, :, :], gd_g[:, 1, :, :], ACT.Exp, scale=-1.0).then_inc(gd_ge, 1)
                        act.wait_ge(gd_ge, 2)
                        act.activation(gd_g[:, 4, :, :], gd_g[:, 2, :, :], ACT.Ln, bias=1.0).then_inc(gd_ge, 1)

                in_product("mix0", q, out, evacuate, {b: (lambda b=b: between(b)) for b in range(1, 7)}, ahead=2)
                act.wait_ge(gd_gs, 1)
                act.activation(gd_exp[:, :, :, :], gd_sum[:, :, :, :], ACT.Exp).then_inc(gd_gx, 1)
                act.wait_ge(gd_yb, 1)
                act.wait_ge(w_used, q.panel + q.per * q.blocks)
                act.activation(h_hi[:, 4:8, :], gd_sc[:, :, :], ACT.Copy).then_inc(gd_ybh, 1)

                for tt in range(TT):
                    one = 1 + tt
                    for n in range(2):
                        act.wait_ge(gd_q, 3 * tt + n + 1)
                        act.activation(gd_sq[:, n, :], ps[:, n, :], ACT.Square).then_inc(gd_qq, 1)
                    for par in range(2):
                        act.wait_ge(gd_da, 2 * tt + par + 1)
                        d = gd_dt[:, 4 * par:4 * par + 4, :]
                        act.activation(d, d, ACT.Exp).then_inc(gd_de, 1)
                    for n, bank in ((0, 3), (2, 5)):
                        act.wait_ge(gd_ft, 4 * tt + n + 1)
                        act.activation(gd_t[:, n, :, :].rearrange("p f t -> p (f t)"), ps[:, bank, :],
                                       ACT.Copy).then_inc(gd_fa, 1)
                    if tt:
                        store_y("mix0", 0, tiles=4, bank=5)
                    for par in range(2):
                        act.wait_ge(gd_xp, 2 * tt + par + 1)
                        act.activation(gd_inv[:, 4 * par:4 * par + 4, :].rearrange("p u t -> p (u t)"), ps[:, 6 + par, :],
                                       ACT.Copy).then_inc(gd_xs, 1)
                    for n in range(10):
                        par = n % 2
                        act.wait_ge(gd_pp, 10 * tt + n + 1)
                        act.activation(gd_p[:, 4 * par:4 * par + 4, :].rearrange("p u t -> p (u t)"), ps[:, par, :],
                                       ACT.Copy).then_inc(gd_ps, 1)
                    act.wait_ge(gd_up, 2 * tt + 1)
                    act.activation(gd_u[:, :], ps[:, 0, :], ACT.Copy).then_inc(gd_us, 1)
                    for c in range(2):
                        rows = slice(64 * c, 64 * c + 64)
                        act.wait_ge(gd_sp, 4 * tt + 2 * c + 2)
                        act.activation(gd_o[rows, :], ps[rows, 3, :], ACT.Copy).then_inc(gd_os, 1)
                    act.wait_ge(gd_of, one)
                    act.activation(gd_osq[:, :], gd_o[:, :], ACT.Square).then_inc(gd_oq, 1)
                store_y("mix0", 1, tiles=4, bank=5)
                out_product("mix0", out)

            def sparse_attention():
                q, out = prod["od_in"], prod["od_out"]

                def split_gate_weights():
                    act.wait_ge(ns_params, 16 * 5)
                    act.activation(ns_wg_hi[:, :], ns_wg[:, :], ACT.Copy).then_inc(ns_split, 1)

                def compressed_silu():
                    act.wait_ge(ns_hp, 1)
                    act.activation(ns_ht[:, :, :, :].rearrange("p k c n -> p (k c n)"), ps[:, 4, 0:256],
                                   ACT.Silu).then_inc(ns_hs, 1)

                def gates():
                    act.wait_ge(ns_gp, 1)
                    for tt in range(TT):
                        done = act.activation(ns_gate[:, tt, :], ps[:, 7, tt * 48:(tt + 1) * 48], ACT.Sigmoid,
                                              scale=rstd[:, tt:tt + 1])
                    done.then_inc(ns_gs, 1)

                def queries(first, end):
                    for n in range(first, end):
                        act.wait_ge(ns_qtp, n + 1)
                        act.activation(ns_qt[:, 2 * n:2 * n + 2, :].rearrange("p f t -> p (f t)"), ps[:, 4 + n, :],
                                       ACT.Copy).then_inc(ns_qts, 1)

                copy = copy_block(q, lambda tt, b: ns_tm[:, tt, b * NB:(b + 1) * NB], ns_in)

                def evacuate(b):
                    if b:
                        copy(b)
                        return
                    act.wait_ge(w_used, q.panel + q.per)
                    for tt in range(TT):
                        for half in range(2):
                            done = act.activation(ns_kcv[:, tt, :, half, :], acc[q.block % 2][tt].rearrange("p (h d) -> p h d", d=64),
                                                  ACT.Copy, scale=rstd[:, tt:tt + 1])
                        done.then_inc(ns_in, 1)

                in_product("mix1", q, out, evacuate,
                           {1: split_gate_weights, 2: lambda: (compressed_silu(), gates()), 3: lambda: queries(0, 1)},
                           lambda: queries(1, 4))

                def store_keys(br, banks):
                    for par in range(2):
                        rows = slice(64 * par, 64 * par + 64)
                        done = act.activation(ns_kt[rows, par, br, :, :].rearrange("p g t -> p (g t)"),
                                              two[banks][rows].rearrange("p b n -> p (b n)"), ACT.Copy)
                    done.then_inc(ns_rts, 1)

                act.wait_ge(ns_kz, 1)
                act.wait_ge(ns_rtp, 1)
                store_keys(0, 0)
                for n in range(4):
                    act.wait_ge(ns_rtp, n + 2)
                    act.activation(ns_qrt[:, 2 * n:2 * n + 2, :].rearrange("p g t -> p (g t)"), ps[:, (2, 3, 0, 1)[n], :],
                                   ACT.Copy).then_inc(ns_rts, 1)
                act.wait_ge(ns_cd, 6)
                act.activation(ns_c[:, :, :], ns_c[:, :, :], ACT.Exp, scale=0.125).then_inc(ns_ce, 1)
                act.wait_ge(ns_rtp, 6)
                store_keys(1, 6)

                n = len(ns_units)

                def exps(u):
                    tt, br, g = ns_units[u]
                    keys = (tt + 1) * P
                    act.wait_ge(ns_nm, u + 1)
                    for j in range(4):
                        act.activation(ns_p[:, u % 3, j, 0:keys], ns_p[:, u % 3, j, 0:keys], ACT.Exp, scale=0.125,
                                       bias=ns_st[:, u % 3, 1, j:j + 1],
                                       accum_out=ns_st[:, u % 3, 2, j:j + 1]).then_inc(ns_e, 1)

                def store_weights(u):
                    tt, br, g = ns_units[u]
                    if u >= 2:
                        act.wait_ge(ns_pv, u - 1)
                    act.wait_ge(ns_tp, u + 1)
                    act.activation(ns_pt[:, u % 2, 0:4 * (tt + 1), :].rearrange("p n t -> p (n t)"),
                                   two[4].rearrange("p b n -> p (b n)")[:, 0:4 * (tt + 1) * P], ACT.Copy).then_inc(ns_ts, 1)

                exps(0)
                act.wait_ge(ns_ctp, 1)
                act.activation(ns_cpt[:, :, :, :].rearrange("p k j t -> p k (j t)"), ps[0:64, 4:6, :], ACT.Copy).then_inc(ns_cts, 1)
                exps(1)
                for u in range(n):
                    store_weights(u)
                    if u + 2 < n:
                        exps(u + 2)
                    if (u + 1) % (n // TT) == 0:
                        tt = u // (n // TT)
                        act.wait_ge(ns_pv, u + 1)
                        store_y("mix1", tt, bank=6)
                out_product("mix1", out)

            for layer in layers:
                if layer[:3] == "mlp":
                    hidden_layer(layer, 4)
                elif layer[:3] == "ffn":
                    hidden_layer(layer, 2)
                elif layer[:3] == "fin":
                    square_sums(layer)
                elif layer == "mix0":
                    delta_rule()
                elif layer == "mix1":
                    sparse_attention()
                elif layer == "sgu":
                    spatial_gating()
                elif layer == "kv":
                    in_product("kv", prod["kv"], None, copy_block(prod["kv"], lambda tt, b: kv_tm[:, tt, :], kv_in))
                elif layer == "sb":
                    stick_breaking()

        @block.vector
        def _(dve):
            def split(q, b, bs, i, j):
                static = q.panel + q.per * bs + j
                panel = q.panel + q.per * b + j
                half = min(PK, q.kt - PK * j) // 2 * NB
                for s in range(2):
                    part = slice(s * half, (s + 1) * half)
                    dve.wait_ge(hi_ready, 2 * panel + s + 1)
                    dve.tensor_tensor(w_lo[:, static % 2, part], raw[:, static % RING, part],
                                      w_hi[:, static % 2, part].bitcast(F32), ALU.subtract).then_inc(lo_ready, 1)

            def norm_store(layer, half):
                t0 = at[layer][0]
                n = NORMS.index(layer)
                batch = 2 * normed.index(layer) + half
                for f in range(4):
                    k = 4 * half + f
                    if f == 0:
                        dve.wait_ge(norm_hi, batch + 1)
                    if f == 2:
                        dve.wait_ge(t_hi, t0 + half + 1)
                    done = dve.scalar_tensor_tensor(h_lo[:, k, :], tps[:, f, :], norm_t[:, n, k:k + 1],
                                                    h_hi[:, k, :].bitcast(F32), ALU.mult, ALU.subtract)
                done.then_inc(t_lo, 1)

            pending = []

            def residual():
                if not pending:
                    return
                q, b, scale = pending.pop()
                dve.wait_ge(w_used, q.panel + q.per * (b + 1))
                bank = acc[(q.block + b) % 2]
                for tt in range(TT):
                    cols = x_sb[:, tt, b * NB:(b + 1) * NB]
                    dve.scalar_tensor_tensor(cols, bank[tt], scale, cols, ALU.mult, ALU.add).then_inc(x_ready, 1)

            def enter(layer, q):
                if at[layer][1] == 0:
                    dve.wait_ge(params_loaded, 32)
                    norm_store(layer, 0)
                split(q, 0, 0, 0, 0)
                residual()
                if layer not in early and at[layer][1]:
                    norm_store(layer, 0)
                if at[layer][1]:
                    split(q, 0, 0, 0, 1)
                norm_store(layer, 1)
                if not at[layer][1]:
                    split(q, 0, 0, 0, 1)
                if layer == "kv" and early_norm(layer):
                    norm_store(early_norm(layer), 0)
                if at[layer][1] == 0:
                    dve.wait_ge(const_loaded, 16)

            def hidden_layer(layer, f_count, scale):
                up, down = prod[layer + "_up"], prod[layer + "_down"]
                t0 = at[layer][0] + 2
                h0 = hidden_before[layer]

                def evacuate(b, bs):
                    bank = acc[(up.block + bs) % 2]
                    if f_count == 4:
                        dve.wait_ge(act_tm, 2 * (h0 + b + 1))
                        dve.tensor_tensor(tm[:, :, :], tm[:, :, :], tm[:, :, :], ALU.mult).then_inc(tm_ready, 1)
                        return
                    if b is not None:
                        dve.wait_ge(act_tm, 2 * (h0 + b + 1))
                    for tt in range(TT):
                        gate = tm[:, tt, 0:256]
                        done = dve.scalar_tensor_tensor(gate, bank[tt][:, 256:512], rstd[:, tt:tt + 1], gate,
                                                        ALU.mult, ALU.mult)
                    done.then_inc(tm_ready, 1)

                def store_t(b):
                    dve.wait_ge(t_hi, t0 + b + 1)
                    cols = bass.ds(b * (f_count * T), f_count * T)
                    dve.tensor_tensor(hid_lo2[:, cols], tps[:, 0:f_count, :].rearrange("p f t -> p (f t)"),
                                      hid_hi2[:, cols].bitcast(F32), ALU.subtract).then_inc(t_lo, 1)

                enter(layer, up)

                def body(b, bs, i):
                    split(up, b, bs, i, 0)
                    split(up, b, bs, i, 1)
                    evacuate(b - 1, bs - 1)
                    store_t(b - 1)

                body(1, 1, 0)
                pairs, rest = steps(2, up.blocks)
                with dve.Fori(0, pairs) as i:
                    for k in range(2):
                        body(2 + 2 * i + k, 2 + k, i)
                for b in range(rest, up.blocks):
                    body(b, b, 0)
                for b in range(down.blocks):
                    for j in range(down.per):
                        if b == 0 and j == 2:
                            evacuate(up.blocks - 1, up.blocks - 1)
                            store_t(up.blocks - 1)
                        if b == 1 and j == 2:
                            residual()
                        if b == 1 and j == 4 and early_norm(layer):
                            norm_store(early_norm(layer), 0)
                        split(down, b, b, 0, j)
                    pending.append((down, b, scale))

            def final_norm(layer):
                _, x0, r0 = at[layer]
                residual()
                dve.wait_ge(rstd_ready, r0 + 1)
                dve.wait_ge(row_loaded if layer == "fin1" or "fin1" not in layers else row2_loaded, 16)
                for half in range(2):
                    for tt in range(TT):
                        cols = slice(half * NB, (half + 1) * NB)
                        done = dve.scalar_tensor_tensor(x_sb[:, tt, cols], x_sb[:, tt, cols], rstd[:, tt:tt + 1], row[:, cols],
                                                        ALU.mult, ALU.mult)
                    done.then_inc(x_ready, 1)

            def in_product(layer, q, out, between={}):
                enter(layer, q)
                for b in range(1, q.blocks):
                    for j in range(q.per):
                        split(q, b, b, 0, j)
                        if j == 0 and b - 0.5 in between:
                            between[b - 0.5]()
                    if b in between:
                        between[b]()
                if out:
                    split(out, 0, 0, 0, 0)
                    split(out, 0, 0, 0, 1)

            def out_product(layer, q, wait_first=2):
                for b in range(q.blocks):
                    for j in range(q.per):
                        if b == 1 and j == 1:
                            residual()
                        if layer == "sgu" and b == 1 and j == 3 and early_norm(layer):
                            norm_store(early_norm(layer), 0)
                        if b or j >= wait_first:
                            split(q, b, b, 0, j)
                    pending.append((q, b, 1.0))
                if layer != "sgu" and early_norm(layer):
                    norm_store(early_norm(layer), 0)

            def store_y(layer, tt, tiles=8, bank=4):
                for k in range(tiles // 4):
                    dve.wait_ge(y_hi, y_banks(layer, tt) + k + 1)
                    cols = (slice(None), slice(4 * k, 4 * k + 4), slice(tt * P, (tt + 1) * P))
                    dve.tensor_tensor(h_lo[cols], ps[:, bank + k, :].rearrange("p (f t) -> p f t", t=P),
                                      h_hi[cols].bitcast(F32), ALU.subtract).then_inc(y_lo, 1)

            def spatial_gating():
                q, out = prod["sgu_in"], prod["sgu_out"]
                t0 = at["sgu"][0] + 2
                enter("sgu", q)
                for b in range(1, q.blocks):
                    for j in range(q.per):
                        if (b, j) != (7, 0):
                            split(q, b, b, 0, j)
                    if b == 4:
                        dve.wait_ge(sgu_in, TT * 4)
                        dve.tensor_reduce(v_stat[:, 1, :], v_sums[:, :, :], AXX, ALU.add).then_inc(sgu_mean, 1)
                        dve.wait_ge(sgu_mean, 1)
                        dve.tensor_scalar(v_stat[:, 0, :], v_stat[:, 1, :], -1.0 / (2 * D), None,
                                          ALU.mult).then_inc(sgu_mean, 1)
                    if b == 6:
                        dve.wait_ge(sgu_rs, 3)
                        dve.wait_ge(sgu_params, 64)
                        for tt in range(TT):
                            v = sgu_z[:, tt, 0:2 * D]
                            dve.tensor_scalar(v, v, v_stat[:, 0, tt:tt + 1], v_stat[:, 2, tt:tt + 1], ALU.add,
                                              ALU.mult).then_inc(sgu_v, 1)
                            dve.wait_ge(sgu_v, 3 * tt + 1)
                            dve.tensor_tensor(v, v, ln_rows[:, 0, :], ALU.mult).then_inc(sgu_v, 1)
                            dve.wait_ge(sgu_v, 3 * tt + 2)
                            dve.tensor_tensor(v, v, ln_rows[:, 1, :], ALU.add).then_inc(sgu_v, 1)
                            if tt == 0:
                                split(q, 7, 7, 0, 0)

                def gate(pair):
                    dve.wait_ge(sgu_in, TT * (5 + pair))
                    for tt in range(TT):
                        dve.wait_ge(sgu_mix, TT * pair + tt + 1)
                        for g in range(2):
                            u = sgu_z[:, tt, 2 * D + (2 * pair + g) * 256:2 * D + (2 * pair + g + 1) * 256]
                            done = dve.scalar_tensor_tensor(u, ps[:, 6 + tt, g * 256:(g + 1) * 256],
                                                            bs_t[:, 2 * pair + g:2 * pair + g + 1], u, ALU.add, ALU.mult)
                        done.then_inc(sgu_s, 1)

                def store(j):
                    dve.wait_ge(t_hi, t0 + j + 1)
                    dve.tensor_tensor(sgu_lo[:, 4 * j:4 * (j + 1), :], tps, hid_hi[:, 4 * j:4 * (j + 1), :].bitcast(F32),
                                      ALU.subtract).then_inc(t_lo, 1)

                gate(0)
                split(out, 0, 0, 0, 0)
                gate(1)
                store(0)
                split(out, 0, 0, 0, 1)
                gate(2)
                store(1)
                split(out, 0, 0, 0, 2)
                gate(3)
                store(2)
                split(out, 0, 0, 0, 3)
                store(3)
                out_product("sgu", out, wait_first=4)

            def stick_breaking():
                q, out = prod["sb_q"], prod["sb_out"]
                in_product("sb", q, out)
                n = len(sb_units)

                def masked_scores(u):
                    g, qt, kt = sb_units[u]
                    z, soft = sb_s[:, u % 8, 0, :, :], sb_s[:, u % 8, 1, :, :]
                    dve.wait_ge(sb_z, u + 1)
                    if u >= 8:
                        dve.wait_ge(sb_av, u - 7)
                    src = ps[:, 2 * (u % 2):2 * (u % 2) + 2, 0:256]
                    if kt == qt:
                        for par in range(2):
                            done = dve.scalar_tensor_tensor(
                                z[:, par, :].rearrange("p (h t) -> p h t", t=P), src[:, par, :].rearrange("p (h t) -> p h t", t=P), 0.125,
                                cst("not_earlier").unsqueeze(1).broadcast_to([P, 2, P]), ALU.mult, ALU.add)
                    else:
                        done = dve.tensor_scalar(z, src, 0.125, None, ALU.mult)
                    done.then_inc(sb_zm, 1)
                    dve.wait_ge(sb_zm, u + 1)
                    dve.scalar_tensor_tensor(soft, z, -1.0, z, ALU.mult, ALU.max).then_inc(sb_abs, 1)

                def softplus(u):
                    z = sb_s[:, u % 8, 0, :, :].rearrange("p a b -> p (a b)")
                    soft = sb_s[:, u % 8, 1, :, :].rearrange("p a b -> p (a b)")
                    dve.wait_ge(sb_ln, u + 1)
                    dve.scalar_tensor_tensor(soft, z, 0.0, soft, ALU.max, ALU.add).then_inc(sb_sp, 1)

                def log_weights(u):
                    z = sb_s[:, u % 8, 0, :, :].rearrange("p a b -> p (a b)")
                    dve.wait_ge(sb_rev, u + 1)
                    dve.tensor_tensor(z, z, ps[:, 4 + u % 2, :], ALU.subtract).then_inc(sb_arg, 1)

                for u in range(4):
                    masked_scores(u)
                for p in range(n // 2):
                    pair = (2 * p, 2 * p + 1)
                    for u in pair:
                        softplus(u)
                    for u in pair:
                        log_weights(u)
                    if p == 3:
                        store_y("sb", 0, bank=6)
                    for u in pair:
                        if u + 4 < n:
                            masked_scores(u + 4)
                store_y("sb", 1, bank=6)
                out_product("sb", out)

            taken = [0]

            def step(ins):
                taken[0] += 1
                ins.then_inc(dve_step, 1)
                dve.wait_ge(dve_step, taken[0])

            def each_head(ap):
                return ap.rearrange("p (h d) -> p h d", d=64)

            def of_heads(ap):
                return ap.unsqueeze(2).broadcast_to([P, 8, 64])

            def delta_rule():
                q, out = prod["ev_in"], prod["ev_out"]

                def convolve(n):
                    dve.wait_ge(gd_ts, n + 1)
                    if n == 0:
                        dve.wait_ge(gd_params, 16 * 6)
                        dve.wait_ge(gd_pad, 2)
                    for tap in range(4):
                        for f in range(4 * n, 4 * n + 4):
                            src, dst, w = gd_x[:, f, tap:tap + T], gd_c[:, f, :], gd_cw[:, f, tap:tap + 1]
                            if tap == 0:
                                done = dve.tensor_scalar(dst, src, w, None, ALU.mult)
                            else:
                                done = dve.scalar_tensor_tensor(dst, src, w, dst, ALU.mult, ALU.add)
                        if tap < 3:
                            step(done)
                    done.then_inc(gd_cv, 1)

                def gates():
                    dve.wait_ge(gd_abp, 1)
                    dve.wait_ge(rstd_ready, at["mix0"][2] + 1)
                    for tt in range(TT):
                        r = rstd[:, tt:tt + 1]
                        dve.scalar_tensor_tensor(gd_g[:, 0, tt, :], ps[:, 6, tt * 16:tt * 16 + 8], r, gd_dt_bias[:, :],
                                                 ALU.mult, ALU.add)
                        done = dve.tensor_scalar(gd_g[:, 1, tt, :], ps[:, 6, tt * 16 + 8:tt * 16 + 16], r, None, ALU.mult)
                    step(done)
                    dve.scalar_tensor_tensor(gd_g[:, 2, :, :], gd_g[:, 0, :, :], -1.0, gd_g[:, 0, :, :],
                                             ALU.mult, ALU.max).then_inc(gd_ga, 1)

                def gates_end():
                    dve.wait_ge(gd_ge, 4)
                    step(dve.scalar_tensor_tensor(gd_g[:, 4, :, :], gd_g[:, 0, :, :], 0.0, gd_g[:, 4, :, :], ALU.max, ALU.add))
                    for tt in range(TT):
                        dve.scalar_tensor_tensor(gd_g[:, 5, tt, :], gd_g[:, 4, tt, :], -1.0, gd_a_log[:, :], ALU.mult, ALU.mult)
                    step(dve.tensor_scalar(gd_g[:, 3, :, :], gd_g[:, 3, :, :], 1.0, None, ALU.add))
                    dve.reciprocal(gd_g[:, 6, :, :], gd_g[:, 3, :, :]).then_inc(gd_gg, 1)

                def sums():
                    dve.wait_ge(gd_gp, 1)
                    step(dve.tensor_copy(gd_sum[:, :, :, :], ps[:, 7, 0:64].rearrange("p (n t h) -> p n t h", n=4, t=TT)))
                    dve.tensor_tensor(gd_sum[:, 1, :, :], gd_sum[:, 1, :, :], gd_sum[:, 0, :, :], ALU.subtract).then_inc(gd_gs, 1)

                def between(b):
                    if b == 3:
                        gates()
                    if b == 5:
                        gates_end()
                    if 2 <= b <= 4:
                        convolve(b - 2)
                    if b == 1:
                        dve.wait_ge(gd_split, 1)
                        dve.tensor_tensor(gd_wab_lo[:, :], gd_wab[:, :], gd_wab_hi[:, :].bitcast(F32),
                                          ALU.subtract).then_inc(gd_split, 1)
                    if b == 5:
                        dve.wait_ge(gd_tp, 5)
                        dve.tensor_tensor(gd_ch[:, :, 2:], gd_ch[:, :, 2:], tps, ALU.mult).then_inc(gd_ts, 1)
                    if b == 6:
                        dve.wait_ge(gd_ts, 5)
                        for tap in range(3):
                            for f in range(4):
                                src, dst, w = gd_ch[:, f, tap:tap + T], gd_sc[:, f, :], gd_scw[:, f, tap:tap + 1]
                                if tap == 0:
                                    done = dve.tensor_scalar(dst, src, w, None, ALU.mult)
                                else:
                                    done = dve.scalar_tensor_tensor(dst, src, w, dst, ALU.mult, ALU.add)
                            step(done)

                in_product("mix0", q, out, {b: (lambda b=b: between(b)) for b in range(1, 7)})
                dve.wait_ge(gd_ts, 6)
                dve.tensor_tensor(gd_sc[:, :, :], gd_sc[:, :, :], gd_b[:, :, :], ALU.mult).then_inc(gd_yb, 1)
                sums()
                dve.wait_ge(gd_gx, 1)
                dve.wait_ge(gd_gg, 1)
                dve.tensor_tensor(gd_g[:, 7, :, :], gd_g[:, 6, :, :], gd_exp[:, 0, :, :], ALU.mult)
                for par in range(2):
                    rows = slice(64 * par, 64 * par + 64)
                    dve.tensor_copy(gd_dec[rows, :, :, :].rearrange("p c t h -> p (c t) h"),
                                    gd_exp[rows, 2:4, :, :].rearrange("p c t (h r) -> p r (c t) h", r=2)[:, par])
                for c, name in enumerate(("even", "odd")):
                    done = dve.tensor_scalar(gd_ez[:, c, :, :], gd_exp[:, 1, :, :], cst(name)[:, 0:1], None, ALU.mult)
                done.then_inc(gd_gt, 1)
                dve.wait_ge(gd_ybh, 1)
                dve.tensor_tensor(h_lo[:, 4:8, :], gd_sc[:, :, :], h_hi[:, 4:8, :].bitcast(F32), ALU.subtract).then_inc(gd_ybl, 1)
                dve.wait_ge(gd_gt, 1)

                def norm_outputs(tt):
                    dve.wait_ge(gd_on, tt + 1)
                    step(dve.tensor_tensor(each_head(gd_o[:, :]), each_head(gd_o[:, :]), of_heads(gd_ro[:, 0, :]), ALU.mult))
                    dve.wait_ge(gd_zn, 2)
                    dve.tensor_tensor(gd_o[:, :], gd_o[:, :], gd_z[:, tt, :], ALU.mult).then_inc(y_tm, 1)

                for tt in range(TT):
                    one = 1 + tt
                    dve.wait_ge(gd_qq, 2 * one)
                    dve.tensor_reduce(gd_rs[:, 0, :, :], gd_sq[:, :, :].rearrange("p n (h d) -> p n h d", d=64), AXX,
                                      ALU.add).then_inc(gd_qs, 1)
                    for par in range(2):
                        dve.wait_ge(gd_bc, 2 * tt + par + 1)
                        for pair in range(4):
                            h = 2 * pair + par
                            done = dve.scalar_tensor_tensor(gd_dt[:, 4 * par + pair, :], ps[:, 6 + par, pair * P:(pair + 1) * P],
                                                            gd_sum[:, 0, tt, h:h + 1], cst("not_later"), ALU.subtract, ALU.add)
                        done.then_inc(gd_da, 1)
                    beta, eg = of_heads(gd_g[:, 6, tt, :]), of_heads(gd_exp[:, 0, tt, :])
                    dve.wait_ge(gd_qr, one)
                    k, kb, qn, qe, vb = [each_head(gd_tm[:, n, :]) for n in range(5)]
                    dve.wait_ge(gd_q, 3 * one)
                    dve.tensor_tensor(k, each_head(ps[:, 1, :]), of_heads(gd_rs[:, 2, 1, :]), ALU.mult).then_inc(gd_kn, 1)
                    dve.wait_ge(gd_kn, 5 * tt + 1)
                    dve.tensor_tensor(kb, k, beta, ALU.mult).then_inc(gd_kn, 1)
                    dve.scalar_tensor_tensor(qn, each_head(ps[:, 0, :]), 0.125, of_heads(gd_rs[:, 2, 0, :]), ALU.mult,
                                             ALU.mult).then_inc(gd_kn, 1)
                    dve.wait_ge(gd_kn, 5 * tt + 3)
                    dve.tensor_tensor(qe, qn, eg, ALU.mult).then_inc(gd_kn, 1)
                    dve.tensor_tensor(vb, each_head(ps[:, 2, :]), beta, ALU.mult).then_inc(gd_kn, 1)
                    if tt:
                        norm_outputs(0)
                    for n, bank in ((1, 4), (3, 0)):
                        dve.wait_ge(gd_ft, 4 * tt + n + 1)
                        dve.tensor_copy(gd_t[:, n, :, :].rearrange("p f t -> p (f t)"), ps[:, bank, :]).then_inc(gd_fv, 1)

                    def units(ap, par):
                        return ap[:, 4 * par:4 * par + 4, :]

                    def bank4(b):
                        return ps[:, b, :].rearrange("p (u t) -> p u t", t=P)

                    level1 = cst("level1").unsqueeze(1).broadcast_to([P, 4, P])
                    eye = ident.unsqueeze(1).broadcast_to([P, 4, P])
                    dve.wait_ge(gd_de, 2 * one)
                    for par in range(2):
                        dve.wait_ge(gd_kk, 4 * tt + par + 1)
                        dve.tensor_tensor(units(gd_mt, par), bank4(1 + par), units(gd_dt, par), ALU.mult).then_inc(gd_m, 1)
                    for par in range(2):
                        dve.wait_ge(gd_m, 2 * tt + par + 1)
                        step(dve.tensor_tensor(units(gd_invt, par), units(gd_mt, par), level1, ALU.mult))
                        dve.tensor_tensor(units(gd_invt, par), eye, units(gd_invt, par), ALU.subtract).then_inc(gd_x1, 1)
                    for par in range(2):
                        dve.wait_ge(gd_kk, 4 * tt + par + 3)
                        dve.tensor_tensor(units(gd_at, par), bank4(3 + par), units(gd_dt, par), ALU.mult).then_inc(gd_a, 1)
                    if tt:
                        store_y("mix0", 0, tiles=4, bank=5)
                    for level in range(2, 7):
                        for par in range(2):
                            n = 10 * tt + 2 * (level - 2) + par
                            dve.wait_ge(gd_qp, n + 1)
                            if level < 6:
                                dve.tensor_tensor(units(gd_inv, par), units(gd_inv, par), bank4(2 + par), ALU.subtract)
                            dve.tensor_tensor(units(gd_invt, par), units(gd_invt, par), bank4(4 + par),
                                              ALU.subtract).then_inc(gd_iv, 1)
                    dve.wait_ge(gd_up, 2 * one)
                    dve.tensor_copy(gd_wt[:, :, :].rearrange("p f t -> p (f t)"), ps[:, 1, :]).then_inc(gd_ws, 1)
                    dve.wait_ge(gd_us, one)
                    for c in range(2):
                        n = 2 * tt + c
                        rows = slice(64 * c, 64 * c + 64)
                        dve.wait_ge(gd_sp, 2 * n + 1)
                        if n == 0:
                            dve.wait_ge(gd_z0, 2)
                        dve.tensor_tensor(gd_vn[rows, :], gd_u[rows, :], ps[rows, 2, :], ALU.subtract).then_inc(gd_vs, 1)
                        dve.wait_ge(gd_sp, 2 * n + 2)
                        step(dve.tensor_tensor(gd_s[:, :, :], gd_s[:, :, :],
                                               gd_dec[:, c, tt, :].unsqueeze(2).broadcast_to([P, 4, P]), ALU.mult))
                        dve.wait_ge(gd_dp, n + 1)
                        for par in range(2):
                            r, cols = slice(64 * par, 64 * par + 64), slice(64 * par, 64 * par + 64)
                            done = dve.tensor_tensor(gd_s[r, :, cols], gd_s[r, :, cols], bank4(4)[r, :, cols], ALU.add)
                        done.then_inc(gd_st, 1)
                    dve.wait_ge(gd_op, one)
                    dve.wait_ge(gd_os, 2 * one)
                    dve.tensor_tensor(gd_o[:, :], gd_o[:, :], ps[:, 5, :], ALU.add).then_inc(gd_of, 1)
                    dve.wait_ge(gd_oq, one)
                    dve.tensor_reduce(gd_ro[:, 0, :], each_head(gd_osq[:, :]), AXX, ALU.add).then_inc(gd_or, 1)
                norm_outputs(1)
                store_y("mix0", 1, tiles=4, bank=5)
                out_product("mix0", out)

            def sparse_attention():
                q, out = prod["od_in"], prod["od_out"]

                def split_gate_weights():
                    dve.wait_ge(ns_split, 1)
                    dve.tensor_tensor(ns_wg_lo[:, :], ns_wg[:, :], ns_wg_hi[:, :].bitcast(F32),
                                      ALU.subtract).then_inc(ns_split, 1)

                def compression_input(kv):
                    dve.wait_ge(ns_params, 16 * 5)
                    dve.memset(ns_xp[:, kv, :, :, :].rearrange("p h u (g n) -> p (h u g) n", n=16)[:, :, 15:16],
                               0.0).then_inc(ns_x, 1)
                    dve.wait_ge(ns_cvt, kv + 1)
                    src = two[4 + 2 * kv].rearrange("p b n -> p (b n)").rearrange("p (g t) -> p g t", t=T)
                    for half in range(2):
                        for par in range(2):
                            rows = slice(64 * par, 64 * par + 64)
                            taps = src[rows, :, 16 * half + par:16 * half + par + 239:2]
                            taps = taps.rearrange("p g (n u) -> p g n u", u=8)
                            pos = ns_pos[rows, half, :].unsqueeze(1).unsqueeze(1).broadcast_to([64, 4, 15, 8])
                            dst = ns_xp[rows, kv, half, :, :].rearrange("p u (g n) -> p g n u", n=16)[:, :, 0:15, :]
                            dve.tensor_tensor(dst, taps, pos, ALU.add).then_inc(ns_x, 1)

                def store_compressed():
                    step(dve.memset(ns_kct[:, :, :, :].rearrange("p g r n -> p (g r n)"), 0.0))
                    dve.wait_ge(ns_kvp, 1)
                    for par in range(2):
                        rows = slice(64 * par, 64 * par + 64)
                        done = dve.tensor_copy(ns_kct[rows, :, par, :], ps[rows, 6, 0:64].rearrange("p (g n) -> p g n", n=16))
                    done.then_inc(ns_kvs, 1)
                    a = CONST_AT["group"][0]
                    for g in range(4):
                        done = dve.tensor_scalar(ns_vc[:, g, :], ps[0:64, 5, 0:64], const[0:64, a + g:a + g + 1], None, ALU.mult)
                    done.then_inc(ns_kvs, 2)

                def rotate_queries():
                    dve.wait_ge(ns_qtp, 4)
                    heads = ns_tm[:, :, NS_COL["q"]:NS_COL["q"] + D].rearrange("p t (h d) -> p t h d", d=64)
                    x1, x2 = heads[:, :, :, 0:8], heads[:, :, :, 8:16]
                    cos, sin = [cst(n).rearrange("p (t f) -> p t f", f=8).unsqueeze(2).broadcast_to([P, TT, 16, 8])
                                for n in ("cos", "sin")]
                    for n, (a, b) in enumerate([(x1, cos), (x2, sin), (x2, cos), (x1, sin)]):
                        for tt in range(TT):
                            done = dve.tensor_tensor(ns_rot[:, n, tt], a[:, tt], b[:, tt], ALU.mult)
                        done.then_inc(ns_rope, 1)
                    dve.wait_ge(ns_rope, 4)
                    for tt in range(TT):
                        dve.tensor_tensor(x1[:, tt], ns_rot[:, 0, tt], ns_rot[:, 1, tt], ALU.subtract)
                        done = dve.tensor_tensor(x2[:, tt], ns_rot[:, 2, tt], ns_rot[:, 3, tt], ALU.add)
                        done.then_inc(ns_rope, 1)

                c = ns_c[:, :, :].rearrange("p t (h n) -> p (t h) n", n=16)
                stat = ns_cst[:, 0:4, :]

                def compressed_maxima():
                    dve.wait_ge(ns_cs, 1)
                    for tt in range(TT):
                        add = cst("cmp_add")[:, 16 * tt:16 * tt + 16]
                        src = ps[:, 4, tt * 256:(tt + 1) * 256].rearrange("p (g j n) -> p g j n", g=4, j=4)
                        dst = ns_c[:, tt, :].rearrange("p (j g n) -> p g j n", j=4, g=4)
                        dve.tensor_tensor(dst, src, add.unsqueeze(1).unsqueeze(1).broadcast_to([P, 4, 4, 16]),
                                          ALU.add).then_inc(ns_cd, 2)
                    dve.wait_ge(ns_cd, 4)
                    dve.tensor_reduce(stat[:, 0, :], c, AXX, ALU.max).then_inc(ns_cd, 1)
                    dve.wait_ge(ns_cd, 5)
                    dve.tensor_tensor(c, c, stat[:, 0, :].unsqueeze(2).broadcast_to([P, 32, 16]), ALU.subtract).then_inc(ns_cd, 1)

                in_product("mix1", q, out, {1: lambda: compression_input(0), 1.5: lambda: compression_input(1),
                                            2: split_gate_weights, 3: store_compressed,
                                            4: lambda: (rotate_queries(), compressed_maxima())})
                n = len(ns_units)

                def maxima(u):
                    tt, br, g = ns_units[u]
                    keys = (tt + 1) * P
                    wide = cst("causal_wide")[:, 2 * P - keys:2 * P]
                    st = ns_st[:, u % 3]
                    dve.wait_ge(ns_s, u + 1)
                    if u >= 3:
                        dve.wait_ge(ns_tp, u - 2)
                    for j in range(4):
                        dve.tensor_tensor_reduce(out=ns_p[:, u % 3, j, 0:keys],
                                                 in0=ps[:, 2 * (u % 2) + j % 2, j // 2 * keys:(j // 2 + 1) * keys],
                                                 in1=wide, scale=1.0, scalar=-3.0e38, op0=ALU.add, op1=ALU.max,
                                                 accum_out=st[:, 0, j:j + 1]).then_inc(ns_m, 1)
                    dve.wait_ge(ns_m, 4 * u + 4)
                    dve.tensor_scalar(st[:, 1, 0:4], st[:, 0, 0:4], -0.125, None, ALU.mult).then_inc(ns_nm, 1)

                def weigh(u):
                    tt, br, g = ns_units[u]
                    keys = (tt + 1) * P
                    st = ns_st[:, u % 3]
                    dve.wait_ge(ns_e, 4 * u + 4)
                    dve.reciprocal(st[:, 3, 0:4], st[:, 2, 0:4]).then_inc(ns_d, 1)
                    dve.wait_ge(ns_d, 2 * u + 1)
                    dve.tensor_tensor(st[:, 3, 4:8], st[:, 3, 0:4],
                                      ns_gate[:, tt, 12 * g + 1 + br:12 * g + 11 + br:3], ALU.mult).then_inc(ns_d, 1)
                    dve.wait_ge(ns_d, 2 * u + 2)
                    rows = ns_p[:, u % 3, :, 0:keys]
                    dve.tensor_tensor(rows, rows, st[:, 3, 4:8].unsqueeze(2).broadcast_to([P, 4, keys]),
                                      ALU.mult).then_inc(ns_w, 1)

                dve.wait_ge(ns_ce, 1)
                for tt in range(TT):
                    row_c = ns_c[:, tt, :].rearrange("p (h n) -> p h n", n=16)
                    dve.tensor_tensor(row_c, row_c, cst("cmp_mul")[:, 16 * tt:16 * tt + 16].unsqueeze(1).broadcast_to([P, 16, 16]),
                                      ALU.mult).then_inc(ns_cd, 1)
                dve.wait_ge(ns_cd, 8)
                dve.tensor_reduce(stat[:, 1, :], c, AXX, ALU.add).then_inc(ns_cd, 1)
                dve.wait_ge(ns_cd, 9)
                dve.tensor_scalar(stat[:, 1, :], stat[:, 1, :], 1.0, None, ALU.max).then_inc(ns_cd, 1)
                dve.wait_ge(ns_cd, 10)
                dve.reciprocal(stat[:, 2, :], stat[:, 1, :]).then_inc(ns_cd, 1)
                dve.wait_ge(ns_gs, 1)
                dve.wait_ge(ns_cd, 11)
                for tt in range(TT):
                    cols = slice(16 * tt, 16 * tt + 16)
                    gate = ns_gate[:, tt, :].rearrange("p (g j b) -> p j g b", g=4, j=4)[:, :, :, 0]
                    dve.tensor_tensor(stat[:, 3, cols].rearrange("p (j g) -> p j g", g=4),
                                      stat[:, 2, cols].rearrange("p (j g) -> p j g", g=4), gate, ALU.mult).then_inc(ns_cg, 1)
                dve.wait_ge(ns_cg, 2)
                dve.tensor_tensor(c, c, stat[:, 3, :].unsqueeze(2).broadcast_to([P, 32, 16]), ALU.mult).then_inc(ns_cd, 1)
                maxima(0)
                maxima(1)
                for u in range(n):
                    weigh(u)
                    if u == n // TT:
                        store_y("mix1", 0, bank=6)
                    if u + 2 < n:
                        maxima(u + 2)
                store_y("mix1", 1, bank=6)
                out_product("mix1", out)

            for layer in layers:
                if layer == "sgu":
                    spatial_gating()
                elif layer == "mix0":
                    delta_rule()
                elif layer == "mix1":
                    sparse_attention()
                elif layer == "kv":
                    in_product("kv", prod["kv"], None)
                elif layer == "sb":
                    stick_breaking()
                elif layer[:3] == "mlp":
                    hidden_layer(layer, 4, 1.0)
                elif layer[:3] == "ffn":
                    hidden_layer(layer, 2, 0.5)
                elif layer[:3] == "fin":
                    final_norm(layer)
            residual()

        @block.gpsimd
        def _(pool):
            pool.wait_ge(params_loaded, 32)

            def inverse_rms(layer):
                r0 = at[layer][2]
                pool.wait_ge(ss_ready, TT * (r0 + 1))
                pool.tensor_scalar(ms[:, :], ss[:, :], 1.0 / D, EPS, ALU.mult, ALU.add).then_inc(ms_ready, 1)
                pool.wait_ge(ms_ready, r0 + 1)
                pool.tensor_tensor(rstd[:, :], ms[:, :], cst("neg_half")[:, 0:TT], ALU.pow).then_inc(rstd_ready, 1)
                if at[layer][1] == 0:
                    pool.wait_ge(const_loaded, 16)

            def spatial_gating():
                pool.wait_ge(x_ready, at["sgu"][1])
                pool.dma_start(ws_raw[:, :, :], dram["ws_t"]).then_inc(sgu_params, 16)
                pool.dma_start(bs_t[:, :], dram["bs_t"]).then_inc(sgu_params, 16)
                for k in range(2):
                    pool.dma_start(ln_rows[:, k, :], dram["ln_rows"][k:k + 1, :].partition_broadcast(P)).then_inc(sgu_params, 16)
                pool.wait_ge(sgu_params, 64)
                pool.tensor_tensor(ws_t[:, :, :], ws_raw[:, :, :], cst("upto").unsqueeze(1).broadcast_to([P, 8, P]),
                                   ALU.mult).then_inc(sgu_ws, 1)
                pool.wait_ge(sgu_sq, 4)
                pool.tensor_tensor(v_stat[:, 2, :], v_sq[:, :, 0], v_sq[:, :, 1], ALU.add).then_inc(sgu_rs, 1)
                pool.wait_ge(sgu_rs, 1)
                pool.tensor_scalar(v_stat[:, 1, :], v_stat[:, 2, :], 1.0 / (2 * D), LN_EPS, ALU.mult,
                                   ALU.add).then_inc(sgu_rs, 1)
                pool.wait_ge(sgu_rs, 2)
                pool.tensor_tensor(v_stat[:, 2, :], v_stat[:, 1, :], cst("neg_half")[:, 0:TT], ALU.pow).then_inc(sgu_rs, 1)

            taken = [0]

            def step(ins):
                taken[0] += 1
                ins.then_inc(pool_step, 1)
                pool.wait_ge(pool_step, taken[0])

            def delta_rule():
                for dst, name in ((gd_wab[:, :], "gd_wab"), (gd_cw[:, :, :], "gd_cw"), (gd_scw[:, :, :], "gd_scw")):
                    pool.dma_start(dst, dram[name]).then_inc(gd_params, 16)
                for dst, name in ((gd_dt_bias, "gd_dt_bias"), (gd_a_log, "gd_a_log"), (gd_onorm, "gd_onorm")):
                    pool.dma_start(dst[:, :], dram[name].partition_broadcast(P)).then_inc(gd_params, 16)
                pool.memset(gd_x[:, :, 0:3], 0.0).then_inc(gd_pad, 1)
                pool.memset(gd_ch[:, :, 0:2], 0.0).then_inc(gd_pad, 1)
                inverse_rms("mix0")
                pool.wait_ge(gd_params, 16 * 6)
                pool.wait_ge(gd_cv, 3)
                pool.memset(gd_s[:, :, :], 0.0).then_inc(gd_z0, 1)
                pool.memset(gd_vn[:, :], 0.0).then_inc(gd_z0, 1)

                def spread_g(tt):
                    pool.wait_ge(gd_gg, 1)
                    if tt:
                        pool.wait_ge(gd_qp, 10 * tt)
                    pool.tensor_copy(gd_gb[:, :, :], gd_g[:, 5, tt, :].unsqueeze(2).broadcast_to([P, 8, P])).then_inc(gd_gbr, 1)

                spread_g(0)
                for tt in range(TT):
                    one = 1 + tt
                    pool.wait_ge(gd_qs, one)
                    step(pool.tensor_scalar(gd_rs[:, 1, :, :], gd_rs[:, 0, :, :], 1.0, EPS, ALU.mult, ALU.add))
                    half = cst("neg_half").rearrange("p (n h) -> p n h", h=8)
                    pool.tensor_tensor(gd_rs[:, 2, :, :], gd_rs[:, 1, :, :], half, ALU.pow).then_inc(gd_qr, 1)
                    pool.wait_ge(gd_kn, 5 * tt + 1)
                    pool.wait_ge(gd_gt, 1)
                    k = gd_tm[:, 0, :].rearrange("p (h d) -> p h d", d=64)
                    for n, f in ((5, gd_g[:, 7, tt, :]), (6, gd_ez[:, 0, tt, :]), (7, gd_ez[:, 1, tt, :])):
                        pool.tensor_tensor(gd_tm[:, n, :].rearrange("p (h d) -> p h d", d=64), k,
                                           f.unsqueeze(2).broadcast_to([P, 8, 64]), ALU.mult).then_inc(gd_kz, 1)
                    pool.wait_ge(gd_m, 2 * one)
                    for level in range(2, 7):
                        if level >= 4:
                            pool.wait_ge(gd_pp, 10 * tt + 2 * (level - 3))
                        pool.tensor_tensor(gd_ml[:, level % 2, :, :], gd_mt[:, :, :],
                                           cst(f"level{level}").unsqueeze(1).broadcast_to([P, 8, P]),
                                           ALU.mult).then_inc(gd_mlr, 1)
                    if tt == 0:
                        pool.wait_ge(gd_in, TT * 7)
                        for t in range(TT):
                            z = gd_z[:, t, :].rearrange("p (h d) -> p h d", d=64)
                            pool.tensor_tensor(z, z, gd_onorm[:, :].unsqueeze(1).broadcast_to([P, 8, 64]), ALU.mult).then_inc(gd_zn, 1)
                        spread_g(1)
                    pool.wait_ge(gd_or, one)
                    step(pool.tensor_scalar(gd_ro[:, 1, :], gd_ro[:, 0, :], 1.0 / 64, EPS, ALU.mult, ALU.add))
                    pool.tensor_tensor(gd_ro[:, 0, :], gd_ro[:, 1, :], cst("neg_half")[:, 0:8],
                                       ALU.pow).then_inc(gd_on, 1)

            def sparse_attention():
                if at["mix1"][1]:
                    pool.wait_ge(x_ready, at["mix1"][1])
                for dst, name in ((ns_w1[:, :, :, :], "ns_w1"), (ns_w2k[:, :, :], "ns_w2k"), (ns_w2v[:, :, :], "ns_w2v"),
                                  (ns_wg[:, :], "ns_wg"), (ns_pos[:, :, :], "ns_pos")):
                    pool.dma_start(dst, dram[name]).then_inc(ns_params, 16)
                inverse_rms("mix1")
                cos, sin = [cst(n).rearrange("p (t f) -> p t f", f=8).unsqueeze(2).broadcast_to([P, TT, 4, 8])
                            for n in ("cos", "sin")]
                pool.wait_ge(ns_hp, 1)
                pool.memset(ns_kt[:, :, :, :, :].rearrange("p r b g t -> p (r b g t)"), 0.0).then_inc(ns_kz, 1)
                for k, col in enumerate((NS_COL["ks"], NS_COL["kw"])):
                    heads = ns_tm[:, :, col:col + 256].rearrange("p t (h d) -> p t h d", d=64)
                    x1, x2 = heads[:, :, :, 0:8], heads[:, :, :, 8:16]
                    pool.wait_ge(ns_in, TT * (4 + k))
                    if k:
                        pool.wait_ge(ns_krope, 14)
                    for n, (a, b) in enumerate([(x1, cos), (x2, sin), (x2, cos), (x1, sin)]):
                        for tt in range(TT):
                            pool.tensor_tensor(ns_krot[:, n, tt], a[:, tt], b[:, tt], ALU.mult).then_inc(ns_krope, 1)
                    pool.wait_ge(ns_krope, 14 * k + 8)
                    for tt in range(TT):
                        pool.tensor_tensor(x1[:, tt], ns_krot[:, 0, tt], ns_krot[:, 1, tt], ALU.subtract).then_inc(ns_krope, 1)
                        pool.tensor_tensor(x2[:, tt], ns_krot[:, 2, tt], ns_krot[:, 3, tt], ALU.add).then_inc(ns_krope, 1)
                    pool.wait_ge(ns_krope, 14 * k + 12)
                    for half in range(2):
                        pool.tensor_copy(ns_kd[:, k, :, :, half, :], heads).then_inc(ns_krope, 1)

            def copy_keys():
                pool.wait_ge(kv_in, TT)
                heads = kv_tm[:, :, 0:256].rearrange("p t (h d) -> p t h d", d=64)
                for half in range(2):
                    pool.tensor_copy(sb_kd[:, :, :, half, :], heads).then_inc(sb_copied, 1)
                pool.memset(sb_kt[:, :, :, :].rearrange("p r g t -> p (r g t)"), 0.0).then_inc(sb_kz, 1)

            for layer in layers:
                if layer == "mix0":
                    delta_rule()
                    continue
                if layer == "mix1":
                    sparse_attention()
                    continue
                inverse_rms(layer)
                if layer == "sgu":
                    spatial_gating()
                if layer == "sb":
                    copy_keys()
                if layer == "fin1":
                    pool.wait_ge(x_ready, at[layer][1] + TT)
                    if "fin2" in layers:
                        pool.dma_start(row[:, :], dram["fin_rows"][1:2, :].partition_broadcast(P)).then_inc(row2_loaded, 16)


def lay_out(a, layers=LAYERS):
    import numpy as np

    def panels(w, gated=False):
        w = np.asarray(w)
        k, n = w.shape
        if gated:
            w = w.reshape(k, 2, n // 512, 256).transpose(0, 2, 1, 3).reshape(k, n)
        kt, blocks = k // P, n // NB
        per = -(-kt // PK)
        out = np.zeros((blocks, per * PK, P, NB), np.float32)
        out[:, :kt] = w.reshape(kt, P, blocks, NB).transpose(2, 0, 1, 3)
        return out.reshape(blocks, per, PK, P, NB).transpose(0, 1, 3, 2, 4).reshape(blocks * per, P, PANEL)

    prod, _ = lay_out_products(layers)
    ev = np.asarray(a["ev_w_in"])[0]
    od = np.asarray(a["od_w_in"])[0]
    od_main = np.concatenate([od[:, 1024:1536], od[:, 0:1024], od[:, 1536:2560]], 1)
    ev_main = np.concatenate([ev[:, 0:1536], ev[:, 2576:3088], ev[:, 3088:3600], ev[:, 2064:2576], ev[:, 1536:2048]], 1)
    sgu = np.asarray(a["a_w_in_2"])[0]
    weights = {
        "ev_in": ev_main, "ev_out": a["ev_w_out"][0],
        "mlp0_up": a["w_up"][0], "mlp0_down": a["w_down"][0],
        "od_in": od_main, "od_out": a["od_w_out"][0],
        "mlp1_up": a["w_up"][1], "mlp1_down": a["w_down"][1],
        "sgu_in": np.concatenate([sgu[:, 2048:], sgu[:, :2048]], 1), "sgu_out": a["a_w_out_2"][0],
        "kv": a["w_kv_2"], "sb_q": a["b_w_q_2"][0], "sb_out": a["b_w_o_2"][0],
    }
    for i in range(2):
        for j in range(2):
            weights[f"ffn{i}{j}_up"] = a["ffn_w_in_2"][i][j]
            weights[f"ffn{i}{j}_down"] = a["ffn_w_out_2"][i][j]
    stream = np.concatenate([panels(weights[n], n.startswith("ffn") and n.endswith("up")) for n in prod])
    norms = {
        "mix0": a["mix_norm"][0], "mlp0": a["mlp_norm"][0], "mix1": a["mix_norm"][1], "mlp1": a["mlp_norm"][1],
        "ffn00": a["ffn_norm_2"][0][0], "ffn01": a["ffn_norm_2"][0][1], "ffn10": a["ffn_norm_2"][1][0],
        "ffn11": a["ffn_norm_2"][1][1], "sgu": a["mix_norm_2"][0], "sb": a["mix_norm_2"][1], "kv": a["kv_norm_2"],
    }
    norm_t = np.stack([np.asarray(norms[n]).reshape(DK, P).T for n in NORMS], 1)
    x = np.asarray(a["x"]).reshape(TT, P, D).transpose(1, 0, 2)
    out = {
        "x": x, "stream": stream, "norm_t": norm_t, "const": const_table()[0],
        "gd_wab": ev[:, 2048:2064].reshape(DK, P, 16).transpose(1, 0, 2).reshape(P, DK * 16),
        "gd_cw": np.asarray(a["ev_qkv_conv"])[0].reshape(4, 12, P).transpose(2, 1, 0),
        "gd_scw": np.asarray(a["ev_sc_conv"])[0].reshape(3, 4, P).transpose(2, 1, 0),
        "gd_dt_bias": np.asarray(a["ev_dt_bias"]), "gd_a_log": np.asarray(a["ev_a_log"]), "gd_onorm": np.asarray(a["ev_o_norm"]),
        "ns_w1": np.stack([np.asarray(a[n])[0].reshape(16, P, 256).transpose(1, 0, 2)
                           for n in ("od_cmp_k_w1", "od_cmp_v_w1")], 1),
        "ns_w2k": np.tile(np.asarray(a["od_cmp_k_w2"])[0].reshape(2, P, 64).transpose(1, 0, 2), (1, 1, 2)),
        "ns_w2v": np.asarray(a["od_cmp_v_w2"])[0].reshape(2, P, 64).transpose(1, 0, 2),
        "ns_wg": od[:, 2560:2608].reshape(DK, P, 48).transpose(1, 0, 2).reshape(P, DK * 48),
        "ns_pos": np.asarray(a["od_cmp_pos"])[0].reshape(2, 8, 2, 64).transpose(2, 3, 0, 1).reshape(P, 2, 8),
        "ws_t": np.asarray(a["a_w_s_2"])[0].transpose(2, 0, 1), "bs_t": np.asarray(a["a_b_s_2"])[0].T,
        "ln_rows": np.stack([np.asarray(a["a_ln_g_2"])[0], np.asarray(a["a_ln_b_2"])[0]]),
        "fin_rows": np.stack([np.asarray(a["final_norm"]), np.asarray(a["final_norm_2"])]),
    }
    return {k: np.ascontiguousarray(v) for k, v in out.items()}


def kernel(**inputs):
    import numpy as np
    import concourse.bacc as bacc
    from concourse.bass_utils import run_bass_kernel_spmd

    nc = bacc.Bacc("TRN2", target_bir_lowering=False, num_devices=1)
    arrays = lay_out({k: np.asarray(v) for k, v in inputs.items()})
    dram = {k: nc.dram_tensor(f"in_{k}", v.shape, F32, kind="ExternalInput").ap() for k, v in arrays.items()}
    dram["out"] = nc.dram_tensor("out", (P, TT, D), F32, kind="ExternalOutput").ap()
    build(nc, dram)
    r = run_bass_kernel_spmd(nc, [{f"in_{k}": v for k, v in arrays.items()}], core_ids=[0])
    return np.asarray(r.results[0]["out"]).transpose(1, 0, 2).reshape(1, T, D)
```
